# Optimizing a Trainium2 kernel written in Bass

```python
import jax, jax.numpy as jnp
from jax import lax
import numpy as np

D_MODEL = 1024
BATCH = 1
SEQ = 256
DEPTH = 1

N_META = 16
POOL_WINDOWS = (2, 4, 8, 16)
N_POOL_GROUPS = 4
POOL_WIDTH = D_MODEL
POOL_GROUP_DIM = POOL_WIDTH // N_POOL_GROUPS
DN_HEADS = 8
DN_HEAD_DIM = 128
DN_WIDTH = DN_HEADS * DN_HEAD_DIM
CONV_WIDTH = 4
CHUNK = 64
N_EXPERT_GROUPS = 4
EXPERTS_PER_GROUP = 8
N_EXPERTS = N_EXPERT_GROUPS * EXPERTS_PER_GROUP
TOP_K_IN_GROUP = 2
D_FF_EXPERT = 512
NORM_EPS = 1e-6
PROJ_SPLITS = [POOL_WIDTH, POOL_WIDTH + 3 * DN_WIDTH, POOL_WIDTH + 4 * DN_WIDTH,
               POOL_WIDTH + 4 * DN_WIDTH + DN_HEADS, POOL_WIDTH + 4 * DN_WIDTH + 2 * DN_HEADS,
               POOL_WIDTH + 4 * DN_WIDTH + 2 * DN_HEADS + D_MODEL]
PROJ_COLS = POOL_WIDTH + 4 * DN_WIDTH + 2 * DN_HEADS + 2 * D_MODEL

kernel_name = "hybrid_pool_gdn_hiermoe_block"

def rmsnorm(x, w):
    xf = x.astype(jnp.float32)
    y = xf * lax.rsqrt(jnp.mean(xf * xf, axis=-1, keepdims=True) + NORM_EPS)
    return (y * w.astype(jnp.float32)).astype(x.dtype)

def l2norm(t):
    return t * lax.rsqrt(jnp.sum(t * t, axis=-1, keepdims=True) + NORM_EPS)

def multiscale_pool_branch(u, pool_w, pool_scale):
    Bsz, L, _ = u.shape
    uf = u.astype(jnp.float32)
    cs = jnp.concatenate([jnp.zeros((Bsz, 1, POOL_WIDTH), jnp.float32), jnp.cumsum(uf, axis=1)], axis=1)
    t = jnp.arange(L)
    outs = []
    for gi, win in enumerate(POOL_WINDOWS):
        cs_g = cs[:, :, gi * POOL_GROUP_DIM:(gi + 1) * POOL_GROUP_DIM]
        start = jnp.maximum(t + 1 - win, 0)
        window_sum = cs_g[:, 1:] - jnp.take(cs_g, start, axis=1)
        count = (t + 1 - start).astype(jnp.float32)
        outs.append(window_sum / count[None, :, None])
    pooled = jnp.concatenate(outs, axis=-1) - uf
    pooled = pooled.reshape(Bsz, L, N_POOL_GROUPS, POOL_GROUP_DIM)
    mixed = jnp.einsum('blgc,gcd->blgd', pooled, pool_w.astype(jnp.float32)).reshape(Bsz, L, POOL_WIDTH)
    return (mixed * pool_scale.astype(jnp.float32)).astype(u.dtype)

def causal_depthwise_conv(x, w):
    C = x.shape[-1]
    return lax.conv_general_dilated(x, w[:, None, :].astype(x.dtype), window_strides=(1,),
                                    padding=[(CONV_WIDTH - 1, 0)],
                                    dimension_numbers=('NWC', 'WIO', 'NWC'), feature_group_count=C)

def chunk_gated_delta_rule(q, k, v, g, beta, S0, chunk):
    Bsz, H, T, dk = q.shape
    dv = v.shape[-1]
    n = T // chunk
    q = q.reshape(Bsz, H, n, chunk, dk) * (dk ** -0.5)
    k = k.reshape(Bsz, H, n, chunk, dk)
    v = v.reshape(Bsz, H, n, chunk, dv)
    beta = beta.reshape(Bsz, H, n, chunk)
    gam = jnp.cumsum(g.reshape(Bsz, H, n, chunk), axis=-1)
    idx = jnp.arange(chunk)
    lower_incl = idx[:, None] >= idx[None, :]
    strict = idx[:, None] > idx[None, :]
    decay_mat = jnp.exp(jnp.where(lower_incl, gam[..., :, None] - gam[..., None, :], -jnp.inf))
    kk = jnp.einsum('bhncd,bhnsd->bhncs', k, k)
    A = jnp.where(strict, beta[..., :, None] * kk * decay_mat, 0.0)
    rhs = jnp.concatenate([v * beta[..., None], k * (beta * jnp.exp(gam))[..., None]], axis=-1)
    sol = lax.linalg.triangular_solve(A, rhs, left_side=True, lower=True, unit_diagonal=True)
    u_w, w_w = sol[..., :dv], sol[..., dv:]
    qk = jnp.einsum('bhncd,bhnsd->bhncs', q, k) * decay_mat
    q_dec = q * jnp.exp(gam)[..., None]
    k_dec = k * jnp.exp(gam[..., -1:] - gam)[..., None]
    chunk_decay = jnp.exp(gam[..., -1])

    def step(S, xs):
        u_c, w_c, qk_c, qd_c, kd_c, cd_c = xs
        v_new = u_c - jnp.einsum('bhck,bhkv->bhcv', w_c, S)
        o_c = jnp.einsum('bhck,bhkv->bhcv', qd_c, S) + jnp.einsum('bhcs,bhsv->bhcv', qk_c, v_new)
        S = S * cd_c[..., None, None] + jnp.einsum('bhck,bhcv->bhkv', kd_c, v_new)
        return S, o_c

    xs = tuple(jnp.moveaxis(t_, 2, 0) for t_ in (u_w, w_w, qk, q_dec, k_dec, chunk_decay))
    S_final, o = lax.scan(step, S0, xs)
    o = jnp.moveaxis(o, 0, 2).reshape(Bsz, H, T, dv)
    return o, S_final

def gated_deltanet_branch(p_qkv, p_z, p_a, p_b, conv_w, a_log, dt_bias, norm_w):
    Bsz, L, _ = p_qkv.shape
    qkv = jax.nn.silu(causal_depthwise_conv(p_qkv, conv_w))
    q, k, v = jnp.split(qkv, 3, axis=-1)

    def heads(t):
        return t.reshape(Bsz, L, DN_HEADS, DN_HEAD_DIM).transpose(0, 2, 1, 3).astype(jnp.float32)

    q = l2norm(heads(q))
    k = l2norm(heads(k))
    v = heads(v)
    beta = jax.nn.sigmoid(p_b.astype(jnp.float32)).transpose(0, 2, 1)
    g = (-jnp.exp(a_log.astype(jnp.float32))
         * jax.nn.softplus(p_a.astype(jnp.float32) + dt_bias.astype(jnp.float32))).transpose(0, 2, 1)
    S0 = jnp.zeros((Bsz, DN_HEADS, DN_HEAD_DIM, DN_HEAD_DIM), jnp.float32)
    o_meta, S_meta = chunk_gated_delta_rule(q[:, :, :N_META], k[:, :, :N_META], v[:, :, :N_META],
                                            g[:, :, :N_META], beta[:, :, :N_META], S0, N_META)
    o_real, _ = chunk_gated_delta_rule(q[:, :, N_META:], k[:, :, N_META:], v[:, :, N_META:],
                                       g[:, :, N_META:], beta[:, :, N_META:], S_meta, CHUNK)
    o = jnp.concatenate([o_meta, o_real], axis=2).transpose(0, 2, 1, 3)
    o = o * lax.rsqrt(jnp.mean(o * o, axis=-1, keepdims=True) + NORM_EPS) * norm_w.astype(jnp.float32)
    z = p_z.astype(jnp.float32).reshape(Bsz, L, DN_HEADS, DN_HEAD_DIM)
    o = o * jax.nn.silu(z)
    return o.reshape(Bsz, L, DN_WIDTH).astype(p_qkv.dtype)

def hierarchical_moe(u, w_grp, b_grp, w_rtr, b_rtr, w_gate, w_up, w_down):
    Bsz, L, D = u.shape
    xt = u.reshape(-1, D)
    grp_probs = jax.nn.softmax((xt @ w_grp + b_grp).astype(jnp.float32), axis=-1)
    p_grp, g_idx = lax.top_k(grp_probs, 1)
    exp_logits = (xt @ w_rtr + b_rtr).astype(jnp.float32).reshape(-1, N_EXPERT_GROUPS, EXPERTS_PER_GROUP)
    sel_logits = jnp.take_along_axis(exp_logits, g_idx[:, :, None], axis=1)[:, 0]
    w_e, e_idx = lax.top_k(jax.nn.softmax(sel_logits, axis=-1), TOP_K_IN_GROUP)
    w_e = w_e / jnp.sum(w_e, axis=-1, keepdims=True)
    exp_weight = jnp.sum(jax.nn.one_hot(e_idx, EXPERTS_PER_GROUP, dtype=jnp.float32) * w_e[..., None], axis=1)
    comb = (jax.nn.one_hot(g_idx[:, 0], N_EXPERT_GROUPS, dtype=jnp.float32)[:, :, None]
            * (p_grp * exp_weight)[:, None, :])
    y = jnp.zeros_like(xt)
    for gi in range(N_EXPERT_GROUPS):
        hdn = (jax.nn.silu(jnp.einsum('nd,edf->nef', xt, w_gate[gi]))
               * jnp.einsum('nd,edf->nef', xt, w_up[gi]))
        hdn = hdn * comb[:, gi, :, None].astype(hdn.dtype)
        y = y + jnp.einsum('nef,efd->nd', hdn, w_down[gi])
    return y.reshape(Bsz, L, D)

def setup_inputs(seed: int = 0) -> dict:
    key = jax.random.key(seed)
    ks = jax.random.split(key, 24)
    f32 = jnp.float32
    dt = jnp.exp(jax.random.uniform(ks[8], (DEPTH, DN_HEADS), f32, np.log(0.001), np.log(0.1)))
    return {
        'x': jax.random.normal(ks[0], (BATCH, SEQ, D_MODEL), f32),
        'meta_tokens': jax.random.normal(ks[1], (N_META, D_MODEL), f32),
        'norm_mix_w': 1.0 + 0.02 * jax.random.normal(ks[2], (DEPTH, D_MODEL), f32),
        'w_in': jax.random.normal(ks[3], (DEPTH, D_MODEL, PROJ_COLS), f32) * D_MODEL ** -0.5,
        'conv_w': jax.random.normal(ks[4], (DEPTH, CONV_WIDTH, 3 * DN_WIDTH), f32) * CONV_WIDTH ** -0.5,
        'pool_w': jax.random.normal(ks[5], (DEPTH, N_POOL_GROUPS, POOL_GROUP_DIM, POOL_GROUP_DIM), f32) * POOL_GROUP_DIM ** -0.5,
        'pool_scale': 1.0 + 0.1 * jax.random.normal(ks[6], (DEPTH, POOL_WIDTH), f32),
        'a_log': jnp.log(jax.random.uniform(ks[7], (DEPTH, DN_HEADS), f32, 1.0, 16.0)),
        'dt_bias': dt + jnp.log(-jnp.expm1(-dt)),
        'dn_norm_w': 1.0 + 0.02 * jax.random.normal(ks[9], (DEPTH, DN_HEAD_DIM), f32),
        'w_out': jax.random.normal(ks[10], (DEPTH, D_MODEL, D_MODEL), f32) * D_MODEL ** -0.5,
        'norm_ffn_w': 1.0 + 0.02 * jax.random.normal(ks[11], (DEPTH, D_MODEL), f32),
        'router_group_w': jax.random.normal(ks[12], (DEPTH, D_MODEL, N_EXPERT_GROUPS), f32) * D_MODEL ** -0.5,
        'router_group_b': 0.01 * jax.random.normal(ks[13], (DEPTH, N_EXPERT_GROUPS), f32),
        'router_expert_w': jax.random.normal(ks[14], (DEPTH, D_MODEL, N_EXPERTS), f32) * D_MODEL ** -0.5,
        'router_expert_b': 0.01 * jax.random.normal(ks[15], (DEPTH, N_EXPERTS), f32),
        'expert_w_gate': jax.random.normal(ks[16], (DEPTH, N_EXPERT_GROUPS, EXPERTS_PER_GROUP, D_MODEL, D_FF_EXPERT), f32) * D_MODEL ** -0.5,
        'expert_w_up': jax.random.normal(ks[17], (DEPTH, N_EXPERT_GROUPS, EXPERTS_PER_GROUP, D_MODEL, D_FF_EXPERT), f32) * D_MODEL ** -0.5,
        'expert_w_down': jax.random.normal(ks[18], (DEPTH, N_EXPERT_GROUPS, EXPERTS_PER_GROUP, D_FF_EXPERT, D_MODEL), f32) * D_FF_EXPERT ** -0.5,
        'norm_final_w': 1.0 + 0.02 * jax.random.normal(ks[19], (D_MODEL,), f32),
    }

def reference(x, meta_tokens, norm_mix_w, w_in, conv_w, pool_w, pool_scale, a_log, dt_bias, dn_norm_w,
              w_out, norm_ffn_w, router_group_w, router_group_b, router_expert_w, router_expert_b,
              expert_w_gate, expert_w_up, expert_w_down, norm_final_w):
    Bsz = x.shape[0]
    meta = jnp.broadcast_to(meta_tokens[None].astype(x.dtype), (Bsz, N_META, D_MODEL))
    h = jnp.concatenate([meta, x], axis=1)
    for layer in range(DEPTH):
        u = rmsnorm(h, norm_mix_w[layer])
        p = u @ w_in[layer]
        p_pool, p_qkv, p_z, p_a, p_b, g_pool, g_dn = jnp.split(p, PROJ_SPLITS, axis=-1)
        y_pool = multiscale_pool_branch(p_pool, pool_w[layer], pool_scale[layer])
        y_dn = gated_deltanet_branch(p_qkv, p_z, p_a, p_b, conv_w[layer], a_log[layer], dt_bias[layer],
                                     dn_norm_w[layer])
        merged = jax.nn.sigmoid(g_pool) * y_pool + jax.nn.sigmoid(g_dn) * y_dn
        h = h + merged @ w_out[layer]
        h = h + hierarchical_moe(rmsnorm(h, norm_ffn_w[layer]), router_group_w[layer], router_group_b[layer],
                                 router_expert_w[layer], router_expert_b[layer], expert_w_gate[layer],
                                 expert_w_up[layer], expert_w_down[layer])
    out = rmsnorm(h, norm_final_w)
    return out[:, N_META:]


_drawn_inputs = setup_inputs


def setup_inputs(seed=0):
    import zlib

    import numpy as np

    out = dict(_drawn_inputs(seed))
    spreads = {}
    factors = {'dn_norm_w': 8.0,
     'router_group_b': 38.012,
     'router_expert_b': 20.128,
     'norm_final_w': 8.049,
     'pool_scale': 2.76,
     'norm_ffn_w': 4.267}
    for name, (base, spread) in spreads.items():
        noise = np.random.default_rng([zlib.crc32(name.encode()), seed]).standard_normal(out[name].shape)
        drawn = base * np.exp(spread * noise) if base else spread * noise
        out[name] = __import__('jax').numpy.asarray(drawn.astype(out[name].dtype))
    for name, factor in factors.items():
        out[name] = (out[name] * factor).astype(out[name].dtype)
    return out
```

```python
from contextlib import ExitStack

import numpy as np
import concourse.bass as bass
from concourse import mybir

F32 = mybir.dt.float32
I32 = mybir.dt.int32
U32 = mybir.dt.uint32
ALU = mybir.AluOpType
ACT = mybir.ActivationFunctionType
AX = mybir.AxisListType

P = 128
D = 1024
KT = D // P
META = 16
SEQ = 256
TT = SEQ // P
L = META + SEQ
HEADS = 8
CH = 96
PAD = 16
LP = PAD + L
NC_ = LP // CH
REAL = PAD + META
TAPS = 4
LEVELS = [2, 4, 8, 16, 32, 64]
NL = len(LEVELS)
GROUPS = 4
PER_GROUP = 8
EXPERTS = GROUPS * PER_GROUP
FF = 512
EPS = 1e-6
NEG = -1e30
COL = {"P": 0, "q": 1024, "k": 2048, "v": 3072, "z": 4096, "gA": 5136, "gB": 6160}
COL_AB = 5120
WIN_SLOTS = 8
CHUNK = 4096
SLOTS = 64
PASSES = -(-SEQ // SLOTS)
DESK = 6192
CONSTS = {n: i + 1 for i, n in enumerate(["ident", "ones", "eps", "abz", "masks", "mups", "kqv_zero"])}
LEAD = 5
ROWS_BUF = 6
BIG = float(1 << 20)
ROW_CONV, ROW_MIX, ROW_FFN, ROW_POOL, ROW_DN, ROWS = 0, 96, 104, 112, 120, 121


def plan_rounds():
    order = []
    tile = 0
    for r in range(HEADS + 2):
        kinds = [(t, r) for t in "kqv"] if r < HEADS else []
        j = r - 2
        if j >= 0:
            kinds += [("z", j), ("gB", j)]
            kinds += [("P", j), ("P", j + 1)] if j % 2 == 0 else [("gA", j - 1), ("gA", j)]
        fill = []
        for n, (t, j2) in enumerate(kinds):
            fill += [("proj", tile, t, j2, k) for k in range(0, KT, 2)]
            fill += [("take", tile, t, j2)]
            if t in "kqv":
                fill += [("silu", t, j2)] if n == 2 else []
                if n == 2:
                    fill[-1:] = [("silu", x, j2) for x in "kqv"]
            if t == "P" and j2 % 2 == 1:
                pass
            if t == "gA" and j2 % 2 == 1:
                fill += [("mix", j2)]
            tile += 1
        chain_a = []
        if 0 <= r - 1 < HEADS:
            h = r - 1
            chain_a = [("norm", h), ("gram", h), ("turn", h)]
            for lv in range(NL):
                chain_a += [("lx", h, lv), ("ly", h, lv)]
            chain_a += [("solve", h)]
        chain_b = []
        if 0 <= r - 2 < HEADS:
            h = r - 2
            chain_b = [("s0", h), ("sa", h, 1), ("sb", h, 1), ("sa", h, 2), ("sb", h, 2), ("onorm", h), ("out", h)]
        late = [x for x in fill if x[0] == "mix"]
        fill = [x for x in fill if x[0] != "mix"]
        steps = max(len(chain_a), 14)
        lists = [(chain_a, steps), (chain_b, steps), (fill, steps)]
        at = [0, 0, 0]
        for s in range(steps):
            for i, (lst, n) in enumerate(lists):
                upto = len(lst) * (s + 1) // n
                order += lst[at[i]:upto]
                at[i] = upto
        order += late
    return order


ORDER = plan_rounds()
PSUM_OF = {
    "norm": ["nk", "nq"], "gram": ["G", "QK", "KT", "VT"], "turn": ["AT"], "lx": ["X"], "ly": ["Y", "YT"],
    "solve": ["u", "wT"], "s0": ["os"], "sa": ["ws", "o1"], "sb": ["os"], "out": ["oT"], "mix": ["m0", "m1"],
}


def plan_banks():
    where, n = {}, 0
    for step in ORDER:
        if step[0] == "take":
            where[("proj", step[1])] = (step[1] % 2, step[1] // 2)
        for name in PSUM_OF.get(step[0], []):
            if name == "Y" and step[2] == NL - 1:
                continue
            where[(name,) + tuple(step[1:])] = (2 + n % 6, n // 6)
            n += 1
    uses = [0] * 8
    for b, u in where.values():
        uses[b] = max(uses[b], u + 1)
    return where, uses


WHERE, USES = plan_banks()
TILES = [(s[2], s[3]) for s in ORDER if s[0] == "take"]
TILE_OF = {t: n for n, t in enumerate(TILES)}


def uses(n, k, slots):
    return (n - k + slots - 1) // slots


def build_block(nc, x, meta_tokens, norm_mix_w, w_in, conv_w, pool_w, pool_scale, a_log, dt_bias, dn_norm_w,
                w_out, norm_ffn_w, router_group_w, router_group_b, router_expert_w, router_expert_b,
                expert_w_gate, expert_w_up, expert_w_down, norm_final_w, out):
    ctx = ExitStack()
    with ctx:
        def sb(name, shape, dt=F32):
            return ctx.enter_context(nc.sbuf_tensor(name, shape, dt))

        def sem(name):
            return ctx.enter_context(nc.semaphore(name))

        class Named:
            def __init__(self):
                self.made = {}

            def __call__(self, name):
                if name not in self.made:
                    self.made[name] = sem("s_" + name)
                return self.made[name]

        S = Named()

        ring = sb("ring", [P, 9, CHUNK])
        room = ring[:, 3:9, :].rearrange("p a b -> p (a b)")
        at = [0]

        def take(n, rows=P):
            at[0] += n
            assert at[0] <= 6 * CHUNK, at[0]
            return room[0:rows, at[0] - n:at[0]]

        win = take(WIN_SLOTS * D).rearrange("p (s k c) -> p s k c", s=WIN_SLOTS, k=KT)
        wout = win.rearrange("p s k c -> p s (k c)")
        uT = take(KT * L).rearrange("p (k t) -> p k t", k=KT)
        kqv = take(9 * LP).rearrange("p (b i t) -> p b i t", b=3, i=3)
        decay_at = at[0]
        Dm = take(HEADS * LP, CH).rearrange("p (h c t) -> p h c t", h=HEADS, c=NC_)
        DT = take(HEADS * LP, CH).rearrange("p (h c t) -> p h c t", h=HEADS, c=NC_)
        hn = room[:, decay_at:decay_at + 3 * D].rearrange("p (i d) -> p i d", i=3)
        sq = take(2 * LP).rearrange("p (i t) -> p i t", i=2)
        rn = take(2 * LP).rearrange("p (i t) -> p i t", i=2)

        def chunks(n, rows=CH):
            return take(n * NC_, rows).rearrange("p (c t) -> p c t", c=NC_)

        Ab = chunks(CH)
        ATb = chunks(CH)
        Tb = chunks(CH)
        Ub = chunks(CH)
        Xb = chunks(CH)

        OTb = take(3 * LP, CH).rearrange("p (b c t) -> p b c t", b=3, c=NC_)
        tmpT = take(2 * LP, CH).rearrange("p (b c t) -> p b c t", b=2, c=NC_)
        late = sb("late", [P, TT * D])
        xn = late[:].rearrange("p (i d) -> p i d", i=TT)
        Kb = late[0:CH, 0:2 * NC_ * P].rearrange("p (b c t) -> p b c t", b=2, c=NC_)
        Kd = take(2 * NC_ * P, CH).rearrange("p (b c t) -> p b c t", b=2, c=NC_)
        ub = take(2 * NC_ * P, CH).rearrange("p (b c t) -> p b c t", b=2, c=NC_)
        desk = sb("desk", [P, DESK])
        desk_at = [0]

        def lay(shape, rows=P):
            n = int(np.prod(shape))
            desk_at[0] += n
            assert desk_at[0] <= DESK, desk_at[0]
            v = desk[0:rows, desk_at[0] - n:desk_at[0]]
            names = "abcd"[:len(shape)]
            return v if len(shape) == 1 else v.rearrange(f"p ({' '.join(names)}) -> p {' '.join(names)}", **dict(zip(names[1:], shape[1:])))

        Vb = lay([2, NC_, P], CH)
        wT = lay([2, NC_, CH])
        vn = lay([2, P], CH)
        St = lay([2, P])
        osb = lay([NC_, P], CH)
        o1s = lay([2, P], CH)
        acc = lay([3, L])
        zs = lay([2, SEQ])
        thB = lay([SEQ])
        thA = lay([2, SEQ])
        pt = lay([2, L])
        ps2 = lay([2, L])
        pooled = lay([2, SEQ])
        poolw = sb("poolw", [P, 2, 2, 2 * P])
        merged = sb("merged", [P, KT, SEQ])
        hres = sb("hres", [P, TT, D])
        ident = sb("ident", [P, P])
        ones = sb("ones", [P, P])
        eps = sb("eps", [P, 1])
        prm = sb("prm", [P, P])
        prmT = sb("prmT", [P, ROWS])
        halfs = sb("halfs", [P, ROWS - ROW_POOL])
        mlow = take(CH, CH)
        mup = take((1 + NL) * CH, CH).rearrange("p (l t) -> p l t", l=1 + NL)
        uincl = sb("uincl", [CH, CH])
        negs = take(2 * CH, CH).rearrange("p (l t) -> p l t", l=2)
        small = sb("small", [P, 40, 24])
        wab = sb("wab", [P, KT, 16])
        abT = sb("abT", [16, LP])
        bc8 = sb("bc8", [CH, 3, 8])

        def plane(i, rows=CH, n=24):
            return small[0:rows, i, 0:n]

        def plane3(i, rows=CH):
            return small[0:rows, i, 0:24].rearrange("p (c h) -> p c h", c=NC_)

        X_, AX_, E_, LN_, RL_, SP_, G_, EB_, BETA_, NBETA_, GAM_, EGAM_, CD_, KD_, GL_, SKB_ = range(16)
        MS_, RS_, OSS_, ORS_ = 16, 17, 18, 20

        pb = [ctx.enter_context(nc.psum_tensor(f"bank{i}", [P, 512], F32)) for i in range(8)]
        full = [sem(f"bank_full{i}") for i in range(8)]
        free = [sem(f"bank_free{i}") for i in range(8)]
        win_land = [sem(f"win_land{i}") for i in range(WIN_SLOTS)]

        xn_dram = nc.dram_tensor("xn_rows", [2 * SEQ, D // 2], F32, kind="Internal").ap()
        y_dram = nc.dram_tensor("y_rows", [4 * SEQ, D // 2], F32, kind="Internal").ap()

        desk_at[0] = 0
        xg = lay([ROWS_BUF, FF])
        xgT = lay([1, KT * SLOTS])
        sgate = lay([1, FF // 2])
        hmid = lay([1, FF // 2])
        hT = lay([1, 2, P])
        yout = [late[:, i * FF:(i + 1) * FF] for i in range(4)]
        yout += [merged[:].rearrange("p k t -> p (k t)")[:, (2 + i) * FF:(3 + i) * FF] for i in range(2)]
        rt = lay([TT, 18, 32])
        hot = merged[:, 0:2, :].rearrange("p k (a t) -> p (k a) t", a=2)
        wff = lay([KT, SLOTS])
        x2T = merged
        routw = poolw[:].rearrange("p a b c -> p (a b c)")[:, 0:KT * 36].rearrange("p (k n) -> p k n", k=KT)
        rbias = sb("rbias", [P, 36])
        rs = sb("rs", [P, TT, 24])
        ru = sb("ru", [P, TT, 16], U32)
        iota_e = sb("iota_e", [P, EXPERTS])
        iota_g = sb("iota_g", [P, EXPERTS])
        iota_c = sb("iota_c", [P, P])
        iota_t = sb("iota_t", [P, TT])
        halfof = sb("halfof", [P, 1])
        before = sb("before", [P, P])
        lists = sb("lists", [P, 3, EXPERTS])
        gidx = sb("gidx", [P, EXPERTS], I32)
        sidx = sb("sidx", [P, EXPERTS], I32)
        gcol = sb("gcol", [P, ROWS_BUF], I32)
        scol = sb("scol", [P, ROWS_BUF], I32)
        most = sb("most", [P, 8])
        mosti = sb("mosti", [P, 1], I32)

        w_in_v = w_in[0].rearrange("(k p) n -> p k n", p=P)
        gate_v = expert_w_gate[0].rearrange("g e (k p) f -> (g e) p k f", p=P)
        up_v = expert_w_up[0].rearrange("g e (k p) f -> (g e) p k f", p=P)
        down_v = expert_w_down[0].rearrange("g e (k p) d -> (g e) p k d", p=P)

        def filled(eng, key):
            b, n = WHERE[key]
            eng.wait_ge(full[b], n + 1)
            return pb[b]

        def freed(ins, key):
            ins.then_inc(free[WHERE[key][0]], 1)

        def bank(pe, key):
            b, n = WHERE[key]
            if n >= 1:
                pe.wait_ge(free[b], n)
            return pb[b]

        LIST = {"k": 0, "q": 1, "v": 2}

        def overflow(eng, one_pass):
            eng.wait_ge(S("most"), 1)
            count = eng.value_load(mosti[0:1, 0:1], min_val=0, max_val=SEQ)
            opened = []
            for ps in range(1, PASSES):
                c = eng.If(count > ps * SLOTS)
                c.__enter__()
                opened.append(c)
                one_pass(ps)
            for c in reversed(opened):
                c.__exit__(None, None, None)

        block = ctx.enter_context(nc.Block())

        @block.sync
        def _(sp):
            sp.dma_start(prm[ROW_CONV:ROW_CONV + 96, :], conv_w[0].rearrange("j (c p) -> (j c) p", p=P)).then_inc(S("params_land"), 16)
            for row, a in ((ROW_MIX, norm_mix_w), (ROW_FFN, norm_ffn_w), (ROW_POOL, pool_scale), (ROW_DN, dn_norm_w)):
                n = a.shape[1] // P
                sp.dma_start(prm[row:row + n, :], a[0].rearrange("(c p) -> c p", p=P)).then_inc(S("params_land"), 16)
            sp.dma_start(wab[:, :, :], w_in_v[:, :, COL_AB:COL_AB + 16]).then_inc(S("params_land"), 16)
            for i, a in ((0, a_log), (1, dt_bias)):
                sp.dma_start(bc8[:, i, :], a[0:1, :].partition_broadcast(CH) if False else a[0:1, :].to_broadcast([CH, 8])).then_inc(S("params_land"), 16)

            def load_tile(n):
                t, j = TILES[n]
                if n >= WIN_SLOTS:
                    sp.wait_ge(S("tile_used"), n - WIN_SLOTS + 1)
                c = COL[t] + j * P
                sp.dma_start(win[:, n % WIN_SLOTS], w_in_v[:, :, c:c + P]).then_inc(win_land[n % WIN_SLOTS], 16)
                if t == "P" and j % 2 == 0:
                    g = j // 2
                    if g >= 2:
                        sp.wait_ge(S("mix"), 2 * (g - 1))
                    sp.dma_start(poolw[:, g % 2], pool_w[0, g].rearrange("(a p) c -> p a c", p=P)).then_inc(S(f"poolw_land{g % 2}"), 16)

            for n in range(WIN_SLOTS):
                load_tile(n)
            for c in range(3):
                sp.dma_start(ring[:, c, :].rearrange("p (k f) -> p k f", k=KT if c < 2 else 4),
                             (gate_v, up_v, down_v)[c][0]).then_inc(S(f"w_land{c}"), 16)
            for n in range(WIN_SLOTS, len(TILES)):
                load_tile(n)
            for k in range(KT):
                n = len(TILES) + k
                sp.wait_ge(S("tile_used"), n - WIN_SLOTS + 1)
                sp.dma_start(wout[:, n % WIN_SLOTS, :], w_out[0, k * P:(k + 1) * P, :]).then_inc(win_land[n % WIN_SLOTS], 16)
            sp.wait_ge(S("mix"), 2 * GROUPS)
            sp.dma_start(routw[:, :, 0:GROUPS], router_group_w[0].rearrange("(k p) n -> p k n", p=P)).then_inc(S("rout_land"), 16)
            sp.dma_start(routw[:, :, GROUPS:36], router_expert_w[0].rearrange("(k p) n -> p k n", p=P)).then_inc(S("rout_land"), 16)
            sp.dma_start(rbias[:, 0:GROUPS], router_group_b[0:1, :].to_broadcast([P, GROUPS])).then_inc(S("rout_land"), 16)
            sp.dma_start(rbias[:, GROUPS:36], router_expert_b[0:1, :].to_broadcast([P, EXPERTS])).then_inc(S("rout_land"), 16)
            sp.wait_ge(S("outproj"), 1)

            def load_expert(e, slot):
                for c in range(3):
                    sp.dma_start(ring[:, 3 * slot + c, :].rearrange("p (k f) -> p k f", k=KT if c < 2 else 4),
                                 (gate_v, up_v, down_v)[c][bass.ds(e, 1)].rearrange("a p k f -> (a p) k f") if not isinstance(e, int)
                                 else (gate_v, up_v, down_v)[c][e]).then_inc(S(f"w_land{3 * slot + c}"), 16)

            def one_pass(ps):
                base = EXPERTS * ps
                for e in range(3):
                    if ps == 0 and e == 0:
                        continue
                    if ps >= 1:
                        sp.wait_ge(S("y"), base)
                    load_expert(e, e)
                with sp.Fori(1, EXPERTS // 3) as i:
                    for j in range(3):
                        sp.wait_ge(S("y"), i * 3 + (base + j - 2))
                        load_expert(i * 3 + j, j)
                for e in range(EXPERTS // 3 * 3, EXPERTS):
                    sp.wait_ge(S("y"), base + e - 2)
                    load_expert(e, e % 3)

            one_pass(0)
            overflow(sp, one_pass)
            sp.wait_ge(S("pe_done"), 1)
            sp.wait_ge(S("y_all"), 1)
            sp.dma_start(ring[:, 5, 0:D], norm_final_w[None, :].to_broadcast([P, D])).then_inc(S("wf_land"), 16)
            for i in range(TT):
                for k in range(2):
                    sp.dma_start(ring[:, 2 * i + k, 0:D],
                                 y_dram.rearrange("(t b) d -> t (b d)", b=2)[k * SEQ + i * P:k * SEQ + (i + 1) * P, :]).then_inc(S(f"y_back{i}"), 16)
            for i in range(TT):
                sp.wait_ge(S("final"), i + 1)
                sp.dma_start(out[0, i * P:(i + 1) * P, :], ring[:, 7 + i, 0:D]).then_inc(S("stored"), 16)
            sp.wait_ge(S("stored"), TT * 16)

        @block.scalar
        def _(act):
            for i in range(TT):
                act.dma_start(hres[:, i, :], x[0, i * P:(i + 1) * P, :]).then_inc(S(f"x_land{i}"), 16)
            act.dma_start(hn[0:META, 2, :], meta_tokens).then_inc(S("meta_land"), 16)
            act.wait_ge(S("meta_land"), 16)
            junk = merged[:].rearrange("p k t -> p (k t)")[:, 0:D]
            for i in range(3):
                rows = META if i == 2 else P
                if i < 2:
                    act.wait_ge(S(f"x_land{i}"), 16)
                if i:
                    act.wait_ge(S("ms"), i)
                nc.scalar.activation(junk[0:rows], hn[0:META, 2, :] if i == 2 else hres[:, i, :], ACT.Square,
                                     scale=1.0 / 32.0, accum_out=small[0:rows, MS_, i:i + 1]).then_inc(S("ms"), 1)
            act.wait_ge(S("ms"), 3)
            act.wait_ge(S("consts"), CONSTS["eps"])
            nc.scalar.activation(small[:, MS_, 4:6], small[:, MS_, 0:2], ACT.Sqrt, bias=eps[:]).then_inc(S("rms"), 1)
            nc.scalar.activation(small[0:META, MS_, 6:7], small[0:META, MS_, 2:3], ACT.Sqrt, bias=eps[0:META]).then_inc(S("rms"), 1)
            act.wait_ge(S("prmT"), 1)
            for k in range(1, KT, 2):
                act.wait_ge(S("turned"), k + 1)
                nc.scalar.activation(uT[:, k, :], pb[k % 4][:, 0:L], ACT.Copy, scale=prmT[:, ROW_MIX + k:ROW_MIX + k + 1]).then_inc(S("uT"), 1)
            act.wait_ge(S("ab"), 1)
            act.wait_ge(S("consts"), CONSTS["abz"])
            nc.scalar.activation(abT[:, PAD:LP], pb[4][0:16, 0:L], ACT.Copy).then_inc(S("abT"), 1)
            act.wait_ge(S("xa"), 1)
            nc.scalar.activation(plane(AX_), plane(X_), ACT.Abs).then_inc(S("a_chain"), 1)
            act.wait_ge(S("a_chain"), 1)
            nc.scalar.activation(plane(E_), plane(AX_), ACT.Exp, scale=-1.0).then_inc(S("a_chain"), 1)
            act.wait_ge(S("a_chain"), 2)
            nc.scalar.activation(plane(LN_), plane(E_), ACT.Ln, bias=1.0).then_inc(S("lnp"), 1)
            nc.scalar.activation(plane3(EB_), pb[5][0:CH, 0:48].rearrange("p (c n) -> p c n", c=3)[:, :, 8:16], ACT.Exp, scale=-1.0).then_inc(S("eb"), 1)
            act.wait_ge(S("params_land"), 8 * 16)
            nc.scalar.activation(bc8[:, 2, :], bc8[:, 0, :], ACT.Exp).then_inc(S("ea"), 1)
            act.wait_ge(S("kdarg"), 1)
            nc.scalar.activation(plane(EGAM_), plane(GAM_), ACT.Exp).then_inc(S("egam"), 1)
            nc.scalar.activation(plane(CD_, P), pb[6][:, 32:56], ACT.Exp).then_inc(S("egam"), 1)
            nc.scalar.activation(plane(KD_), plane(GL_), ACT.Exp).then_inc(S("egam"), 1)
            for h in range(HEADS):
                act.wait_ge(S("darg"), 2 * h + 1)
                nc.scalar.activation(Dm[:, h], Dm[:, h], ACT.Exp).then_inc(S("Dexp"), 1)
                act.wait_ge(S("darg"), 2 * h + 2)
                nc.scalar.activation(DT[:, h], DT[:, h], ACT.Exp).then_inc(S("DTexp"), 1)

            def take_tile(n, t, j):
                p = filled(act, ("proj", n))
                if t in "kqv":
                    i = LIST[t]
                    col = {"q": 0, "k": 8, "v": 16}[t] + j
                    w3 = prmT[:, 3 * 24 + col:3 * 24 + col + 1]
                    if j >= 1:
                        act.wait_ge(S("silu"), 3 * j)
                    nc.scalar.activation(acc[:, i, :], p[:, 0:L], ACT.Copy, scale=w3).then_inc(S("tap3"), 1)
                elif t == "z":
                    if j >= 2:
                        act.wait_ge(S("out"), j - 1)
                    freed(nc.scalar.activation(zs[:, j % 2, :], p[:, 0:SEQ], ACT.Silu), ("proj", n))
                elif t == "gB":
                    if j >= 1:
                        act.wait_ge(S("zg"), j)
                    freed(nc.scalar.activation(thB[:, :], p[:, 0:SEQ], ACT.Tanh, scale=0.5), ("proj", n))
                elif t == "gA":
                    if j >= 2:
                        act.wait_ge(S("mixed"), j // 2 * 2)
                    freed(nc.scalar.activation(thA[:, j % 2, :], p[:, 0:SEQ], ACT.Tanh, scale=0.5), ("proj", n))
                else:
                    if j >= 2:
                        act.wait_ge(S("pooled"), j // 2 * 2)
                    freed(nc.scalar.activation(pt[:, j % 2, :], p[:, 0:L], ACT.Copy), ("proj", n))

            def silu(t, h):
                i = LIST[t]
                act.wait_ge(S("conv"), 3 * h + i + 1)
                if h >= 3:
                    act.wait_ge(S("scan_done"), h - 2)
                if h < 3:
                    act.wait_ge(S("consts"), CONSTS["kqv_zero"])
                nc.scalar.activation(kqv[:, h % 3, i, PAD:LP], acc[:, i, :], ACT.Silu).then_inc(S("silu"), 1)

            def copy(dst, src, key, done, **kw):
                ins = nc.scalar.activation(dst, src, ACT.Copy, **kw)
                freed(ins, key)
                act.wait_ge(free[WHERE[key][0]], WHERE[key][1] + 1)
                act.sem_inc(done, 1)

            for step in ORDER:
                if step[0] == "take":
                    take_tile(*step[1:])
                if step[0] == "silu":
                    silu(*step[1:])
                if step[0] == "norm":
                    h = step[1]
                    act.wait_ge(S("silu"), 3 * h + 2)
                    if h >= 1:
                        act.wait_ge(S("nsum"), 2 * h)
                    for i in range(2):
                        nc.scalar.activation(sq[:, i, :], kqv[:, h % 3, i, :], ACT.Square).then_inc(S("sq"), 1)
                    if h >= 1:
                        act.wait_ge(S("kn"), 2 * h)
                    for i, name in enumerate(("nk", "nq")):
                        p = filled(act, (name, h))
                        freed(nc.scalar.activation(rn[:, i, :], p[:, 0:LP], ACT.Sqrt, bias=eps[:]), (name, h))
                if step[0] == "turn":
                    h = step[1]
                    p = filled(act, ("AT", h))
                    if h >= 1:
                        act.wait_ge(S("OT"), NL * h)
                        act.wait_ge(S("base"), 2 * h)
                    nc.scalar.activation(ATb[:], p[0:CH, 0:LP].rearrange("p (c t) -> p c t", c=3), ACT.Copy).then_inc(S("AT"), 1)
                    act.wait_ge(S("AT"), h + 1)
                    act.sem_inc(free[WHERE[("AT", h)][0]], 1)
                if step[0] == "lx":
                    h, lv = step[1:]
                    p = filled(act, ("X", h, lv))
                    if h or lv:
                        act.wait_ge(S("ly"), NL * h + lv)
                    nc.scalar.activation(Xb[:], p[0:CH, 0:LP].rearrange("p (c t) -> p c t", c=3), ACT.Copy).then_inc(S("X"), 1)
                    act.wait_ge(S("X"), NL * h + lv + 1)
                    act.sem_inc(free[WHERE[("X", h, lv)][0]], 1)
                if step[0] == "solve":
                    h = step[1]
                    p = filled(act, ("u", h))
                    if h >= 2:
                        act.wait_ge(S("scan_done"), h - 1)
                        act.wait_ge(S("vn"), 2 * (h - 1))
                    nc.scalar.activation(ub[:, h % 2], p[0:CH, 0:NC_ * P].rearrange("p (c t) -> p c t", c=3), ACT.Copy).then_inc(S("u"), 1)
                    act.wait_ge(S("u"), h + 1)
                    act.sem_inc(free[WHERE[("u", h)][0]], 1)
                    p = filled(act, ("wT", h))
                    nc.scalar.activation(wT[:, h % 2], p[:, 0:LP].rearrange("p (c t) -> p c t", c=3), ACT.Copy).then_inc(S("wT"), 1)
                    act.wait_ge(S("wT"), h + 1)
                    act.sem_inc(free[WHERE[("wT", h)][0]], 1)
                if step[0] == "sa":
                    h, c = step[1:]
                    p = filled(act, ("o1", h, c))
                    if h >= 1:
                        act.wait_ge(S("o"), 3 * (h - 1) + c + 1)
                    nc.scalar.activation(o1s[:, c - 1, :], p[0:CH, 0:P], ACT.Copy, scale=small[0:CH, EGAM_, c * 8 + h:c * 8 + h + 1]).then_inc(S("o1"), 1)
                    act.wait_ge(S("o1"), 2 * h + c)
                    act.sem_inc(free[WHERE[("o1", h, c)][0]], 1)
                if step[0] == "onorm":
                    h = step[1]
                    act.wait_ge(S("o"), 3 * (h + 1))
                    for c in range(NC_):
                        if h or c:
                            act.wait_ge(S("oss"), 3 * h + c)
                        if h:
                            act.wait_ge(S("ors"), h)
                        nc.scalar.activation(o1s[:, 0, :], osb[:, c, :], ACT.Square, scale=float(P) ** -0.5,
                                             accum_out=small[0:CH, OSS_, c:c + 1]).then_inc(S("oss"), 1)
                    act.wait_ge(S("oss"), 3 * h + 3)
                    nc.scalar.activation(small[0:CH, ORS_, 4:7], small[0:CH, OSS_, 0:3], ACT.Sqrt, bias=eps[0:CH]).then_inc(S("orms"), 1)

            junk2 = late[:, 0:D]
            for i in range(TT):
                act.wait_ge(S("res"), 2 * (i + 1))
                if i:
                    act.wait_ge(S("ms"), 3 + i)
                nc.scalar.activation(junk2, hres[:, i, :], ACT.Square, scale=1.0 / 32.0,
                                     accum_out=rs[:, i, 0:1]).then_inc(S("ms"), 1)
            for i in range(TT):
                act.wait_ge(S("ms"), 3 + TT)
                nc.scalar.activation(rs[:, i, 22:23], rs[:, i, 0:1], ACT.Sqrt, bias=eps[:]).then_inc(S("rms"), 1)
            for k in range(1, KT, 2):
                act.wait_ge(S("turned"), KT + k + 1)
                nc.scalar.activation(x2T[:, k, :], pb[k % 4][:, 0:SEQ], ACT.Copy, scale=prmT[:, ROW_FFN + k:ROW_FFN + k + 1]).then_inc(S("uT"), 1)
            for i in range(TT):
                act.wait_ge(S("rexp_in"), i + 1)
                nc.scalar.activation(rs[:, i, 8:12], rt[:, i, 0, 0:GROUPS], ACT.Exp, bias=rs[:, i, 2:3],
                                     accum_out=rs[:, i, 3:4]).then_inc(S("rexp"), 1)
                nc.scalar.activation(rs[:, i, 4:5], rs[:, i, 5:6], ACT.Exp).then_inc(S("rexp"), 1)

            def one_pass(ps):
                base = EXPERTS * ps

                def one(e, k, left, first):
                    n = e + base
                    act.wait_ge(S("gate"), n + 1)
                    if not first:
                        act.wait_ge(S("hmid"), n)
                    nc.scalar.activation(sgate[:, 0, :], pb[1][:, 0:FF // 2], ACT.Silu).then_inc(S("sgate"), 1)
                    act.wait_ge(S("y"), n + 1)
                    if left is not None:
                        act.wait_ge(S(f"y_left{k}"), left)
                    nc.scalar.activation(yout[k], pb[4][:], ACT.Copy).then_inc(S("yout"), 1)

                used = [ps * uses(EXPERTS, k, ROWS_BUF) for k in range(ROWS_BUF)]
                for e in range(ROWS_BUF):
                    one(e, e, 16 * used[e] if ps else None, ps == 0 and e == 0)
                with act.Fori(1, EXPERTS // ROWS_BUF) as i:
                    for j in range(ROWS_BUF):
                        one(i * ROWS_BUF + j, j, i * 16 + 16 * used[j], False)
                for e in range(EXPERTS // ROWS_BUF * ROWS_BUF, EXPERTS):
                    k = e % ROWS_BUF
                    one(e, k, 16 * (used[k] + e // ROWS_BUF), False)

            one_pass(0)
            overflow(act, one_pass)
            for i in range(TT):
                act.wait_ge(S("fin_h"), i + 1)
                if i:
                    act.wait_ge(S("ms"), 3 + TT + i)
                nc.scalar.activation(ring[:, 6, 0:D], hres[:, i, :], ACT.Square, scale=1.0 / 32.0,
                                     accum_out=rs[:, i, 12:13]).then_inc(S("ms"), 1)
            for i in range(TT):
                act.wait_ge(S("ms"), 3 + TT + i + 1)
                nc.scalar.activation(rs[:, i, 23:24], rs[:, i, 12:13], ACT.Sqrt, bias=eps[:]).then_inc(S("rms"), 1)

        @block.gpsimd
        def _(pool):
            done = [0]

            def chain(ins):
                done[0] += 1
                ins.then_inc(S("pool_chain"), 1)
                pool.wait_ge(S("pool_chain"), done[0])

            chain(nc.gpsimd.memset(ident[:], 0.0))
            chain(nc.gpsimd.affine_select(out=ident[:], in_=ident[:], compare_op=ALU.not_equal, fill=1.0, base=0,
                                          pattern=[[-1, P]], channel_multiplier=1))
            pool.sem_inc(S("consts"), 1)
            nc.gpsimd.memset(ones[:], 1.0).then_inc(S("consts"), 1)
            nc.gpsimd.memset(eps[:], EPS).then_inc(S("consts"), 1)
            nc.gpsimd.memset(abT[:, 0:PAD], 0.0).then_inc(S("consts"), 1)
            chain(nc.gpsimd.memset(uincl[:], 1.0))
            chain(nc.gpsimd.affine_select(out=uincl[:], in_=uincl[:], compare_op=ALU.is_ge, fill=0.0, base=0,
                                          pattern=[[1, CH]], channel_multiplier=-1))
            chain(nc.gpsimd.memset(negs[:], 0.0))
            chain(nc.gpsimd.affine_select(out=negs[:, 0, :], in_=negs[:, 0, :], compare_op=ALU.is_gt, fill=NEG, base=0,
                                          pattern=[[-1, CH]], channel_multiplier=1))
            chain(nc.gpsimd.affine_select(out=negs[:, 1, :], in_=negs[:, 1, :], compare_op=ALU.is_ge, fill=NEG, base=0,
                                          pattern=[[1, CH]], channel_multiplier=-1))
            pool.sem_inc(S("consts"), 1)
            chain(nc.gpsimd.memset(mlow[:], 0.0))
            v = mlow[:].rearrange("p (a r) -> p a r", r=2)[:, :, 0]
            chain(nc.gpsimd.affine_select(out=v, in_=v, compare_op=ALU.not_equal, fill=1.0, base=-1,
                                          pattern=[[-2, CH // 2]], channel_multiplier=1))
            chain(nc.gpsimd.memset(mup[:], 0.0))
            for lv, b in enumerate([1] + LEVELS):
                if 2 * b <= CH and CH % (2 * b) == 0:
                    v = mup[:, lv, :].rearrange("p (a r) -> p a r", r=2 * b)[:, :, b:2 * b]
                    na, nb = CH // (2 * b), b
                elif b == 32:
                    v, na, nb = mup[:, lv, 32:64].rearrange("p (a r) -> p a r", a=1), 1, 32
                else:
                    v, na, nb = mup[:, lv, b:CH].rearrange("p (a r) -> p a r", a=1), 1, CH - b
                chain(nc.gpsimd.memset(v, 1.0))
                chain(nc.gpsimd.affine_select(out=v, in_=v, compare_op=ALU.is_ge, fill=0.0, base=0,
                                              pattern=[[-2 * b, na], [0, nb]], channel_multiplier=1))
                chain(nc.gpsimd.affine_select(out=v, in_=v, compare_op=ALU.is_ge, fill=0.0, base=b - 1,
                                              pattern=[[2 * b, na], [0, nb]], channel_multiplier=-1))
            pool.sem_inc(S("consts"), 1)
            for b in range(3):
                nc.gpsimd.memset(kqv[:, b, :, 0:PAD], 0.0).then_inc(S("pool_chain"), 1)
                done[0] += 1
            pool.wait_ge(S("pool_chain"), done[0])
            pool.sem_inc(S("consts"), 1)
            for h in range(HEADS):
                pool.wait_ge(S("Dexp"), h + 1)
                pool.wait_ge(S("beta"), 1)
                nc.gpsimd.tensor_tensor(Dm[:, h], Dm[:, h],
                                        plane3(NBETA_)[:, :, h:h + 1].to_broadcast([CH, NC_, CH]), ALU.mult).then_inc(S("Dm"), 1)

            pools = [0]

            def window(j):
                g = j // 2
                b = j % 2
                src = pt[:, b, :]
                pool.wait_ge(free[WHERE[("proj", TILE_OF[("P", j)])][0]], WHERE[("proj", TILE_OF[("P", j)])][1] + 1)
                lo = 0
                a, n = src, 0
                for s in range(g + 1):
                    w = 1 << s
                    dst = ps2[:, s % 2, :]
                    lo += w
                    pools[0] += 1
                    nc.gpsimd.tensor_tensor(dst[:, lo:L], a[:, lo:L], a[:, lo - w:L - w], ALU.add).then_inc(S("win_chain"), 1)
                    pool.wait_ge(S("win_chain"), pools[0])
                    a = dst
                pools[0] += 1
                nc.gpsimd.tensor_scalar(ps2[:, (g + 1) % 2, META:L], a[:, META:L], 1.0 / (2 << g), None, ALU.mult).then_inc(S("win_chain"), 1)
                pool.wait_ge(S("win_chain"), pools[0])
                if j >= 2:
                    pool.wait_ge(S("mix"), j // 2 * 2)
                nc.gpsimd.tensor_tensor(pooled[:, b, :], ps2[:, (g + 1) % 2, META:L], src[:, META:L], ALU.subtract).then_inc(S("pooled"), 1)
                pool.wait_ge(S("pooled"), j + 1)

            for step in ORDER:
                if step[0] == "take" and step[2] == "P":
                    window(step[3])
                if step[0] == "turn":
                    h = step[1]
                    pool.wait_ge(S("AT"), h + 1)
                    for lv in range(NL):
                        n = NL * h + lv
                        if n >= 3:
                            pool.wait_ge(S("lxp"), n - 2)
                        nc.gpsimd.tensor_tensor(OTb[:, n % 3], ATb[:], mup[:, 1 + lv:2 + lv, :].to_broadcast([CH, NC_, CH]), ALU.mult).then_inc(S("OT"), 1)

            chain(nc.gpsimd.iota(iota_e[:], pattern=[[1, EXPERTS]], base=0, channel_multiplier=0, allow_small_or_imprecise_dtypes=True))
            chain(nc.gpsimd.iota(iota_g[:], pattern=[[1, GROUPS], [0, PER_GROUP]], base=0, channel_multiplier=0, allow_small_or_imprecise_dtypes=True))
            chain(nc.gpsimd.iota(iota_c[:], pattern=[[0, P // SLOTS], [1, SLOTS]], base=0, channel_multiplier=0, allow_small_or_imprecise_dtypes=True))
            chain(nc.gpsimd.iota(iota_t[:], pattern=[[2 * P, TT]], base=-int(BIG), channel_multiplier=2, allow_small_or_imprecise_dtypes=True))
            chain(nc.gpsimd.memset(halfof[:], BIG + 1.0))
            chain(nc.gpsimd.affine_select(out=halfof[:], in_=halfof[:], compare_op=ALU.is_ge, fill=BIG, base=-SLOTS,
                                          pattern=[[0, 1]], channel_multiplier=1))
            chain(nc.gpsimd.memset(before[:], 1.0))
            chain(nc.gpsimd.affine_select(out=before[:], in_=before[:], compare_op=ALU.is_gt, fill=0.0, base=0,
                                          pattern=[[1, P]], channel_multiplier=-1))
            pool.wait_ge(S("outproj"), 1)
            chain(nc.gpsimd.memset(xg[:], 0.0))
            pool.sem_inc(S("rconst"), 1)
            for i in range(TT):
                pool.wait_ge(S("xn"), i + 1)
                nc.gpsimd.dma_start(xn_dram.rearrange("(t b) d -> t (b d)", b=2)[i * P:(i + 1) * P, :], xn[:, i, :]).then_inc(S("xn_out"), 16)

            def one_pass(ps):
                base = EXPERTS * ps
                pool.wait_ge(S("lists"), ps + 1)
                pool.wait_ge(S("xn_out"), 32)

                def gather(e, k, first):
                    n = e + base
                    if not first:
                        pool.wait_ge(S("xT"), n - (ROWS_BUF - 1))
                    nc.gpsimd.tensor_copy(gcol[:, k:k + 1], gidx[:, bass.ds(e, 1)]).then_inc(S("gcol"), 1)
                    pool.wait_ge(S("gcol"), n + 1)
                    pool.sem_inc(S("go"), 1)
                    nc.gpsimd.indirect_dma_start(out=xg[:, k, :], out_offset=None, in_=xn_dram,
                                                 in_offset=bass.IndirectOffsetOnAxis(ap=gcol[:, k:k + 1], axis=0),
                                                 bounds_check=2 * SEQ - 1, oob_is_err=False).then_inc(S(f"xg_land{k}"), 16)

                def scatter(e, k, left):
                    n = e + base
                    if left is not None:
                        pool.wait_ge(S(f"y_left{k}"), left)
                    nc.gpsimd.tensor_copy(scol[:, k:k + 1], sidx[:, bass.ds(e, 1)]).then_inc(S("scol"), 1)
                    pool.wait_ge(S("scol"), n + 1)
                    pool.wait_ge(S("yout"), n + 1)
                    pool.sem_inc(S("go"), 1)
                    nc.gpsimd.indirect_dma_start(out=y_dram, out_offset=bass.IndirectOffsetOnAxis(ap=scol[:, k:k + 1], axis=0),
                                                 in_=yout[k], in_offset=None,
                                                 bounds_check=4 * SEQ - 1, oob_is_err=False).then_inc(S(f"y_left{k}"), 16)

                used = [ps * uses(EXPERTS, k, ROWS_BUF) for k in range(ROWS_BUF)]
                for e in range(LEAD):
                    gather(e, e, ps == 0)
                for e in range(ROWS_BUF):
                    gather(e + LEAD, (e + LEAD) % ROWS_BUF, ps == 0 and e + LEAD < ROWS_BUF)
                    scatter(e, e, 16 * used[e] if ps else None)
                with pool.Fori(1, EXPERTS // ROWS_BUF - 1) as i:
                    for j in range(ROWS_BUF):
                        gather(i * ROWS_BUF + (j + LEAD), (j + LEAD) % ROWS_BUF, False)
                        scatter(i * ROWS_BUF + j, j, i * 16 + 16 * used[j])
                for e in range((EXPERTS // ROWS_BUF - 1) * ROWS_BUF, EXPERTS):
                    if e + LEAD < EXPERTS:
                        gather(e + LEAD, (e + LEAD) % ROWS_BUF, False)
                    k = e % ROWS_BUF
                    scatter(e, k, 16 * (used[k] + e // ROWS_BUF))
                for k in range(ROWS_BUF):
                    pool.wait_ge(S(f"y_left{k}"), 16 * (ps + 1) * uses(EXPERTS, k, ROWS_BUF))

            one_pass(0)
            overflow(pool, one_pass)
            pool.sem_inc(S("y_all"), 1)

        @block.vector
        def _(dve):
            V = nc.vector
            counts = {"dve_chain": 0, "dve_chain_over": 0, "dve_chain_last": 0}
            which = ["dve_chain"]

            def chain(ins):
                counts[which[0]] += 1
                ins.then_inc(S(which[0]), 1)
                dve.wait_ge(S(which[0]), counts[which[0]])

            dve.wait_ge(S("rms"), 2)
            chain(V.reciprocal(small[:, RS_, 0:2], small[:, MS_, 4:6]))
            chain(V.reciprocal(small[0:META, RS_, 2:3], small[0:META, MS_, 6:7]))
            for i in range(3):
                rows = META if i == 2 else P
                src = hn[0:META, 2, :] if i == 2 else hres[:, i, :]
                V.tensor_scalar(hn[0:rows, i, :], src, small[0:rows, RS_, i:i + 1], None, ALU.mult).then_inc(S("hn"), 1)
            dve.wait_ge(S("prmp"), 1)
            V.tensor_copy(prmT[:], pb[7][:, 0:ROWS]).then_inc(S("prmT"), 1)
            dve.wait_ge(S("prmT"), 1)
            chain(V.tensor_scalar(halfs[:], prmT[:, ROW_POOL:ROWS], 0.5, None, ALU.mult))
            for k in range(0, KT, 2):
                dve.wait_ge(S("turned"), k + 1)
                V.tensor_scalar(uT[:, k, :], pb[k % 4][:, 0:L], prmT[:, ROW_MIX + k:ROW_MIX + k + 1], None, ALU.mult).then_inc(S("uTd"), 1)
            dve.wait_ge(S("abt"), 1)
            dve.wait_ge(S("params_land"), 8 * 16)
            abp = pb[5][0:CH, 0:48].rearrange("p (c n) -> p c n", c=3)
            V.tensor_tensor(plane3(X_), abp[:, :, 0:8], bc8[:, 1:2, :].to_broadcast([CH, 3, 8]), ALU.add).then_inc(S("xa"), 1)
            dve.wait_ge(S("xa"), 1)
            chain(V.tensor_scalar(plane(RL_), plane(X_), 0.0, None, ALU.max))
            dve.wait_ge(S("lnp"), 1)
            chain(V.tensor_tensor(plane(SP_), plane(RL_), plane(LN_), ALU.add))
            dve.wait_ge(S("ea"), 1)
            V.scalar_tensor_tensor(plane3(G_), plane3(SP_), -1.0, bc8[:, 2:3, :].to_broadcast([CH, 3, 8]), ALU.mult, ALU.mult).then_inc(S("g"), 1)
            dve.wait_ge(S("eb"), 1)
            chain(V.tensor_scalar(plane(BETA_), plane(EB_), 1.0, None, ALU.add))
            chain(V.reciprocal(plane(BETA_), plane(BETA_)))
            V.tensor_scalar(plane(NBETA_), plane(BETA_), -1.0, None, ALU.mult).then_inc(S("beta"), 1)
            dve.wait_ge(S("gamp"), 1)
            chain(V.tensor_copy(plane(GAM_), pb[6][0:CH, 0:24]))
            V.tensor_tensor(plane(GL_), pb[6][0:CH, 32:56], plane(GAM_), ALU.subtract).then_inc(S("kdarg"), 1)
            dve.wait_ge(S("egam"), 1)
            chain(V.tensor_tensor(plane(SKB_), plane(BETA_), plane(EGAM_), ALU.mult))
            dve.wait_ge(S("consts"), CONSTS["masks"])
            dve.wait_ge(S("turned"), KT)
            for h in range(HEADS):
                dve.wait_ge(S("gamB"), h + 1)
                chain(V.tensor_tensor(tmpT[:, h % 2], pb[h % 4][0:CH, 0:LP].rearrange("p (c t) -> p c t", c=3),
                                      plane3(GAM_)[:, :, h:h + 1].to_broadcast([CH, 3, CH]), ALU.subtract))
                V.tensor_tensor(Dm[:, h], negs[:, 0:1, :].to_broadcast([CH, 3, CH]), tmpT[:, h % 2], ALU.subtract).then_inc(S("darg"), 1)
                V.tensor_tensor(DT[:, h], negs[:, 1:2, :].to_broadcast([CH, 3, CH]), tmpT[:, h % 2], ALU.add).then_inc(S("darg"), 1)
                dve.wait_ge(S("darg"), 2 * h + 2)
                dve.sem_inc(S("gamB_free"), 1)

            def c3(ap, n=CH):
                return ap.rearrange("p (c t) -> p c t", c=NC_)

            def per_token(i, h, n):
                return plane3(i)[:, :, h:h + 1].to_broadcast([CH, NC_, n])

            for step in ORDER:
                kind = step[0]
                if kind == "take":
                    n, t, j = step[1:]
                    if t in "kqv":
                        i = LIST[t]
                        p = filled(dve, ("proj", n))
                        dve.wait_ge(S("tap3"), 3 * j + i + 1)
                        col = {"q": 0, "k": 8, "v": 16}[t] + j
                        for tap in (2, 1, 0):
                            s = 3 - tap
                            ins = V.scalar_tensor_tensor(acc[:, i, s:L], p[:, 0:L - s], prmT[:, tap * 24 + col:tap * 24 + col + 1],
                                                         acc[:, i, s:L], ALU.mult, ALU.add)
                            if tap:
                                chain(ins)
                            else:
                                ins.then_inc(S("conv"), 1)
                                dve.wait_ge(S("conv"), 3 * j + i + 1)
                                dve.sem_inc(free[WHERE[("proj", n)][0]], 1)
                    if t == "gB":
                        b, u = WHERE[("proj", n)]
                        dve.wait_ge(free[b], u + 1)
                        bz, uz = WHERE[("proj", TILE_OF[("z", j)])]
                        dve.wait_ge(free[bz], uz + 1)
                        V.scalar_tensor_tensor(zs[:, j % 2, :], thB[:, :], 1.0, zs[:, j % 2, :], ALU.add, ALU.mult).then_inc(S("zg"), 1)
                if kind == "norm":
                    h = step[1]
                    for i, name in enumerate(("nk", "nq")):
                        b, u = WHERE[(name, h)]
                        dve.wait_ge(free[b], u + 1)
                        chain(V.reciprocal(rn[:, i, :], rn[:, i, :]))
                        src = kqv[:, h % 3, i, :]
                        V.scalar_tensor_tensor(src, src, 1.0 if i == 0 else float(P) ** -0.5, rn[:, i, :], ALU.mult, ALU.mult).then_inc(S("kn"), 1)
                if kind == "gram":
                    h = step[1]
                    dve.wait_ge(S("Dm"), h + 1)
                    dve.wait_ge(S("DTexp"), h + 1)
                    p = filled(dve, ("G", h))
                    if h:
                        dve.wait_ge(S("ATp"), h)
                    ins = V.tensor_tensor(Ab[:], c3(p[0:CH, 0:LP]), Dm[:, h], ALU.mult)
                    ins.then_inc(S("A"), 1)
                    dve.wait_ge(S("A"), h + 1)
                    dve.sem_inc(free[WHERE[("G", h)][0]], 1)
                    if h == 0:
                        dve.wait_ge(S("consts"), CONSTS["mups"])
                        dve.wait_ge(S("consts"), CONSTS["ident"])
                    chain(V.tensor_tensor(tmpT[:, 0], Ab[:], mlow[:].rearrange("p (o t) -> p o t", o=1).to_broadcast([CH, 3, CH]), ALU.mult))
                    if h:
                        dve.wait_ge(S("ly"), NL * h)
                        dve.wait_ge(S("solved"), h)
                    V.tensor_tensor(Tb[:], tmpT[:, 0], ident[0:CH, 0:CH].rearrange("p (o t) -> p o t", o=1).to_broadcast([CH, 3, CH]), ALU.add).then_inc(S("base"), 1)
                    p = filled(dve, ("QK", h))
                    freed(V.tensor_tensor(DT[:, h], c3(p[0:CH, 0:LP]), DT[:, h], ALU.mult), ("QK", h))
                    dve.wait_ge(free[WHERE[("QK", h)][0]], WHERE[("QK", h)][1] + 1)
                    if h >= 2:
                        dve.wait_ge(S("scan_done"), h - 1)
                    p = filled(dve, ("KT", h))
                    chain(V.tensor_tensor(Kb[:, h % 2], c3(p[0:CH, 0:NC_ * P]), per_token(SKB_, h, P), ALU.mult))
                    if h == 0:
                        dve.wait_ge(S("egam"), 3)
                    freed(V.tensor_tensor(Kd[:, h % 2], c3(p[0:CH, 0:NC_ * P]), per_token(KD_, h, P), ALU.mult), ("KT", h))
                    dve.wait_ge(free[WHERE[("KT", h)][0]], WHERE[("KT", h)][1] + 1)
                    p = filled(dve, ("VT", h))
                    freed(V.tensor_tensor(Vb[:, h % 2], c3(p[0:CH, 0:NC_ * P]), per_token(BETA_, h, P), ALU.mult), ("VT", h))
                    dve.wait_ge(free[WHERE[("VT", h)][0]], WHERE[("VT", h)][1] + 1)
                    dve.sem_inc(S("kv"), 1)
                if kind == "turn":
                    h = step[1]
                    dve.wait_ge(S("AT"), h + 1)
                    chain(V.tensor_tensor(tmpT[:, 1], ATb[:], mup[:, 0:1, :].to_broadcast([CH, 3, CH]), ALU.mult))
                    V.tensor_tensor(Ub[:], tmpT[:, 1], ident[0:CH, 0:CH].rearrange("p (o t) -> p o t", o=1).to_broadcast([CH, 3, CH]), ALU.add).then_inc(S("base"), 1)
                    dve.wait_ge(S("base"), 2 * h + 2)
                if kind == "ly":
                    h, lv = step[1:]
                    if lv < NL - 1:
                        p = filled(dve, ("Y", h, lv))
                        dve.wait_ge(S("ly"), NL * h + lv + 1)
                        freed(V.tensor_tensor(Tb[:], c3(p[0:CH, 0:LP]), Tb[:], ALU.add), ("Y", h, lv))
                    p = filled(dve, ("YT", h, lv))
                    dve.wait_ge(S("ly"), NL * h + lv + 1)
                    freed(V.tensor_tensor(Ub[:], c3(p[0:CH, 0:LP]), Ub[:], ALU.add), ("YT", h, lv))
                    if lv < NL - 1:
                        b, u = WHERE[("Y", h, lv)]
                        dve.wait_ge(free[b], u + 1)
                    b, u = WHERE[("YT", h, lv)]
                    dve.wait_ge(free[b], u + 1)
                    dve.sem_inc(S("TU"), 1)
                if kind in ("s0", "sb"):
                    h = step[1]
                    c = 0 if kind == "s0" else step[2]
                    key = ("os",) + tuple(step[1:])
                    p = filled(dve, key)
                    if h:
                        dve.wait_ge(S("ors"), h)
                        dve.wait_ge(S("oTp"), h)
                    if c == 0:
                        V.tensor_copy(osb[:, 0, :], p[0:CH, 0:P]).then_inc(S("o"), 1)
                        if h:
                            dve.wait_ge(S("sap"), 4 * h)
                        V.tensor_copy(St[:, 0, :], p[:, P:2 * P]).then_inc(S("S"), 1)
                        dve.wait_ge(S("S"), 2 * h + 1)
                    else:
                        dve.wait_ge(S("o1"), 2 * h + c)
                        V.tensor_tensor(osb[:, c, :], p[0:CH, 0:P], o1s[:, c - 1, :], ALU.add).then_inc(S("o"), 1)
                        if c == 1:
                            if h:
                                dve.wait_ge(S("sap"), 4 * h)
                            V.scalar_tensor_tensor(St[:, 1, :], St[:, 0, :], small[:, CD_, c * 8 + h:c * 8 + h + 1],
                                                   p[:, P:2 * P], ALU.mult, ALU.add).then_inc(S("S"), 1)
                            dve.wait_ge(S("S"), 2 * h + 2)
                    dve.wait_ge(S("o"), 3 * h + c + 1)
                    dve.sem_inc(free[WHERE[key][0]], 1)
                if kind == "sa":
                    h, c = step[1:]
                    p = filled(dve, ("ws", h, c))
                    if h:
                        dve.wait_ge(S("scan_done"), h)
                    V.scalar_tensor_tensor(vn[:, c - 1, :], p[0:CH, 0:P], -1.0, ub[:, h % 2, c, :], ALU.mult, ALU.add).then_inc(S("vn"), 1)
                    dve.wait_ge(S("vn"), 2 * h + c)
                    dve.sem_inc(free[WHERE[("ws", h, c)][0]], 1)
                if kind == "onorm":
                    h = step[1]
                    dve.wait_ge(S("orms"), h + 1)
                    chain(V.reciprocal(small[0:CH, ORS_, 0:3], small[0:CH, ORS_, 4:7]))
                    V.tensor_tensor(osb[:], osb[:], small[0:CH, ORS_, 0:3].rearrange("p (c o) -> p c o", o=1).to_broadcast([CH, 3, P]), ALU.mult).then_inc(S("ors"), 1)
                if kind == "out":
                    h = step[1]
                    p = filled(dve, ("oT", h))
                    dve.wait_ge(S("zg"), h + 1)
                    V.scalar_tensor_tensor(merged[:, h, :], p[:, REAL:LP], halfs[:, 8:9], zs[:, h % 2, :], ALU.mult, ALU.mult).then_inc(S("out"), 1)
                    dve.wait_ge(S("out"), h + 1)
                    dve.sem_inc(free[WHERE[("oT", h)][0]], 1)
                if kind == "mix":
                    j = step[1]
                    for d in range(2):
                        ch = j - 1 + d
                        p = filled(dve, (f"m{d}", j))
                        b, u = WHERE[("proj", TILE_OF[("gA", ch)])]
                        dve.wait_ge(free[b], u + 1)
                        ins = V.scalar_tensor_tensor(thA[:, d, :], thA[:, d, :], 1.0, p[:, 0:SEQ], ALU.add, ALU.mult)
                        freed(ins, (f"m{d}", j))
                        dve.wait_ge(free[WHERE[(f"m{d}", j)][0]], WHERE[(f"m{d}", j)][1] + 1)
                        dve.wait_ge(S("out"), ch + 1)
                        V.scalar_tensor_tensor(merged[:, ch, :], thA[:, d, :], halfs[:, ch:ch + 1], merged[:, ch, :], ALU.mult, ALU.add).then_inc(S("mixed"), 1)
                        dve.wait_ge(S("mixed"), ch + 1)

            for i in range(TT):
                for half in range(2):
                    dve.wait_ge(S("outproj"), 1)
                    o = hres[:, i, half * 512:(half + 1) * 512]
                    V.tensor_tensor(o, pb[2 * i + half][:], o, ALU.add).then_inc(S("res"), 1)
            for i in range(TT):
                dve.wait_ge(S("rms"), 2 + TT)
                chain(V.reciprocal(rs[:, i, 1:2], rs[:, i, 22:23]))
                V.tensor_scalar(xn[:, i, :], hres[:, i, :], rs[:, i, 1:2], None, ALU.mult).then_inc(S("xn"), 1)
            for k in range(KT):
                b, half = k % 4, k // 4
                V.tensor_scalar(wff[:, 2 * b + half, :], ones[:, 0:SLOTS], prmT[:, ROW_FFN + k:ROW_FFN + k + 1], None, ALU.mult).then_inc(S("wff"), 1)
            for k in range(0, KT, 2):
                dve.wait_ge(S("turned"), KT + k + 1)
                V.tensor_scalar(x2T[:, k, :], pb[k % 4][:, 0:SEQ], prmT[:, ROW_FFN + k:ROW_FFN + k + 1], None, ALU.mult).then_inc(S("uTd"), 1)
            dve.wait_ge(S("rconst"), 1)
            dve.wait_ge(S("rout_land"), 64)
            for i in range(TT):
                dve.wait_ge(S("logits"), i + 1)
                lg, le = rt[:, i, 0, 0:8], rt[:, i, 1, :]
                chain(V.memset(rt[:, i, 0, 0:8], NEG))
                chain(V.tensor_tensor(rt[:, i, 0, 0:GROUPS], pb[4 + i][:, 0:GROUPS], rbias[:, 0:GROUPS], ALU.add))
                chain(V.tensor_tensor(le, pb[4 + i][:, GROUPS:36], rbias[:, GROUPS:36], ALU.add))
                chain(V.max(rt[:, i, 2, 0:8], lg))
                chain(V.max_index(ru[:, i, 0:8], rt[:, i, 2, 0:8], lg))
                chain(V.tensor_copy(rs[:, i, 13:14], ru[:, i, 0:1]))
                chain(V.tensor_scalar(rt[:, i, 3, :], iota_g[:], rs[:, i, 13:14], 1.0, ALU.is_equal, ALU.subtract))
                chain(V.scalar_tensor_tensor(rt[:, i, 4, :], rt[:, i, 3, :], -NEG, le, ALU.mult, ALU.add))
                chain(V.max(rt[:, i, 5, 0:8], rt[:, i, 4, :]))
                chain(V.max_index(ru[:, i, 8:16], rt[:, i, 5, 0:8], rt[:, i, 4, :]))
                chain(V.tensor_copy(rs[:, i, 14:16], ru[:, i, 8:10]))
                for k in range(2):
                    chain(V.tensor_scalar(rt[:, i, 6 + k, :], iota_e[:], rs[:, i, 14 + k:15 + k], None, ALU.is_equal))
                V.tensor_tensor(rt[:, i, 8, :], rt[:, i, 6, :], rt[:, i, 7, :], ALU.add).then_inc(S("picked"), 1)
                chain(V.tensor_scalar(rs[:, i, 2:3], rt[:, i, 2, 0:1], -1.0, None, ALU.mult))
                V.tensor_tensor(rs[:, i, 5:6], rt[:, i, 5, 1:2], rt[:, i, 5, 0:1], ALU.subtract).then_inc(S("rexp_in"), 1)
            dve.wait_ge(S("pos"), 3)
            for i in range(TT):
                for k in range(2):
                    chain(V.tensor_tensor(rt[:, i, 9 + k, :], rt[:, i, 6 + k, :], pb[6][:, 32 * i:32 * i + 32], ALU.mult))
                    chain(V.tensor_reduce(rs[:, i, 16 + k:17 + k], rt[:, i, 9 + k, :], AX.X, ALU.add))
            chain(V.max(most[:], pb[6][:, 64:96]))
            V.tensor_copy(mosti[:], most[:, 0:1]).then_inc(S("most"), 1)

            def build_lists(ps):
                if ps:
                    chain(V.tensor_scalar(rs[:, 0, 16:18], rs[:, 0, 16:18], -float(SLOTS), None, ALU.add))
                    chain(V.tensor_scalar(rs[:, 1, 16:18], rs[:, 1, 16:18], -float(SLOTS), None, ALU.add))
                    dve.wait_ge(S("scol"), EXPERTS * ps)
                    dve.wait_ge(S("gcol"), EXPERTS * ps)
                for i in range(TT):
                    for k in range(2):
                        V.tensor_scalar(hot[:, 2 * i + k, :], iota_c[:], rs[:, i, 16 + k:17 + k], iota_t[:, i:i + 1], ALU.is_equal, ALU.mult).then_inc(S("hot"), 1)
                dve.wait_ge(S("listp"), ps + 1)
                chain(V.tensor_scalar(lists[:, 0, :], pb[7][:, 0:EXPERTS], halfof[:, 0:1], None, ALU.add))
                chain(V.tensor_scalar(lists[:, 1, :], pb[7][:, EXPERTS:2 * EXPERTS], 0.0, float(2 * SEQ), ALU.not_equal, ALU.mult))
                chain(V.tensor_tensor(lists[:, 0, :], pb[7][:, EXPERTS:2 * EXPERTS], lists[:, 0, :], ALU.add))
                chain(V.tensor_copy(gidx[:], lists[:, 0, :]))
                chain(V.tensor_tensor(sidx[:], lists[:, 0, :], lists[:, 1, :], ALU.add))
                dve.sem_inc(S("lists"), 1)

            def one_pass(ps):
                base = EXPERTS * ps
                build_lists(ps)
                if ps == 0:
                    weights()

                def one(e, first):
                    n = e + base
                    dve.wait_ge(S("xT"), n + 1)
                    if not first:
                        dve.wait_ge(S("up"), n)
                    V.tensor_tensor(xgT[:, 0, :], pb[0][:], wff[:].rearrange("p k s -> p (k s)"), ALU.mult).then_inc(S("xgT"), 1)

                def mid(e, first):
                    n = e + base
                    dve.wait_ge(S("sgate"), n + 1)
                    dve.wait_ge(S("up"), n + 1)
                    if not first:
                        dve.wait_ge(S("hTp"), n)
                    V.tensor_tensor(hmid[:, 0, :], pb[2][:, 0:FF // 2], sgate[:, 0, :], ALU.mult).then_inc(S("hmid"), 1)
                    dve.wait_ge(S("hTp"), n + 1)
                    if not first:
                        dve.wait_ge(S("y"), n)
                    V.tensor_copy(hT[:, 0].rearrange("p a b -> p (a b)"), pb[3][:, 0:2 * P]).then_inc(S("hT"), 1)

                one(0, ps == 0)
                for e in range(3):
                    mid(e, ps == 0 and e == 0)
                    one(e + 1, False)
                with dve.Fori(1, EXPERTS // 3) as i:
                    for j in range(3):
                        mid(i * 3 + j, False)
                        one(i * 3 + (j + 1), False)
                for e in range(EXPERTS // 3 * 3, EXPERTS):
                    mid(e, False)
                    if e < EXPERTS - 1:
                        one(e + 1, False)

            def weights():
                for i in range(TT):
                    dve.wait_ge(S("rexp"), 2 * i + 2)
                    chain(V.reciprocal(rs[:, i, 6:7], rs[:, i, 3:4]))
                    chain(V.tensor_scalar(rs[:, i, 7:8], rs[:, i, 4:5], 1.0, None, ALU.add))
                    chain(V.reciprocal(rs[:, i, 18:19], rs[:, i, 7:8]))
                    chain(V.tensor_tensor(rs[:, i, 19:20], rs[:, i, 18:19], rs[:, i, 6:7], ALU.mult))
                    chain(V.tensor_tensor(rs[:, i, 20:21], rs[:, i, 19:20], rs[:, i, 4:5], ALU.mult))

            one_pass(0)
            which[0] = "dve_chain_over"
            overflow(dve, one_pass)
            which[0] = "dve_chain_last"
            for i in range(TT):
                for k in range(2):
                    dve.wait_ge(S(f"y_back{i}"), 32)
                    chain(V.scalar_tensor_tensor(hres[:, i, :], ring[:, 2 * i + k, 0:D], rs[:, i, 19 + k:20 + k], hres[:, i, :], ALU.mult, ALU.add))
                dve.sem_inc(S("fin_h"), 1)
            for i in range(TT):
                dve.wait_ge(S("rms"), 2 + TT + i + 1)
                chain(V.reciprocal(rs[:, i, 21:22], rs[:, i, 23:24]))
                dve.wait_ge(S("wf_land"), 16)
                V.scalar_tensor_tensor(ring[:, 7 + i, 0:D], hres[:, i, :], rs[:, i, 21:22], ring[:, 5, 0:D], ALU.mult, ALU.mult).then_inc(S("final"), 1)

        @block.tensor
        def _(pe):
            T = nc.tensor
            pe.wait_ge(S("consts"), CONSTS["ident"])
            pe.wait_ge(S("params_land"), 8 * 16)
            T.transpose(pb[7][:, 0:ROWS], prm[0:ROWS, :], ident[0:ROWS, 0:ROWS]).then_inc(S("prmp"), 1)
            pe.wait_ge(S("hn"), 3)
            for k in range(KT):
                if k >= 4:
                    pe.wait_ge(S("uT" if k % 2 else "uTd"), (k - 4) // 2 + 1)
                for i, (c0, rows) in enumerate(((META, P), (META + P, P), (0, META))):
                    ins = T.transpose(pb[k % 4][:, c0:c0 + rows], hn[0:rows, i, k * P:(k + 1) * P], ident[0:rows, 0:rows])
                ins.then_inc(S("turned"), 1)
            pe.wait_ge(S("uT"), KT // 2)
            pe.wait_ge(S("uTd"), KT // 2)
            pe.wait_ge(S("params_land"), 8 * 16)
            for k in range(KT):
                ins = T.matmul(pb[4][0:16, 0:L], wab[:, k, :], uT[:, k, :], start=(k == 0), stop=(k == KT - 1))
            ins.then_inc(S("ab"), 1)
            pe.wait_ge(S("abT"), 1)
            for c in range(NC_):
                ins = T.transpose(pb[5][0:CH, 16 * c:16 * c + 16], abT[:, c * CH:(c + 1) * CH], ident[0:16, 0:16])
            ins.then_inc(S("abt"), 1)
            pe.wait_ge(S("g"), 1)
            pe.wait_ge(S("consts"), CONSTS["masks"])
            pe.wait_ge(S("consts"), CONSTS["ones"])
            T.matmul(pb[6][0:CH, 0:24], uincl[:], plane(G_), start=True, stop=True)
            T.matmul(pb[6][:, 32:56], ones[0:CH, :], plane(G_), start=True, stop=True).then_inc(S("gamp"), 1)
            for h in range(HEADS):
                if h >= 4:
                    pe.wait_ge(S("gamB_free"), h - 3)
                for c in range(NC_):
                    ins = T.matmul(pb[h % 4][0:CH, c * CH:(c + 1) * CH], small[0:CH, G_, c * 8 + h:c * 8 + h + 1].to_broadcast([CH, CH]),
                                   uincl[:], start=True, stop=True)
                ins.then_inc(S("gamB"), 1)
            pe.wait_ge(S("gamB_free"), HEADS)
            pe.wait_ge(S("prmT"), 1)
            pe.wait_ge(S("eb"), 1)
            pe.wait_ge(S("kdarg"), 1)
            pe.wait_ge(S("egam"), 2)

            def cs(ap, c, n):
                return ap[:, c * n:(c + 1) * n]

            for step in ORDER:
                kind = step[0]
                if kind == "proj":
                    n, t, j, k0 = step[1:]
                    if k0 == 0:
                        pe.wait_ge(win_land[n % WIN_SLOTS], 16 * (n // WIN_SLOTS + 1))
                        bank(pe, ("proj", n))
                    p = pb[WHERE[("proj", n)][0]]
                    lo = 0 if t in "kqvP" else META
                    for k in range(k0, k0 + 2):
                        ins = T.matmul(p[:, 0:L - lo], win[:, n % WIN_SLOTS, k, :], uT[:, k, lo:L], start=(k == 0), stop=(k == KT - 1))
                    if k0 == KT - 2:
                        ins.then_inc(full[WHERE[("proj", n)][0]], 1)
                        pe.wait_ge(full[WHERE[("proj", n)][0]], WHERE[("proj", n)][1] + 1)
                        pe.sem_inc(S("tile_used"), 1)
                if kind == "norm":
                    h = step[1]
                    for i, name in enumerate(("nk", "nq")):
                        p = bank(pe, (name, h))
                        pe.wait_ge(S("sq"), 2 * h + i + 1)
                        T.matmul(p[:, 0:LP], ones[:], sq[:, i, :], start=True, stop=True).then_inc(full[WHERE[(name, h)][0]], 1)
                    pe.wait_ge(full[WHERE[("nq", h)][0]], WHERE[("nq", h)][1] + 1)
                    pe.sem_inc(S("nsum"), 2)
                if kind == "gram":
                    h = step[1]
                    b3 = h % 3
                    pe.wait_ge(S("kn"), 2 * h + 1)
                    p = bank(pe, ("G", h))
                    for c in range(NC_):
                        kc = kqv[:, b3, 0, c * CH:(c + 1) * CH]
                        ins = T.matmul(p[0:CH, c * CH:(c + 1) * CH], kc, kc, start=True, stop=True)
                    ins.then_inc(full[WHERE[("G", h)][0]], 1)
                    pe.wait_ge(S("kn"), 2 * h + 2)
                    p = bank(pe, ("QK", h))
                    for c in range(NC_):
                        ins = T.matmul(p[0:CH, c * CH:(c + 1) * CH], kqv[:, b3, 0, c * CH:(c + 1) * CH],
                                       kqv[:, b3, 1, c * CH:(c + 1) * CH], start=True, stop=True)
                    ins.then_inc(full[WHERE[("QK", h)][0]], 1)
                    pe.wait_ge(S("silu"), 3 * h + 3)
                    for i, name in ((0, "KT"), (2, "VT")):
                        p = bank(pe, (name, h))
                        for c in range(NC_):
                            ins = T.transpose(p[0:CH, c * P:(c + 1) * P], kqv[:, b3, i, c * CH:(c + 1) * CH], ident[:])
                        ins.then_inc(full[WHERE[(name, h)][0]], 1)
                if kind == "turn":
                    h = step[1]
                    pe.wait_ge(S("A"), h + 1)
                    p = bank(pe, ("AT", h))
                    for c in range(NC_):
                        ins = T.transpose(p[0:CH, c * CH:(c + 1) * CH], Ab[:, c, :], ident[0:CH, 0:CH])
                    ins.then_inc(full[WHERE[("AT", h)][0]], 1)
                    pe.wait_ge(full[WHERE[("AT", h)][0]], WHERE[("AT", h)][1] + 1)
                    pe.sem_inc(S("ATp"), 1)
                if kind == "lx":
                    h, lv = step[1:]
                    n = NL * h + lv
                    pe.wait_ge(S("OT"), n + 1)
                    if lv == 0:
                        pe.wait_ge(S("base"), 2 * h + 2)
                    if n:
                        pe.wait_ge(S("TU"), n)
                    p = bank(pe, ("X", h, lv))
                    for c in range(NC_):
                        ins = T.matmul(p[0:CH, c * CH:(c + 1) * CH], OTb[:, n % 3, c, :], Tb[:, c, :], start=True, stop=True)
                    ins.then_inc(full[WHERE[("X", h, lv)][0]], 1)
                    pe.wait_ge(full[WHERE[("X", h, lv)][0]], WHERE[("X", h, lv)][1] + 1)
                    pe.sem_inc(S("lxp"), 1)
                if kind == "ly":
                    h, lv = step[1:]
                    n = NL * h + lv
                    pe.wait_ge(S("X"), n + 1)
                    if lv < NL - 1:
                        p = bank(pe, ("Y", h, lv))
                        for c in range(NC_):
                            ins = T.matmul(p[0:CH, c * CH:(c + 1) * CH], Ub[:, c, :], Xb[:, c, :], start=True, stop=True)
                        ins.then_inc(full[WHERE[("Y", h, lv)][0]], 1)
                    p = bank(pe, ("YT", h, lv))
                    for c in range(NC_):
                        ins = T.matmul(p[0:CH, c * CH:(c + 1) * CH], Xb[:, c, :], Ub[:, c, :], start=True, stop=True)
                    ins.then_inc(full[WHERE[("YT", h, lv)][0]], 1)
                    pe.wait_ge(full[WHERE[("YT", h, lv)][0]], WHERE[("YT", h, lv)][1] + 1)
                    pe.sem_inc(S("ly"), 1)
                if kind == "solve":
                    h = step[1]
                    pe.wait_ge(S("TU"), NL * (h + 1))
                    pe.wait_ge(S("kv"), h + 1)
                    p = bank(pe, ("u", h))
                    for c in range(NC_):
                        ins = T.matmul(p[0:CH, c * P:(c + 1) * P], Ub[:, c, :], Vb[:, h % 2, c, :], start=True, stop=True)
                    ins.then_inc(full[WHERE[("u", h)][0]], 1)
                    p = bank(pe, ("wT", h))
                    for c in range(NC_):
                        ins = T.matmul(p[:, c * CH:(c + 1) * CH], Kb[:, h % 2, c, :], Ub[:, c, :], start=True, stop=True)
                    ins.then_inc(full[WHERE[("wT", h)][0]], 1)
                    pe.wait_ge(full[WHERE[("wT", h)][0]], WHERE[("wT", h)][1] + 1)
                    pe.sem_inc(S("solved"), 1)
                if kind in ("s0", "sb"):
                    h = step[1]
                    c = 0 if kind == "s0" else step[2]
                    if c == 0:
                        pe.wait_ge(S("u"), h + 1)
                        new = ub[:, h % 2, 0, :]
                    else:
                        pe.wait_ge(S("vn"), 2 * h + c)
                        new = vn[:, c - 1, :]
                    key = ("os",) + tuple(step[1:])
                    p = bank(pe, key)
                    ins = T.matmul(p[0:CH, 0:P], DT[:, h, c, :], new, start=True, stop=True)
                    if c < NC_ - 1:
                        ins = T.matmul(p[:, P:2 * P], Kd[:, h % 2, c, :], new, start=True, stop=True)
                    ins.then_inc(full[WHERE[key][0]], 1)
                    if c == NC_ - 1:
                        pe.wait_ge(full[WHERE[key][0]], WHERE[key][1] + 1)
                        pe.sem_inc(S("scan_done"), 1)
                if kind == "sa":
                    h, c = step[1:]
                    pe.wait_ge(S("S"), 2 * h + c)
                    pe.wait_ge(S("wT"), h + 1)
                    p = bank(pe, ("ws", h, c))
                    T.matmul(p[0:CH, 0:P], wT[:, h % 2, c, :], St[:, c - 1, :], start=True, stop=True).then_inc(full[WHERE[("ws", h, c)][0]], 1)
                    p = bank(pe, ("o1", h, c))
                    T.matmul(p[0:CH, 0:P], kqv[:, h % 3, 1, c * CH:(c + 1) * CH], St[:, c - 1, :], start=True, stop=True).then_inc(full[WHERE[("o1", h, c)][0]], 1)
                    pe.wait_ge(full[WHERE[("o1", h, c)][0]], WHERE[("o1", h, c)][1] + 1)
                    pe.sem_inc(S("sap"), 2)
                if kind == "out":
                    h = step[1]
                    pe.wait_ge(S("ors"), h + 1)
                    p = bank(pe, ("oT", h))
                    for c in range(NC_):
                        ins = T.transpose(p[:, c * CH:(c + 1) * CH], osb[:, c, :], ident[0:CH, 0:CH])
                    ins.then_inc(full[WHERE[("oT", h)][0]], 1)
                    pe.wait_ge(full[WHERE[("oT", h)][0]], WHERE[("oT", h)][1] + 1)
                    pe.sem_inc(S("oTp"), 1)
                if kind == "mix":
                    j = step[1]
                    g = j // 2
                    pe.wait_ge(S("pooled"), j + 1)
                    pe.wait_ge(S(f"poolw_land{g % 2}"), 16 * (g // 2 + 1))
                    for d in range(2):
                        p = bank(pe, (f"m{d}", j))
                        for a in range(2):
                            ins = T.matmul(p[:, 0:SEQ], poolw[:, g % 2, a, d * P:(d + 1) * P], pooled[:, a, :], start=(a == 0), stop=(a == 1))
                        ins.then_inc(full[WHERE[(f"m{d}", j)][0]], 1)
                        pe.wait_ge(full[WHERE[(f"m{d}", j)][0]], WHERE[(f"m{d}", j)][1] + 1)
                        pe.sem_inc(S("mix"), 1)

            for b in range(8):
                if USES[b]:
                    pe.wait_ge(free[b], USES[b])
            for k in range(KT):
                n = len(TILES) + k
                pe.wait_ge(S("mixed"), k + 1)
                pe.wait_ge(win_land[n % WIN_SLOTS], 16 * (n // WIN_SLOTS + 1))
                for i in range(TT):
                    for half in range(2):
                        ins = T.matmul(pb[2 * i + half][:], merged[:, k, i * P:(i + 1) * P],
                                       wout[:, n % WIN_SLOTS, half * 512:(half + 1) * 512], start=(k == 0), stop=(k == KT - 1))
            ins.then_inc(S("outproj"), 1)
            pe.wait_ge(S("res"), 4)
            for k in range(KT):
                if k >= 4:
                    pe.wait_ge(S("uT" if k % 2 else "uTd"), KT // 2 + (k - 4) // 2 + 1)
                for i in range(TT):
                    pe.wait_ge(S("xn"), i + 1)
                    ins = T.transpose(pb[k % 4][:, i * P:(i + 1) * P], xn[:, i, k * P:(k + 1) * P], ident[:])
                ins.then_inc(S("turned"), 1)
            pe.wait_ge(S("rout_land"), 64)
            for i in range(TT):
                for k in range(KT):
                    pe.wait_ge(S("uT" if k % 2 else "uTd"), KT // 2 + k // 2 + 1)
                    ins = T.matmul(pb[4 + i][:, 0:36], x2T[:, k, i * P:(i + 1) * P], routw[:, k, :], start=(k == 0), stop=(k == KT - 1))
                ins.then_inc(S("logits"), 1)
            pe.wait_ge(S("picked"), 1)
            T.matmul(pb[6][:, 0:32], before[:], rt[:, 0, 8, :], start=True, stop=True).then_inc(S("pos"), 1)
            pe.wait_ge(S("picked"), 2)
            T.matmul(pb[6][:, 32:64], ones[:], rt[:, 0, 8, :], start=True, stop=False)
            T.matmul(pb[6][:, 32:64], before[:], rt[:, 1, 8, :], start=False, stop=True).then_inc(S("pos"), 1)
            T.matmul(pb[6][:, 64:96], ones[:], rt[:, 0, 8, :], start=True, stop=False)
            T.matmul(pb[6][:, 64:96], ones[:], rt[:, 1, 8, :], start=False, stop=True).then_inc(S("pos"), 1)

            def one_pass(ps):
                base = EXPERTS * ps
                for k in range(2):
                    for i in range(TT):
                        pe.wait_ge(S("hot"), 4 * ps + 2 * i + k + 1)
                        ins = T.matmul(pb[7][:, 32 * k:32 * k + 32], hot[:, 2 * i + k, :], rt[:, i, 6 + k, :], start=(i == 0), stop=(i == TT - 1))
                ins.then_inc(S("listp"), 1)

                def turn(n, k, landed, first):
                    pe.wait_ge(S(f"xg_land{k}"), landed)
                    if not first:
                        pe.wait_ge(S("xgT"), n)
                    for b in range(4):
                        ins = T.transpose(pb[0][:, b * P:(b + 1) * P], xg[:, k, b * P:(b + 1) * P], ident[:])
                    ins.then_inc(S("xT"), 1)

                def gate_up(n, k, landed, first):
                    pe.wait_ge(S("xgT"), n + 1)
                    for c, name in ((0, "gate"), (1, "up")):
                        pe.wait_ge(S(f"w_land{3 * k + c}"), landed)
                        if not first:
                            pe.wait_ge(S("hmid"), n)
                        w = ring[:, 3 * k + c, :].rearrange("p (k f) -> p k f", k=KT)
                        for kt in range(KT):
                            b = 2 * (kt % 4) + kt // 4
                            lhs = xgT[:, 0, b * SLOTS:(b + 1) * SLOTS]
                            for g in range(2):
                                ins = T.matmul(pb[1 + c][g * 64:g * 64 + SLOTS, 0:256], lhs, w[:, kt, g * 256:(g + 1) * 256],
                                               start=(kt == 0), stop=(kt == KT - 1), skip_group_check=True)
                        ins.then_inc(S(name), 1)

                def down(n, k, landed, first):
                    pe.wait_ge(S("hmid"), n + 1)
                    if not first:
                        pe.wait_ge(S("hT"), n)
                    for b in range(2):
                        ins = T.transpose(pb[3][:, b * P:(b + 1) * P], hmid[:, 0, b * P:(b + 1) * P], ident[:])
                    ins.then_inc(S("hTp"), 1)
                    pe.wait_ge(S("hT"), n + 1)
                    pe.wait_ge(S(f"w_land{3 * k + 2}"), landed)
                    if not first:
                        pe.wait_ge(S("yout"), n)
                    w = ring[:, 3 * k + 2, :].rearrange("p (k d) -> p k d", k=4)
                    for f in range(4):
                        g, b = f // 2, f % 2
                        for half in range(2):
                            ins = T.matmul(pb[4][half * 64:half * 64 + SLOTS, :], hT[:, 0, b, g * 64:g * 64 + SLOTS],
                                           w[:, f, half * 512:(half + 1) * 512], start=(f == 0), stop=(f == 3), skip_group_check=True)
                    ins.then_inc(S("y"), 1)

                wused = [ps * uses(EXPERTS, k, 3) for k in range(3)]
                xused = [ps * uses(EXPERTS, k, ROWS_BUF) for k in range(ROWS_BUF)]

                def step(e, i, j, first, last):
                    n = e + base
                    k = j % 3
                    landed = i * (16 * (ROWS_BUF // 3)) + 16 * (wused[k] + j // 3 + 1)
                    gate_up(n, k, landed, first)
                    if not last:
                        k2 = (j + 1) % ROWS_BUF
                        turn(e + (base + 1), k2, i * 16 + 16 * (xused[k2] + 1 + (j + 1) // ROWS_BUF), False)
                    down(n, k, landed, first)

                turn(base, 0, 16 * (xused[0] + 1), ps == 0)
                for e in range(ROWS_BUF):
                    step(e, 0, e, ps == 0 and e == 0, False)
                with pe.Fori(1, EXPERTS // ROWS_BUF) as i:
                    for j in range(ROWS_BUF):
                        step(i * ROWS_BUF + j, i, j, False, False)
                for e in range(EXPERTS // ROWS_BUF * ROWS_BUF, EXPERTS):
                    step(e, e // ROWS_BUF, e % ROWS_BUF, False, e == EXPERTS - 1)

            one_pass(0)
            overflow(pe, one_pass)
            pe.sem_inc(S("pe_done"), 1)

_INS = ["x", "meta_tokens", "norm_mix_w", "w_in", "conv_w", "pool_w", "pool_scale", "a_log", "dt_bias", "dn_norm_w",
        "w_out", "norm_ffn_w", "router_group_w", "router_group_b", "router_expert_w", "router_expert_b",
        "expert_w_gate", "expert_w_up", "expert_w_down", "norm_final_w"]
_OUTS = [((1, SEQ, D), "float32")]


def kernel(**inputs):
    import numpy as _np
    import concourse.bacc as _bacc
    from concourse import mybir as _mybir
    from concourse.bass_utils import run_bass_kernel_spmd as _run

    nc = _bacc.Bacc("TRN2", target_bir_lowering=False, num_devices=1)
    arrays, args = {}, []
    for name in _INS:
        a = _np.ascontiguousarray(inputs[name])
        arrays[f"in_{name}_dram"] = a
        args.append(nc.dram_tensor(f"in_{name}_dram", a.shape, _mybir.dt.from_np(a.dtype), kind="ExternalInput").ap())
    for i, (shape, dtype) in enumerate(_OUTS):
        dt = _mybir.dt.from_np(_np.dtype(dtype))
        args.append(nc.dram_tensor(f"out_{i}_dram", shape, dt, kind="ExternalOutput").ap())
    build_block(nc, *args)
    r = _run(nc, [arrays], core_ids=[0])
    got = tuple(r.results[0][f"out_{i}_dram"] for i in range(len(_OUTS)))
    return got[0]
```

```python
from contextlib import ExitStack

import numpy as np
import concourse.bass as bass
from concourse import mybir

F32 = mybir.dt.float32
I32 = mybir.dt.int32
U32 = mybir.dt.uint32
ALU = mybir.AluOpType
ACT = mybir.ActivationFunctionType
AX = mybir.AxisListType

P = 128
D = 1024
KT = D // P
META = 16
SEQ = 256
TT = SEQ // P
L = META + SEQ
HEADS = 8
CH = 96
PAD = 16
LP = PAD + L
NC_ = LP // CH
REAL = PAD + META
TAPS = 4
LEVELS = [2, 4, 8, 16, 32, 64]
NL = len(LEVELS)
GROUPS = 4
PER_GROUP = 8
EXPERTS = GROUPS * PER_GROUP
FF = 512
EPS = 1e-6
NEG = -1e30
COL = {"P": 0, "q": 1024, "k": 2048, "v": 3072, "z": 4096, "gA": 5136, "gB": 6160}
COL_AB = 5120
WIN_SLOTS = 6
CHUNK = 4096
SLOTS = 64
SPLIT = 3
PASSES = -(-SEQ // SLOTS)
DESK = 6192
CONSTS = {n: i + 1 for i, n in enumerate(["ident", "ones", "eps", "abz", "masks", "mups", "kqv_zero"])}
LEAD = 5
ROWS_BUF = 6
KQV = 4
BIG = float(1 << 20)
ROW_CONV, ROW_MIX, ROW_FFN, ROW_POOL, ROW_DN, ROWS = 0, 96, 104, 112, 120, 121


def plan_rounds():
    order = []
    tile = 0
    for r in range(HEADS + 3):
        kinds = [(t, r) for t in "kqv"] if r < HEADS else []
        j = r - 3
        if j >= 0:
            kinds = [("z", j), ("gB", j)] + kinds
            kinds += [("P", j), ("P", j + 1)] if j % 2 == 0 else [("gA", j - 1), ("gA", j)]
        fill = []
        for t, j2 in kinds:
            fill += [("proj", tile, t, j2, k) for k in range(KT)]
            fill += [("take", tile, t, j2)]
            if t == "v":
                fill += [("silu", x, j2) for x in "kqv"]
            tile += 1
        lists = [fill]
        if 0 <= r - 1 < HEADS:
            h = r - 1
            lists.append([("norm", h), ("gram", h), ("turn", h)] + [(s, h, lv) for lv in range(SPLIT) for s in ("lx", "ly")])
        if 0 <= r - 2 < HEADS:
            h = r - 2
            lists.append([(s, h, lv) for lv in range(SPLIT, NL) for s in ("lx", "ly")] + [("solve", h)])
        if 0 <= r - 3 < HEADS:
            h = r - 3
            lists.append([("s0", h), ("sa", h, 1), ("sb", h, 1), ("sa", h, 2), ("sb", h, 2), ("onorm", h), ("out", h)])
        at = [((i + 1) / len(lst), n, i) for n, lst in enumerate(lists) for i in range(len(lst))]
        order += [lists[n][i] for _, n, i in sorted(at)]
        if j >= 0 and j % 2 == 1:
            order += [("mix", j)]
    return order


ORDER = plan_rounds()
PSUM_OF = {
    "norm": ["nk", "nq"], "gram": ["G", "QK", "KT", "VT"], "turn": ["AT"], "lx": ["X"], "ly": ["Y", "YT"],
    "solve": ["u", "wT"], "s0": ["os"], "sa": ["ws", "o1"], "sb": ["os"], "out": ["oT"], "mix": ["m0", "m1"],
}


def plan_banks():
    where, n = {}, 0
    for step in ORDER:
        if step[0] == "take":
            where[("proj", step[1])] = (step[1] % 2, step[1] // 2)
        for name in PSUM_OF.get(step[0], []):
            if name == "Y" and step[2] == NL - 1:
                continue
            key = (name,) + tuple(step[1:]) + ((0,) if step[0] == "s0" else ())
            where[key] = (2 + n % 6, n // 6)
            n += 1
    uses = [0] * 8
    for b, u in where.values():
        uses[b] = max(uses[b], u + 1)
    return where, uses


WHERE, USES = plan_banks()
TILES = [(s[2], s[3]) for s in ORDER if s[0] == "take"]
OT_ORDER = []
for _s in ORDER:
    if _s[0] == "turn":
        OT_ORDER += [(_s[1], 0), (_s[1], 1)]
    if _s[0] == "ly" and _s[2] + 2 < NL:
        OT_ORDER.append((_s[1], _s[2] + 2))
OT_AT = {k: n + 1 for n, k in enumerate(OT_ORDER)}
TILE_OF = {t: n for n, t in enumerate(TILES)}


def uses(n, k, slots):
    return (n - k + slots - 1) // slots


def build_block(nc, x, meta_tokens, norm_mix_w, w_in, conv_w, pool_w, pool_scale, a_log, dt_bias, dn_norm_w,
                w_out, norm_ffn_w, router_group_w, router_group_b, router_expert_w, router_expert_b,
                expert_w_gate, expert_w_up, expert_w_down, norm_final_w, out):
    ctx = ExitStack()
    with ctx:
        def sb(name, shape, dt=F32):
            return ctx.enter_context(nc.sbuf_tensor(name, shape, dt))

        def sem(name):
            return ctx.enter_context(nc.semaphore(name))

        class Named:
            def __init__(self):
                self.made = {}

            def __call__(self, name):
                if name not in self.made:
                    self.made[name] = sem("s_" + name)
                return self.made[name]

        S = Named()

        ring = sb("ring", [P, 9, CHUNK])
        room = ring[:, 3:9, :].rearrange("p a b -> p (a b)")
        at = [0]

        def take(n, rows=P):
            at[0] += n
            assert at[0] <= 6 * CHUNK, at[0]
            return room[0:rows, at[0] - n:at[0]]

        win = take(WIN_SLOTS * D).rearrange("p (s k c) -> p s k c", s=WIN_SLOTS, k=KT)
        wout = win.rearrange("p s k c -> p s (k c)")
        uT = take(KT * L).rearrange("p (k t) -> p k t", k=KT)
        kqv = take(KQV * 3 * LP).rearrange("p (b i t) -> p b i t", b=KQV, i=3)
        decay_at = at[0]
        Dm = take(HEADS * LP, CH).rearrange("p (h c t) -> p h c t", h=HEADS, c=NC_)
        DT = take(HEADS * LP, CH).rearrange("p (h c t) -> p h c t", h=HEADS, c=NC_)
        hn = room[:, decay_at:decay_at + 3 * D].rearrange("p (i d) -> p i d", i=3)
        sq = take(2 * LP).rearrange("p (i t) -> p i t", i=2)
        rn = take(2 * LP).rearrange("p (i t) -> p i t", i=2)

        def chunks(n, rows=CH):
            return take(n * NC_, rows).rearrange("p (c t) -> p c t", c=NC_)

        def two_chunks():
            return take(2 * LP, CH).rearrange("p (b c t) -> p b c t", b=2, c=NC_)

        Ab = chunks(CH)
        ATb = two_chunks()
        Tb = two_chunks()
        Ub = two_chunks()
        Xb = two_chunks()

        OTb = take(4 * LP, CH).rearrange("p (b l c t) -> p b l c t", b=2, l=2, c=NC_)
        tmpT = take(2 * LP, CH).rearrange("p (b c t) -> p b c t", b=2, c=NC_)
        late = sb("late", [P, TT * D])
        xn = late[:].rearrange("p (i d) -> p i d", i=TT)
        Kb = late[0:CH, 0:2 * NC_ * P].rearrange("p (b c t) -> p b c t", b=2, c=NC_)
        Kd = late[0:CH, 2 * NC_ * P:5 * NC_ * P].rearrange("p (b c t) -> p b c t", b=3, c=NC_)
        ub = take(2 * NC_ * P, CH).rearrange("p (b c t) -> p b c t", b=2, c=NC_)
        desk = sb("desk", [P, DESK])
        desk_at = [0]

        def lay(shape, rows=P):
            n = int(np.prod(shape))
            desk_at[0] += n
            assert desk_at[0] <= DESK, desk_at[0]
            v = desk[0:rows, desk_at[0] - n:desk_at[0]]
            names = "abcd"[:len(shape)]
            return v if len(shape) == 1 else v.rearrange(f"p ({' '.join(names)}) -> p {' '.join(names)}", **dict(zip(names[1:], shape[1:])))

        Vb = lay([2, NC_, P], CH)
        wT = lay([2, NC_, CH])
        vn = lay([2, P], CH)
        St = lay([2, P])
        osb = lay([NC_, P], CH)
        o1s = lay([2, P], CH)
        acc = lay([3, L])
        zs = lay([2, SEQ])
        thB = lay([SEQ])
        thA = lay([2, SEQ])
        pt = lay([2, L])
        ps2 = lay([2, L])
        pooled = lay([2, SEQ])
        poolw = sb("poolw", [P, 2, 2, 2 * P])
        merged = sb("merged", [P, KT, SEQ])
        hres = sb("hres", [P, TT, D])
        ident = sb("ident", [P, P])
        ones = sb("ones", [P, P])
        eps = sb("eps", [P, 1])
        prm = sb("prm", [P, P])
        prmT = sb("prmT", [P, ROWS])
        halfs = sb("halfs", [P, ROWS - ROW_POOL])
        mlow = take(CH, CH)
        mup = take((1 + NL) * CH, CH).rearrange("p (l t) -> p l t", l=1 + NL)
        uincl = sb("uincl", [CH, CH])
        negs = take(2 * CH, CH).rearrange("p (l t) -> p l t", l=2)
        small = sb("small", [P, 40, 24])
        wab = sb("wab", [P, KT, 16])
        abT = sb("abT", [16, LP])
        bc8 = sb("bc8", [CH, 3, 8])

        def plane(i, rows=CH, n=24):
            return small[0:rows, i, 0:n]

        def plane3(i, rows=CH):
            return small[0:rows, i, 0:24].rearrange("p (c h) -> p c h", c=NC_)

        X_, AX_, E_, LN_, RL_, SP_, G_, EB_, BETA_, NBETA_, GAM_, EGAM_, CD_, KD_, GL_, SKB_ = range(16)
        MS_, RS_, OSS_, ORS_ = 16, 17, 18, 20

        pb = [ctx.enter_context(nc.psum_tensor(f"bank{i}", [P, 512], F32)) for i in range(8)]
        full = [sem(f"bank_full{i}") for i in range(8)]
        free = [sem(f"bank_free{i}") for i in range(8)]
        win_land = [sem(f"win_land{i}") for i in range(WIN_SLOTS)]

        xn_dram = nc.dram_tensor("xn_rows", [2 * SEQ, D // 2], F32, kind="Internal").ap()
        y_dram = nc.dram_tensor("y_rows", [4 * SEQ, D // 2], F32, kind="Internal").ap()

        desk_at[0] = 0
        xg = lay([ROWS_BUF, FF])
        xgT = lay([1, KT * SLOTS])
        sgate = lay([1, FF // 2])
        hmid = lay([1, FF // 2])
        hT = lay([1, 2, P])
        yout = [late[:, i * FF:(i + 1) * FF] for i in range(4)]
        yout += [merged[:].rearrange("p k t -> p (k t)")[:, (2 + i) * FF:(3 + i) * FF] for i in range(2)]
        rt = lay([TT, 18, 32])
        hot = merged[:, 0:2, :].rearrange("p k (a t) -> p (k a) t", a=2)
        wff = lay([KT, SLOTS])
        x2T = merged
        routw = poolw[:].rearrange("p a b c -> p (a b c)")[:, 0:KT * 36].rearrange("p (k n) -> p k n", k=KT)
        rbias = sb("rbias", [P, 36])
        rs = sb("rs", [P, TT, 24])
        ru = sb("ru", [P, TT, 16], U32)
        iota_e = sb("iota_e", [P, EXPERTS])
        iota_g = sb("iota_g", [P, EXPERTS])
        iota_c = sb("iota_c", [P, P])
        iota_t = sb("iota_t", [P, TT])
        halfof = sb("halfof", [P, 1])
        before = sb("before", [P, P])
        lists = sb("lists", [P, 3, EXPERTS])
        gidx = sb("gidx", [P, EXPERTS], I32)
        sidx = sb("sidx", [P, EXPERTS], I32)
        gcol = sb("gcol", [P, ROWS_BUF], I32)
        scol = sb("scol", [P, ROWS_BUF], I32)
        most = sb("most", [P, 8])
        mosti = sb("mosti", [P, 1], I32)

        w_in_v = w_in[0].rearrange("(k p) n -> p k n", p=P)
        gate_v = expert_w_gate[0].rearrange("g e (k p) f -> (g e) p k f", p=P)
        up_v = expert_w_up[0].rearrange("g e (k p) f -> (g e) p k f", p=P)
        down_v = expert_w_down[0].rearrange("g e (k p) d -> (g e) p k d", p=P)

        def filled(eng, key):
            b, n = WHERE[key]
            eng.wait_ge(full[b], n + 1)
            return pb[b]

        def taken(eng, key):
            b, n = WHERE[key]
            eng.wait_ge(free[b], n + 1)

        def fills(ins, key):
            ins.then_inc(full[WHERE[key][0]], 1)

        def takes(ins, key):
            ins.then_inc(free[WHERE[key][0]], 1)

        def bank(pe, key):
            b, n = WHERE[key]
            if n >= 1:
                pe.wait_ge(free[b], n)
            return pb[b]

        LIST = {"k": 0, "q": 1, "v": 2}

        def overflow(eng, one_pass):
            eng.wait_ge(S("most"), 1)
            count = eng.value_load(mosti[0:1, 0:1], min_val=0, max_val=SEQ)
            opened = []
            for ps in range(1, PASSES):
                c = eng.If(count > ps * SLOTS)
                c.__enter__()
                opened.append(c)
                one_pass(ps)
            for c in reversed(opened):
                c.__exit__(None, None, None)

        block = ctx.enter_context(nc.Block())

        @block.sync
        def _(sp):
            sp.dma_start(prm[ROW_CONV:ROW_CONV + 96, :], conv_w[0].rearrange("j (c p) -> (j c) p", p=P)).then_inc(S("params_land"), 16)
            for row, a in ((ROW_MIX, norm_mix_w), (ROW_FFN, norm_ffn_w), (ROW_POOL, pool_scale), (ROW_DN, dn_norm_w)):
                n = a.shape[1] // P
                sp.dma_start(prm[row:row + n, :], a[0].rearrange("(c p) -> c p", p=P)).then_inc(S("params_land"), 16)
            sp.dma_start(wab[:, :, :], w_in_v[:, :, COL_AB:COL_AB + 16]).then_inc(S("params_land"), 16)
            for i, a in ((0, a_log), (1, dt_bias)):
                sp.dma_start(bc8[:, i, :], a[0:1, :].partition_broadcast(CH) if False else a[0:1, :].to_broadcast([CH, 8])).then_inc(S("params_land"), 16)

            def load_tile(n):
                t, j = TILES[n]
                if n >= WIN_SLOTS:
                    filled(sp, ("proj", n - WIN_SLOTS))
                c = COL[t] + j * P
                sp.dma_start(win[:, n % WIN_SLOTS], w_in_v[:, :, c:c + P]).then_inc(win_land[n % WIN_SLOTS], 16)
                if t == "P" and j % 2 == 0:
                    g = j // 2
                    if g >= 2:
                        filled(sp, ("m1", 2 * g - 3))
                    sp.dma_start(poolw[:, g % 2], pool_w[0, g].rearrange("(a p) c -> p a c", p=P)).then_inc(S(f"poolw_land{g % 2}"), 16)

            for n in range(WIN_SLOTS):
                load_tile(n)
            for c in range(3):
                sp.dma_start(ring[:, c, :].rearrange("p (k f) -> p k f", k=KT if c < 2 else 4),
                             (gate_v, up_v, down_v)[c][0]).then_inc(S(f"w_land{c}"), 16)
            for n in range(WIN_SLOTS, len(TILES)):
                load_tile(n)
            for k in range(KT):
                n = len(TILES) + k
                if k < WIN_SLOTS:
                    filled(sp, ("proj", n - WIN_SLOTS))
                else:
                    sp.wait_ge(S("wout_used"), k - WIN_SLOTS + 1)
                sp.dma_start(wout[:, n % WIN_SLOTS, :], w_out[0, k * P:(k + 1) * P, :]).then_inc(win_land[n % WIN_SLOTS], 16)
            filled(sp, ("m1", HEADS - 1))
            sp.dma_start(routw[:, :, 0:GROUPS], router_group_w[0].rearrange("(k p) n -> p k n", p=P)).then_inc(S("rout_land"), 16)
            sp.dma_start(routw[:, :, GROUPS:36], router_expert_w[0].rearrange("(k p) n -> p k n", p=P)).then_inc(S("rout_land"), 16)
            sp.dma_start(rbias[:, 0:GROUPS], router_group_b[0:1, :].to_broadcast([P, GROUPS])).then_inc(S("rout_land"), 16)
            sp.dma_start(rbias[:, GROUPS:36], router_expert_b[0:1, :].to_broadcast([P, EXPERTS])).then_inc(S("rout_land"), 16)
            sp.wait_ge(S("outproj"), 1)

            def load_expert(e, slot):
                for c in range(3):
                    sp.dma_start(ring[:, 3 * slot + c, :].rearrange("p (k f) -> p k f", k=KT if c < 2 else 4),
                                 (gate_v, up_v, down_v)[c][bass.ds(e, 1)].rearrange("a p k f -> (a p) k f") if not isinstance(e, int)
                                 else (gate_v, up_v, down_v)[c][e]).then_inc(S(f"w_land{3 * slot + c}"), 16)

            def one_pass(ps):
                base = EXPERTS * ps
                for e in range(3):
                    if ps == 0 and e == 0:
                        continue
                    if ps >= 1:
                        sp.wait_ge(S("y"), base)
                    load_expert(e, e)
                with sp.Fori(1, EXPERTS // 3) as i:
                    for j in range(3):
                        sp.wait_ge(S("y"), i * 3 + (base + j - 2))
                        load_expert(i * 3 + j, j)
                for e in range(EXPERTS // 3 * 3, EXPERTS):
                    sp.wait_ge(S("y"), base + e - 2)
                    load_expert(e, e % 3)

            one_pass(0)
            overflow(sp, one_pass)
            sp.wait_ge(S("pe_done"), 1)
            sp.wait_ge(S("y_all"), 1)
            sp.dma_start(ring[:, 5, 0:D], norm_final_w[None, :].to_broadcast([P, D])).then_inc(S("wf_land"), 16)
            for i in range(TT):
                for k in range(2):
                    sp.dma_start(ring[:, 2 * i + k, 0:D],
                                 y_dram.rearrange("(t b) d -> t (b d)", b=2)[k * SEQ + i * P:k * SEQ + (i + 1) * P, :]).then_inc(S(f"y_back{i}"), 16)
            for i in range(TT):
                sp.wait_ge(S("final"), i + 1)
                sp.dma_start(out[0, i * P:(i + 1) * P, :], ring[:, 7 + i, 0:D]).then_inc(S("stored"), 16)
            sp.wait_ge(S("stored"), TT * 16)

        @block.scalar
        def _(act):
            for i in range(TT):
                act.dma_start(hres[:, i, :], x[0, i * P:(i + 1) * P, :]).then_inc(S(f"x_land{i}"), 16)
            act.dma_start(hn[0:META, 2, :], meta_tokens).then_inc(S("meta_land"), 16)
            act.wait_ge(S("meta_land"), 16)
            junk = merged[:].rearrange("p k t -> p (k t)")[:, 0:D]
            for i in range(3):
                rows = META if i == 2 else P
                if i < 2:
                    act.wait_ge(S(f"x_land{i}"), 16)
                if i:
                    act.wait_ge(S("ms"), i)
                nc.scalar.activation(junk[0:rows], hn[0:META, 2, :] if i == 2 else hres[:, i, :], ACT.Square,
                                     scale=1.0 / 32.0, accum_out=small[0:rows, MS_, i:i + 1]).then_inc(S("ms"), 1)
            act.wait_ge(S("ms"), 3)
            act.wait_ge(S("consts"), CONSTS["eps"])
            nc.scalar.activation(small[:, MS_, 4:6], small[:, MS_, 0:2], ACT.Sqrt, bias=eps[:]).then_inc(S("rms"), 1)
            nc.scalar.activation(small[0:META, MS_, 6:7], small[0:META, MS_, 2:3], ACT.Sqrt, bias=eps[0:META]).then_inc(S("rms"), 1)
            act.wait_ge(S("prmT"), 1)
            for k in range(1, KT, 2):
                act.wait_ge(S("turned"), k + 1)
                nc.scalar.activation(uT[:, k, :], pb[k % 4][:, 0:L], ACT.Copy, scale=prmT[:, ROW_MIX + k:ROW_MIX + k + 1]).then_inc(S("uT"), 1)
            act.wait_ge(S("ab"), 1)
            act.wait_ge(S("consts"), CONSTS["abz"])
            nc.scalar.activation(abT[:, PAD:LP], pb[4][0:16, 0:L], ACT.Copy).then_inc(S("abT"), 1)
            act.wait_ge(S("xa"), 1)
            nc.scalar.activation(plane(AX_), plane(X_), ACT.Abs).then_inc(S("a_chain"), 1)
            act.wait_ge(S("a_chain"), 1)
            nc.scalar.activation(plane(E_), plane(AX_), ACT.Exp, scale=-1.0).then_inc(S("a_chain"), 1)
            act.wait_ge(S("a_chain"), 2)
            nc.scalar.activation(plane(LN_), plane(E_), ACT.Ln, bias=1.0).then_inc(S("lnp"), 1)
            nc.scalar.activation(plane3(EB_), pb[5][0:CH, 0:48].rearrange("p (c n) -> p c n", c=3)[:, :, 8:16], ACT.Exp, scale=-1.0).then_inc(S("eb"), 1)
            act.wait_ge(S("params_land"), 8 * 16)
            nc.scalar.activation(bc8[:, 2, :], bc8[:, 0, :], ACT.Exp).then_inc(S("ea"), 1)
            act.wait_ge(S("kdarg"), 1)
            nc.scalar.activation(plane(EGAM_), plane(GAM_), ACT.Exp).then_inc(S("egam"), 1)
            nc.scalar.activation(plane(CD_, P), pb[6][:, 32:56], ACT.Exp).then_inc(S("egam"), 1)
            nc.scalar.activation(plane(KD_), plane(GL_), ACT.Exp).then_inc(S("egam"), 1)
            for h in range(HEADS):
                act.wait_ge(S("darg"), 2 * h + 1)
                nc.scalar.activation(Dm[:, h], Dm[:, h], ACT.Exp).then_inc(S("Dexp"), 1)
                act.wait_ge(S("darg"), 2 * h + 2)
                nc.scalar.activation(DT[:, h], DT[:, h], ACT.Exp).then_inc(S("DTexp"), 1)

            def take_tile(n, t, j):
                p = filled(act, ("proj", n))
                if t in "kqv":
                    i = LIST[t]
                    col = {"q": 0, "k": 8, "v": 16}[t] + j
                    w3 = prmT[:, 3 * 24 + col:3 * 24 + col + 1]
                    if j >= 1:
                        act.wait_ge(S("silu"), 3 * j)
                    nc.scalar.activation(acc[:, i, :], p[:, 0:L], ACT.Copy, scale=w3).then_inc(S("tap3"), 1)
                elif t == "z":
                    if j >= 2:
                        taken(act, ("oT", j - 2))
                    takes(nc.scalar.activation(zs[:, j % 2, :], p[:, 0:SEQ], ACT.Silu), ("proj", n))
                elif t == "gB":
                    if j >= 1:
                        act.wait_ge(S("zg"), j)
                    takes(nc.scalar.activation(thB[:, :], p[:, 0:SEQ], ACT.Tanh, scale=0.5), ("proj", n))
                elif t == "gA":
                    if j >= 2:
                        act.wait_ge(S("mixed"), j // 2 * 2)
                    takes(nc.scalar.activation(thA[:, j % 2, :], p[:, 0:SEQ], ACT.Tanh, scale=0.5), ("proj", n))
                else:
                    if j >= 2:
                        act.wait_ge(S("pooled"), j // 2 * 2)
                    takes(nc.scalar.activation(pt[:, j % 2, :], p[:, 0:L], ACT.Copy), ("proj", n))

            def copy(dst, key, n, rows=CH, **kw):
                p = filled(act, key)
                takes(nc.scalar.activation(dst, p[0:rows, 0:NC_ * n].rearrange("p (c t) -> p c t", c=NC_), ACT.Copy, **kw), key)

            for step in ORDER:
                kind = step[0]
                if kind == "take":
                    take_tile(*step[1:])
                if kind == "silu":
                    t, h = step[1:]
                    i = LIST[t]
                    act.wait_ge(S("conv"), 3 * h + i + 1)
                    if h >= KQV:
                        filled(act, ("os", h - KQV, 2))
                    else:
                        act.wait_ge(S("consts"), CONSTS["kqv_zero"])
                    nc.scalar.activation(kqv[:, h % KQV, i, PAD:LP], acc[:, i, :], ACT.Silu).then_inc(S("silu"), 1)
                if kind == "norm":
                    h = step[1]
                    act.wait_ge(S("silu"), 3 * h + 2)
                    if h >= 1:
                        filled(act, ("nq", h - 1))
                    for i in range(2):
                        nc.scalar.activation(sq[:, i, :], kqv[:, h % KQV, i, :], ACT.Square).then_inc(S("sq"), 1)
                    if h >= 1:
                        act.wait_ge(S("kn"), 2 * h)
                    for i, name in enumerate(("nk", "nq")):
                        p = filled(act, (name, h))
                        takes(nc.scalar.activation(rn[:, i, :], p[:, 0:LP], ACT.Sqrt, bias=eps[:]), (name, h))
                if kind == "turn":
                    h = step[1]
                    if h >= 2:
                        act.wait_ge(S("OT"), OT_AT[(h - 2, NL - 1)])
                        act.wait_ge(S("base"), 2 * (h - 1))
                    copy(ATb[:, h % 2], ("AT", h), CH)
                if kind == "lx":
                    h, lv = step[1:]
                    if lv:
                        filled(act, ("YT", h, lv - 1))
                    elif h >= 2:
                        filled(act, ("YT", h - 2, NL - 1))
                    copy(Xb[:, h % 2], ("X", h, lv), CH)
                if kind == "solve":
                    h = step[1]
                    if h >= 2:
                        filled(act, ("os", h - 2, 2))
                        taken(act, ("ws", h - 2, 2))
                    copy(ub[:, h % 2], ("u", h), P)
                    copy(wT[:, h % 2], ("wT", h), CH, rows=P)
                if kind == "sa":
                    h, c = step[1:]
                    p = filled(act, ("o1", h, c))
                    if h >= 1:
                        taken(act, ("os", h - 1, c))
                    takes(nc.scalar.activation(o1s[:, c - 1, :], p[0:CH, 0:P], ACT.Copy,
                                               scale=small[0:CH, EGAM_, c * 8 + h:c * 8 + h + 1]), ("o1", h, c))
                if kind == "onorm":
                    h = step[1]
                    taken(act, ("os", h, 2))
                    for c in range(NC_):
                        if h or c:
                            act.wait_ge(S("oss"), 3 * h + c)
                        if h:
                            act.wait_ge(S("ors"), h)
                        nc.scalar.activation(o1s[:, 0, :], osb[:, c, :], ACT.Square, scale=float(P) ** -0.5,
                                             accum_out=small[0:CH, OSS_, c:c + 1]).then_inc(S("oss"), 1)
                    act.wait_ge(S("oss"), 3 * h + 3)
                    nc.scalar.activation(small[0:CH, ORS_, 4:7], small[0:CH, OSS_, 0:3], ACT.Sqrt, bias=eps[0:CH]).then_inc(S("orms"), 1)

            junk2 = late[:, 0:D]
            for i in range(TT):
                act.wait_ge(S("res"), 2 * (i + 1))
                if i:
                    act.wait_ge(S("ms"), 3 + i)
                nc.scalar.activation(junk2, hres[:, i, :], ACT.Square, scale=1.0 / 32.0,
                                     accum_out=rs[:, i, 0:1]).then_inc(S("ms"), 1)
            for i in range(TT):
                act.wait_ge(S("ms"), 3 + TT)
                nc.scalar.activation(rs[:, i, 22:23], rs[:, i, 0:1], ACT.Sqrt, bias=eps[:]).then_inc(S("rms"), 1)
            for k in range(1, KT, 2):
                act.wait_ge(S("turned"), KT + k + 1)
                nc.scalar.activation(x2T[:, k, :], pb[k % 4][:, 0:SEQ], ACT.Copy, scale=prmT[:, ROW_FFN + k:ROW_FFN + k + 1]).then_inc(S("uT"), 1)
            for i in range(TT):
                act.wait_ge(S("rexp_in"), i + 1)
                nc.scalar.activation(rs[:, i, 8:12], rt[:, i, 0, 0:GROUPS], ACT.Exp, bias=rs[:, i, 2:3],
                                     accum_out=rs[:, i, 3:4]).then_inc(S("rexp"), 1)
                nc.scalar.activation(rs[:, i, 4:5], rs[:, i, 5:6], ACT.Exp).then_inc(S("rexp"), 1)

            def one_pass(ps):
                base = EXPERTS * ps

                def one(e, k, left, first):
                    n = e + base
                    act.wait_ge(S("gate"), n + 1)
                    if not first:
                        act.wait_ge(S("hmid"), n)
                    nc.scalar.activation(sgate[:, 0, :], pb[1][:, 0:FF // 2], ACT.Silu).then_inc(S("sgate"), 1)
                    act.wait_ge(S("y"), n + 1)
                    if left is not None:
                        act.wait_ge(S(f"y_left{k}"), left)
                    nc.scalar.activation(yout[k], pb[4][:], ACT.Copy).then_inc(S("yout"), 1)

                used = [ps * uses(EXPERTS, k, ROWS_BUF) for k in range(ROWS_BUF)]
                for e in range(ROWS_BUF):
                    one(e, e, 16 * used[e] if ps else None, ps == 0 and e == 0)
                with act.Fori(1, EXPERTS // ROWS_BUF) as i:
                    for j in range(ROWS_BUF):
                        one(i * ROWS_BUF + j, j, i * 16 + 16 * used[j], False)
                for e in range(EXPERTS // ROWS_BUF * ROWS_BUF, EXPERTS):
                    k = e % ROWS_BUF
                    one(e, k, 16 * (used[k] + e // ROWS_BUF), False)

            one_pass(0)
            overflow(act, one_pass)
            for i in range(TT):
                act.wait_ge(S("fin_h"), i + 1)
                if i:
                    act.wait_ge(S("ms"), 3 + TT + i)
                nc.scalar.activation(ring[:, 6, 0:D], hres[:, i, :], ACT.Square, scale=1.0 / 32.0,
                                     accum_out=rs[:, i, 12:13]).then_inc(S("ms"), 1)
            for i in range(TT):
                act.wait_ge(S("ms"), 3 + TT + i + 1)
                nc.scalar.activation(rs[:, i, 23:24], rs[:, i, 12:13], ACT.Sqrt, bias=eps[:]).then_inc(S("rms"), 1)

        @block.gpsimd
        def _(pool):
            done = [0]

            def chain(ins):
                done[0] += 1
                ins.then_inc(S("pool_chain"), 1)
                pool.wait_ge(S("pool_chain"), done[0])

            chain(nc.gpsimd.memset(ident[:], 0.0))
            chain(nc.gpsimd.affine_select(out=ident[:], in_=ident[:], compare_op=ALU.not_equal, fill=1.0, base=0,
                                          pattern=[[-1, P]], channel_multiplier=1))
            pool.sem_inc(S("consts"), 1)
            nc.gpsimd.memset(ones[:], 1.0).then_inc(S("consts"), 1)
            nc.gpsimd.memset(eps[:], EPS).then_inc(S("consts"), 1)
            nc.gpsimd.memset(abT[:, 0:PAD], 0.0).then_inc(S("consts"), 1)
            chain(nc.gpsimd.memset(uincl[:], 1.0))
            chain(nc.gpsimd.affine_select(out=uincl[:], in_=uincl[:], compare_op=ALU.is_ge, fill=0.0, base=0,
                                          pattern=[[1, CH]], channel_multiplier=-1))
            chain(nc.gpsimd.memset(negs[:], 0.0))
            chain(nc.gpsimd.affine_select(out=negs[:, 0, :], in_=negs[:, 0, :], compare_op=ALU.is_gt, fill=NEG, base=0,
                                          pattern=[[-1, CH]], channel_multiplier=1))
            chain(nc.gpsimd.affine_select(out=negs[:, 1, :], in_=negs[:, 1, :], compare_op=ALU.is_ge, fill=NEG, base=0,
                                          pattern=[[1, CH]], channel_multiplier=-1))
            pool.sem_inc(S("consts"), 1)
            chain(nc.gpsimd.memset(mlow[:], 0.0))
            v = mlow[:].rearrange("p (a r) -> p a r", r=2)[:, :, 0]
            chain(nc.gpsimd.affine_select(out=v, in_=v, compare_op=ALU.not_equal, fill=1.0, base=-1,
                                          pattern=[[-2, CH // 2]], channel_multiplier=1))
            chain(nc.gpsimd.memset(mup[:], 0.0))
            for lv, b in enumerate([1] + LEVELS):
                if 2 * b <= CH and CH % (2 * b) == 0:
                    v = mup[:, lv, :].rearrange("p (a r) -> p a r", r=2 * b)[:, :, b:2 * b]
                    na, nb = CH // (2 * b), b
                elif b == 32:
                    v, na, nb = mup[:, lv, 32:64].rearrange("p (a r) -> p a r", a=1), 1, 32
                else:
                    v, na, nb = mup[:, lv, b:CH].rearrange("p (a r) -> p a r", a=1), 1, CH - b
                chain(nc.gpsimd.memset(v, 1.0))
                chain(nc.gpsimd.affine_select(out=v, in_=v, compare_op=ALU.is_ge, fill=0.0, base=0,
                                              pattern=[[-2 * b, na], [0, nb]], channel_multiplier=1))
                chain(nc.gpsimd.affine_select(out=v, in_=v, compare_op=ALU.is_ge, fill=0.0, base=b - 1,
                                              pattern=[[2 * b, na], [0, nb]], channel_multiplier=-1))
            pool.sem_inc(S("consts"), 1)
            for b in range(KQV):
                nc.gpsimd.memset(kqv[:, b, :, 0:PAD], 0.0).then_inc(S("pool_chain"), 1)
                done[0] += 1
            pool.wait_ge(S("pool_chain"), done[0])
            pool.sem_inc(S("consts"), 1)
            for h in range(HEADS):
                pool.wait_ge(S("Dexp"), h + 1)
                pool.wait_ge(S("beta"), 1)
                nc.gpsimd.tensor_tensor(Dm[:, h], Dm[:, h],
                                        plane3(NBETA_)[:, :, h:h + 1].to_broadcast([CH, NC_, CH]), ALU.mult).then_inc(S("Dm"), 1)

            def mask_blocks(h, lv):
                nc.gpsimd.tensor_tensor(OTb[:, h % 2, lv % 2], ATb[:, h % 2], mup[:, 1 + lv:2 + lv, :].to_broadcast([CH, NC_, CH]), ALU.mult).then_inc(S("OT"), 1)

            pools = [0]

            def window(j):
                g = j // 2
                b = j % 2
                src = pt[:, b, :]
                taken(pool, ("proj", TILE_OF[("P", j)]))
                lo = 0
                a, n = src, 0
                for s in range(g + 1):
                    w = 1 << s
                    dst = ps2[:, s % 2, :]
                    lo += w
                    pools[0] += 1
                    nc.gpsimd.tensor_tensor(dst[:, lo:L], a[:, lo:L], a[:, lo - w:L - w], ALU.add).then_inc(S("win_chain"), 1)
                    pool.wait_ge(S("win_chain"), pools[0])
                    a = dst
                pools[0] += 1
                nc.gpsimd.tensor_scalar(ps2[:, (g + 1) % 2, META:L], a[:, META:L], 1.0 / (2 << g), None, ALU.mult).then_inc(S("win_chain"), 1)
                pool.wait_ge(S("win_chain"), pools[0])
                if j >= 2:
                    filled(pool, ("m1", j // 2 * 2 - 1))
                nc.gpsimd.tensor_tensor(pooled[:, b, :], ps2[:, (g + 1) % 2, META:L], src[:, META:L], ALU.subtract).then_inc(S("pooled"), 1)
                pool.wait_ge(S("pooled"), j + 1)

            for step in ORDER:
                if step[0] == "take" and step[2] == "P":
                    window(step[3])
                if step[0] == "turn":
                    h = step[1]
                    taken(pool, ("AT", h))
                    for lv in range(2):
                        if h >= 2:
                            filled(pool, ("X", h - 2, NL - 2 + lv))
                        mask_blocks(h, lv)
                if step[0] == "ly" and step[2] + 2 < NL:
                    h, lv = step[1:]
                    filled(pool, ("X", h, lv))
                    mask_blocks(h, lv + 2)

            chain(nc.gpsimd.iota(iota_e[:], pattern=[[1, EXPERTS]], base=0, channel_multiplier=0, allow_small_or_imprecise_dtypes=True))
            chain(nc.gpsimd.iota(iota_g[:], pattern=[[1, GROUPS], [0, PER_GROUP]], base=0, channel_multiplier=0, allow_small_or_imprecise_dtypes=True))
            chain(nc.gpsimd.iota(iota_c[:], pattern=[[0, P // SLOTS], [1, SLOTS]], base=0, channel_multiplier=0, allow_small_or_imprecise_dtypes=True))
            chain(nc.gpsimd.iota(iota_t[:], pattern=[[2 * P, TT]], base=-int(BIG), channel_multiplier=2, allow_small_or_imprecise_dtypes=True))
            chain(nc.gpsimd.memset(halfof[:], BIG + 1.0))
            chain(nc.gpsimd.affine_select(out=halfof[:], in_=halfof[:], compare_op=ALU.is_ge, fill=BIG, base=-SLOTS,
                                          pattern=[[0, 1]], channel_multiplier=1))
            chain(nc.gpsimd.memset(before[:], 1.0))
            chain(nc.gpsimd.affine_select(out=before[:], in_=before[:], compare_op=ALU.is_gt, fill=0.0, base=0,
                                          pattern=[[1, P]], channel_multiplier=-1))
            pool.wait_ge(S("outproj"), 1)
            chain(nc.gpsimd.memset(xg[:], 0.0))
            pool.sem_inc(S("rconst"), 1)
            for i in range(TT):
                pool.wait_ge(S("xn"), i + 1)
                nc.gpsimd.dma_start(xn_dram.rearrange("(t b) d -> t (b d)", b=2)[i * P:(i + 1) * P, :], xn[:, i, :]).then_inc(S("xn_out"), 16)

            def one_pass(ps):
                base = EXPERTS * ps
                pool.wait_ge(S("lists"), ps + 1)
                pool.wait_ge(S("xn_out"), 32)

                def gather(e, k, first):
                    n = e + base
                    if not first:
                        pool.wait_ge(S("xT"), n - (ROWS_BUF - 1))
                    nc.gpsimd.tensor_copy(gcol[:, k:k + 1], gidx[:, bass.ds(e, 1)]).then_inc(S("gcol"), 1)
                    pool.wait_ge(S("gcol"), n + 1)
                    pool.sem_inc(S("go"), 1)
                    nc.gpsimd.indirect_dma_start(out=xg[:, k, :], out_offset=None, in_=xn_dram,
                                                 in_offset=bass.IndirectOffsetOnAxis(ap=gcol[:, k:k + 1], axis=0),
                                                 bounds_check=2 * SEQ - 1, oob_is_err=False).then_inc(S(f"xg_land{k}"), 16)

                def scatter(e, k, left):
                    n = e + base
                    if left is not None:
                        pool.wait_ge(S(f"y_left{k}"), left)
                    nc.gpsimd.tensor_copy(scol[:, k:k + 1], sidx[:, bass.ds(e, 1)]).then_inc(S("scol"), 1)
                    pool.wait_ge(S("scol"), n + 1)
                    pool.wait_ge(S("yout"), n + 1)
                    pool.sem_inc(S("go"), 1)
                    nc.gpsimd.indirect_dma_start(out=y_dram, out_offset=bass.IndirectOffsetOnAxis(ap=scol[:, k:k + 1], axis=0),
                                                 in_=yout[k], in_offset=None,
                                                 bounds_check=4 * SEQ - 1, oob_is_err=False).then_inc(S(f"y_left{k}"), 16)

                used = [ps * uses(EXPERTS, k, ROWS_BUF) for k in range(ROWS_BUF)]
                for e in range(LEAD):
                    gather(e, e, ps == 0)
                for e in range(ROWS_BUF):
                    gather(e + LEAD, (e + LEAD) % ROWS_BUF, ps == 0 and e + LEAD < ROWS_BUF)
                    scatter(e, e, 16 * used[e] if ps else None)
                with pool.Fori(1, EXPERTS // ROWS_BUF - 1) as i:
                    for j in range(ROWS_BUF):
                        gather(i * ROWS_BUF + (j + LEAD), (j + LEAD) % ROWS_BUF, False)
                        scatter(i * ROWS_BUF + j, j, i * 16 + 16 * used[j])
                for e in range((EXPERTS // ROWS_BUF - 1) * ROWS_BUF, EXPERTS):
                    if e + LEAD < EXPERTS:
                        gather(e + LEAD, (e + LEAD) % ROWS_BUF, False)
                    k = e % ROWS_BUF
                    scatter(e, k, 16 * (used[k] + e // ROWS_BUF))
                for k in range(ROWS_BUF):
                    pool.wait_ge(S(f"y_left{k}"), 16 * (ps + 1) * uses(EXPERTS, k, ROWS_BUF))

            one_pass(0)
            overflow(pool, one_pass)
            pool.sem_inc(S("y_all"), 1)

        @block.vector
        def _(dve):
            V = nc.vector
            counts = {"dve_chain": 0, "dve_chain_over": 0, "dve_chain_last": 0}
            which = ["dve_chain"]

            def chain(ins):
                counts[which[0]] += 1
                ins.then_inc(S(which[0]), 1)
                dve.wait_ge(S(which[0]), counts[which[0]])

            dve.wait_ge(S("rms"), 2)
            chain(V.reciprocal(small[:, RS_, 0:2], small[:, MS_, 4:6]))
            chain(V.reciprocal(small[0:META, RS_, 2:3], small[0:META, MS_, 6:7]))
            for i in range(3):
                rows = META if i == 2 else P
                src = hn[0:META, 2, :] if i == 2 else hres[:, i, :]
                V.tensor_scalar(hn[0:rows, i, :], src, small[0:rows, RS_, i:i + 1], None, ALU.mult).then_inc(S("hn"), 1)
            dve.wait_ge(S("prmp"), 1)
            V.tensor_copy(prmT[:], pb[7][:, 0:ROWS]).then_inc(S("prmT"), 1)
            dve.wait_ge(S("prmT"), 1)
            chain(V.tensor_scalar(halfs[:], prmT[:, ROW_POOL:ROWS], 0.5, None, ALU.mult))
            for k in range(0, KT, 2):
                dve.wait_ge(S("turned"), k + 1)
                V.tensor_scalar(uT[:, k, :], pb[k % 4][:, 0:L], prmT[:, ROW_MIX + k:ROW_MIX + k + 1], None, ALU.mult).then_inc(S("uTd"), 1)
            dve.wait_ge(S("abt"), 1)
            dve.wait_ge(S("params_land"), 8 * 16)
            abp = pb[5][0:CH, 0:48].rearrange("p (c n) -> p c n", c=3)
            V.tensor_tensor(plane3(X_), abp[:, :, 0:8], bc8[:, 1:2, :].to_broadcast([CH, 3, 8]), ALU.add).then_inc(S("xa"), 1)
            dve.wait_ge(S("xa"), 1)
            chain(V.tensor_scalar(plane(RL_), plane(X_), 0.0, None, ALU.max))
            dve.wait_ge(S("lnp"), 1)
            chain(V.tensor_tensor(plane(SP_), plane(RL_), plane(LN_), ALU.add))
            dve.wait_ge(S("ea"), 1)
            V.scalar_tensor_tensor(plane3(G_), plane3(SP_), -1.0, bc8[:, 2:3, :].to_broadcast([CH, 3, 8]), ALU.mult, ALU.mult).then_inc(S("g"), 1)
            dve.wait_ge(S("eb"), 1)
            chain(V.tensor_scalar(plane(BETA_), plane(EB_), 1.0, None, ALU.add))
            chain(V.reciprocal(plane(BETA_), plane(BETA_)))
            V.tensor_scalar(plane(NBETA_), plane(BETA_), -1.0, None, ALU.mult).then_inc(S("beta"), 1)
            dve.wait_ge(S("gamp"), 1)
            chain(V.tensor_copy(plane(GAM_), pb[6][0:CH, 0:24]))
            V.tensor_tensor(plane(GL_), pb[6][0:CH, 32:56], plane(GAM_), ALU.subtract).then_inc(S("kdarg"), 1)
            dve.wait_ge(S("egam"), 1)
            chain(V.tensor_tensor(plane(SKB_), plane(BETA_), plane(EGAM_), ALU.mult))
            dve.wait_ge(S("consts"), CONSTS["masks"])
            dve.wait_ge(S("turned"), KT)
            for h in range(HEADS):
                dve.wait_ge(S("gamB"), h + 1)
                chain(V.tensor_tensor(tmpT[:, h % 2], pb[h % 4][0:CH, 0:LP].rearrange("p (c t) -> p c t", c=3),
                                      plane3(GAM_)[:, :, h:h + 1].to_broadcast([CH, 3, CH]), ALU.subtract))
                V.tensor_tensor(Dm[:, h], negs[:, 0:1, :].to_broadcast([CH, 3, CH]), tmpT[:, h % 2], ALU.subtract).then_inc(S("darg"), 1)
                V.tensor_tensor(DT[:, h], negs[:, 1:2, :].to_broadcast([CH, 3, CH]), tmpT[:, h % 2], ALU.add).then_inc(S("darg"), 1)
                dve.wait_ge(S("darg"), 2 * h + 2)
                dve.sem_inc(S("gamB_free"), 1)

            def c3(ap, n=CH):
                return ap.rearrange("p (c t) -> p c t", c=NC_)

            def per_token(i, h, n):
                return plane3(i)[:, :, h:h + 1].to_broadcast([CH, NC_, n])

            def spread(mask, n=CH):
                return mask.rearrange("p (o t) -> p o t", o=1).to_broadcast([CH, NC_, n])

            for step in ORDER:
                kind = step[0]
                if kind == "take":
                    n, t, j = step[1:]
                    if t in "kqv":
                        i = LIST[t]
                        p = pb[WHERE[("proj", n)][0]]
                        dve.wait_ge(S("tap3"), 3 * j + i + 1)
                        filled(dve, ("proj", n))
                        col = {"q": 0, "k": 8, "v": 16}[t] + j
                        for tap in (2, 1, 0):
                            sh = 3 - tap
                            ins = V.scalar_tensor_tensor(acc[:, i, sh:L], p[:, 0:L - sh], prmT[:, tap * 24 + col:tap * 24 + col + 1],
                                                         acc[:, i, sh:L], ALU.mult, ALU.add)
                            if tap:
                                chain(ins)
                            else:
                                ins.then_inc(S("conv"), 1)
                                dve.wait_ge(S("conv"), 3 * j + i + 1)
                                dve.sem_inc(free[WHERE[("proj", n)][0]], 1)
                    if t == "gB":
                        taken(dve, ("proj", n))
                        taken(dve, ("proj", TILE_OF[("z", j)]))
                        V.scalar_tensor_tensor(zs[:, j % 2, :], thB[:, :], 1.0, zs[:, j % 2, :], ALU.add, ALU.mult).then_inc(S("zg"), 1)
                if kind == "norm":
                    h = step[1]
                    for i, name in enumerate(("nk", "nq")):
                        taken(dve, (name, h))
                        chain(V.reciprocal(rn[:, i, :], rn[:, i, :]))
                        src = kqv[:, h % KQV, i, :]
                        V.scalar_tensor_tensor(src, src, 1.0 if i == 0 else float(P) ** -0.5, rn[:, i, :], ALU.mult, ALU.mult).then_inc(S("kn"), 1)
                if kind == "gram":
                    h = step[1]
                    dve.wait_ge(S("Dm"), h + 1)
                    p = filled(dve, ("G", h))
                    if h:
                        filled(dve, ("AT", h - 1))
                    takes(V.tensor_tensor(Ab[:], c3(p[0:CH, 0:LP]), Dm[:, h], ALU.mult), ("G", h))
                    taken(dve, ("G", h))
                    if h == 0:
                        dve.wait_ge(S("consts"), CONSTS["mups"])
                    chain(V.tensor_tensor(tmpT[:, 0], Ab[:], spread(mlow), ALU.mult))
                    if h >= 2:
                        filled(dve, ("X", h - 2, NL - 1))
                    V.tensor_tensor(Tb[:, h % 2], tmpT[:, 0], spread(ident[0:CH, 0:CH]), ALU.add).then_inc(S("base"), 1)
                    dve.wait_ge(S("DTexp"), h + 1)
                    p = filled(dve, ("QK", h))
                    takes(V.tensor_tensor(DT[:, h], c3(p[0:CH, 0:LP]), DT[:, h], ALU.mult), ("QK", h))
                    if h >= 2:
                        filled(dve, ("wT", h - 2))
                    p = filled(dve, ("KT", h))
                    chain(V.tensor_tensor(Kb[:, h % 2], c3(p[0:CH, 0:NC_ * P]), per_token(SKB_, h, P), ALU.mult))
                    if h == 0:
                        dve.wait_ge(S("egam"), 3)
                    if h >= 3:
                        filled(dve, ("os", h - 3, 1))
                    takes(V.tensor_tensor(Kd[:, h % 3], c3(p[0:CH, 0:NC_ * P]), per_token(KD_, h, P), ALU.mult), ("KT", h))
                    p = filled(dve, ("VT", h))
                    takes(V.tensor_tensor(Vb[:, h % 2], c3(p[0:CH, 0:NC_ * P]), per_token(BETA_, h, P), ALU.mult), ("VT", h))
                if kind == "turn":
                    h = step[1]
                    taken(dve, ("AT", h))
                    chain(V.tensor_tensor(tmpT[:, 1], ATb[:, h % 2], spread(mup[:, 0, :]), ALU.mult))
                    if h >= 2:
                        filled(dve, ("wT", h - 2))
                    V.tensor_tensor(Ub[:, h % 2], tmpT[:, 1], spread(ident[0:CH, 0:CH]), ALU.add).then_inc(S("base"), 1)
                if kind == "ly":
                    h, lv = step[1:]
                    q = filled(dve, ("YT", h, lv))
                    if lv < NL - 1:
                        p = pb[WHERE[("Y", h, lv)][0]]
                        takes(V.tensor_tensor(Tb[:, h % 2], c3(p[0:CH, 0:LP]), Tb[:, h % 2], ALU.add), ("Y", h, lv))
                    takes(V.tensor_tensor(Ub[:, h % 2], c3(q[0:CH, 0:LP]), Ub[:, h % 2], ALU.add), ("YT", h, lv))
                if kind in ("s0", "sb"):
                    h = step[1]
                    c = 0 if kind == "s0" else step[2]
                    key = ("os",) + ((h, 0) if kind == "s0" else (h, c))
                    p = filled(dve, key)
                    if h:
                        filled(dve, ("oT", h - 1))
                    if c == 0:
                        V.tensor_copy(osb[:, 0, :], p[0:CH, 0:P]).then_inc(S("o"), 1)
                        if h:
                            filled(dve, ("o1", h - 1, 2))
                        takes(V.tensor_copy(St[:, 0, :], p[:, P:2 * P]), key)
                    else:
                        taken(dve, ("o1", h, c))
                        ins = V.tensor_tensor(osb[:, c, :], p[0:CH, 0:P], o1s[:, c - 1, :], ALU.add)
                        if c == 1:
                            ins.then_inc(S("o"), 1)
                            if h:
                                filled(dve, ("o1", h - 1, 2))
                            takes(V.scalar_tensor_tensor(St[:, 1, :], St[:, 0, :], small[:, CD_, c * 8 + h:c * 8 + h + 1],
                                                         p[:, P:2 * P], ALU.mult, ALU.add), key)
                        else:
                            takes(ins, key)
                if kind == "sa":
                    h, c = step[1:]
                    p = filled(dve, ("ws", h, c))
                    if h:
                        filled(dve, ("os", h - 1, c))
                    takes(V.scalar_tensor_tensor(vn[:, c - 1, :], p[0:CH, 0:P], -1.0, ub[:, h % 2, c, :], ALU.mult, ALU.add), ("ws", h, c))
                if kind == "onorm":
                    h = step[1]
                    dve.wait_ge(S("orms"), h + 1)
                    chain(V.reciprocal(small[0:CH, ORS_, 0:3], small[0:CH, ORS_, 4:7]))
                    V.tensor_tensor(osb[:], osb[:], small[0:CH, ORS_, 0:3].rearrange("p (c o) -> p c o", o=1).to_broadcast([CH, 3, P]), ALU.mult).then_inc(S("ors"), 1)
                if kind == "out":
                    h = step[1]
                    p = filled(dve, ("oT", h))
                    dve.wait_ge(S("zg"), h + 1)
                    takes(V.scalar_tensor_tensor(merged[:, h, :], p[:, REAL:LP], halfs[:, 8:9], zs[:, h % 2, :], ALU.mult, ALU.mult), ("oT", h))
                if kind == "mix":
                    j = step[1]
                    for d in range(2):
                        ch = j - 1 + d
                        p = filled(dve, (f"m{d}", j))
                        taken(dve, ("proj", TILE_OF[("gA", ch)]))
                        takes(V.scalar_tensor_tensor(thA[:, d, :], thA[:, d, :], 1.0, p[:, 0:SEQ], ALU.add, ALU.mult), (f"m{d}", j))
                        taken(dve, (f"m{d}", j))
                        taken(dve, ("oT", ch))
                        V.scalar_tensor_tensor(merged[:, ch, :], thA[:, d, :], halfs[:, ch:ch + 1], merged[:, ch, :], ALU.mult, ALU.add).then_inc(S("mixed"), 1)

            for i in range(TT):
                for half in range(2):
                    dve.wait_ge(S("outproj"), 1)
                    o = hres[:, i, half * 512:(half + 1) * 512]
                    V.tensor_tensor(o, pb[2 * i + half][:], o, ALU.add).then_inc(S("res"), 1)
            for i in range(TT):
                dve.wait_ge(S("rms"), 2 + TT)
                chain(V.reciprocal(rs[:, i, 1:2], rs[:, i, 22:23]))
                V.tensor_scalar(xn[:, i, :], hres[:, i, :], rs[:, i, 1:2], None, ALU.mult).then_inc(S("xn"), 1)
            for k in range(KT):
                b, half = k % 4, k // 4
                V.tensor_scalar(wff[:, 2 * b + half, :], ones[:, 0:SLOTS], prmT[:, ROW_FFN + k:ROW_FFN + k + 1], None, ALU.mult).then_inc(S("wff"), 1)
            for k in range(0, KT, 2):
                dve.wait_ge(S("turned"), KT + k + 1)
                V.tensor_scalar(x2T[:, k, :], pb[k % 4][:, 0:SEQ], prmT[:, ROW_FFN + k:ROW_FFN + k + 1], None, ALU.mult).then_inc(S("uTd"), 1)
            dve.wait_ge(S("rconst"), 1)
            dve.wait_ge(S("rout_land"), 64)
            for i in range(TT):
                dve.wait_ge(S("logits"), i + 1)
                lg, le = rt[:, i, 0, 0:8], rt[:, i, 1, :]
                chain(V.memset(rt[:, i, 0, 0:8], NEG))
                chain(V.tensor_tensor(rt[:, i, 0, 0:GROUPS], pb[4 + i][:, 0:GROUPS], rbias[:, 0:GROUPS], ALU.add))
                chain(V.tensor_tensor(le, pb[4 + i][:, GROUPS:36], rbias[:, GROUPS:36], ALU.add))
                chain(V.max(rt[:, i, 2, 0:8], lg))
                chain(V.max_index(ru[:, i, 0:8], rt[:, i, 2, 0:8], lg))
                chain(V.tensor_copy(rs[:, i, 13:14], ru[:, i, 0:1]))
                chain(V.tensor_scalar(rt[:, i, 3, :], iota_g[:], rs[:, i, 13:14], 1.0, ALU.is_equal, ALU.subtract))
                chain(V.scalar_tensor_tensor(rt[:, i, 4, :], rt[:, i, 3, :], -NEG, le, ALU.mult, ALU.add))
                chain(V.max(rt[:, i, 5, 0:8], rt[:, i, 4, :]))
                chain(V.max_index(ru[:, i, 8:16], rt[:, i, 5, 0:8], rt[:, i, 4, :]))
                chain(V.tensor_copy(rs[:, i, 14:16], ru[:, i, 8:10]))
                for k in range(2):
                    chain(V.tensor_scalar(rt[:, i, 6 + k, :], iota_e[:], rs[:, i, 14 + k:15 + k], None, ALU.is_equal))
                V.tensor_tensor(rt[:, i, 8, :], rt[:, i, 6, :], rt[:, i, 7, :], ALU.add).then_inc(S("picked"), 1)
                chain(V.tensor_scalar(rs[:, i, 2:3], rt[:, i, 2, 0:1], -1.0, None, ALU.mult))
                V.tensor_tensor(rs[:, i, 5:6], rt[:, i, 5, 1:2], rt[:, i, 5, 0:1], ALU.subtract).then_inc(S("rexp_in"), 1)
            dve.wait_ge(S("pos"), 3)
            for i in range(TT):
                for k in range(2):
                    chain(V.tensor_tensor(rt[:, i, 9 + k, :], rt[:, i, 6 + k, :], pb[6][:, 32 * i:32 * i + 32], ALU.mult))
                    chain(V.tensor_reduce(rs[:, i, 16 + k:17 + k], rt[:, i, 9 + k, :], AX.X, ALU.add))
            chain(V.max(most[:], pb[6][:, 64:96]))
            V.tensor_copy(mosti[:], most[:, 0:1]).then_inc(S("most"), 1)

            def build_lists(ps):
                if ps:
                    chain(V.tensor_scalar(rs[:, 0, 16:18], rs[:, 0, 16:18], -float(SLOTS), None, ALU.add))
                    chain(V.tensor_scalar(rs[:, 1, 16:18], rs[:, 1, 16:18], -float(SLOTS), None, ALU.add))
                    dve.wait_ge(S("scol"), EXPERTS * ps)
                    dve.wait_ge(S("gcol"), EXPERTS * ps)
                for i in range(TT):
                    for k in range(2):
                        V.tensor_scalar(hot[:, 2 * i + k, :], iota_c[:], rs[:, i, 16 + k:17 + k], iota_t[:, i:i + 1], ALU.is_equal, ALU.mult).then_inc(S("hot"), 1)
                dve.wait_ge(S("listp"), ps + 1)
                chain(V.tensor_scalar(lists[:, 0, :], pb[7][:, 0:EXPERTS], halfof[:, 0:1], None, ALU.add))
                chain(V.tensor_scalar(lists[:, 1, :], pb[7][:, EXPERTS:2 * EXPERTS], 0.0, float(2 * SEQ), ALU.not_equal, ALU.mult))
                chain(V.tensor_tensor(lists[:, 0, :], pb[7][:, EXPERTS:2 * EXPERTS], lists[:, 0, :], ALU.add))
                chain(V.tensor_copy(gidx[:], lists[:, 0, :]))
                chain(V.tensor_tensor(sidx[:], lists[:, 0, :], lists[:, 1, :], ALU.add))
                dve.sem_inc(S("lists"), 1)

            def one_pass(ps):
                base = EXPERTS * ps
                build_lists(ps)
                if ps == 0:
                    weights()

                def one(e, first):
                    n = e + base
                    dve.wait_ge(S("xT"), n + 1)
                    if not first:
                        dve.wait_ge(S("up"), n)
                    V.tensor_tensor(xgT[:, 0, :], pb[0][:], wff[:].rearrange("p k s -> p (k s)"), ALU.mult).then_inc(S("xgT"), 1)

                def mid(e, first):
                    n = e + base
                    dve.wait_ge(S("sgate"), n + 1)
                    dve.wait_ge(S("up"), n + 1)
                    if not first:
                        dve.wait_ge(S("hTp"), n)
                    V.tensor_tensor(hmid[:, 0, :], pb[2][:, 0:FF // 2], sgate[:, 0, :], ALU.mult).then_inc(S("hmid"), 1)
                    dve.wait_ge(S("hTp"), n + 1)
                    if not first:
                        dve.wait_ge(S("y"), n)
                    V.tensor_copy(hT[:, 0].rearrange("p a b -> p (a b)"), pb[3][:, 0:2 * P]).then_inc(S("hT"), 1)

                one(0, ps == 0)
                for e in range(3):
                    mid(e, ps == 0 and e == 0)
                    one(e + 1, False)
                with dve.Fori(1, EXPERTS // 3) as i:
                    for j in range(3):
                        mid(i * 3 + j, False)
                        one(i * 3 + (j + 1), False)
                for e in range(EXPERTS // 3 * 3, EXPERTS):
                    mid(e, False)
                    if e < EXPERTS - 1:
                        one(e + 1, False)

            def weights():
                for i in range(TT):
                    dve.wait_ge(S("rexp"), 2 * i + 2)
                    chain(V.reciprocal(rs[:, i, 6:7], rs[:, i, 3:4]))
                    chain(V.tensor_scalar(rs[:, i, 7:8], rs[:, i, 4:5], 1.0, None, ALU.add))
                    chain(V.reciprocal(rs[:, i, 18:19], rs[:, i, 7:8]))
                    chain(V.tensor_tensor(rs[:, i, 19:20], rs[:, i, 18:19], rs[:, i, 6:7], ALU.mult))
                    chain(V.tensor_tensor(rs[:, i, 20:21], rs[:, i, 19:20], rs[:, i, 4:5], ALU.mult))

            one_pass(0)
            which[0] = "dve_chain_over"
            overflow(dve, one_pass)
            which[0] = "dve_chain_last"
            for i in range(TT):
                for k in range(2):
                    dve.wait_ge(S(f"y_back{i}"), 32)
                    chain(V.scalar_tensor_tensor(hres[:, i, :], ring[:, 2 * i + k, 0:D], rs[:, i, 19 + k:20 + k], hres[:, i, :], ALU.mult, ALU.add))
                dve.sem_inc(S("fin_h"), 1)
            for i in range(TT):
                dve.wait_ge(S("rms"), 2 + TT + i + 1)
                chain(V.reciprocal(rs[:, i, 21:22], rs[:, i, 23:24]))
                dve.wait_ge(S("wf_land"), 16)
                V.scalar_tensor_tensor(ring[:, 7 + i, 0:D], hres[:, i, :], rs[:, i, 21:22], ring[:, 5, 0:D], ALU.mult, ALU.mult).then_inc(S("final"), 1)

        @block.tensor
        def _(pe):
            T = nc.tensor
            pe.wait_ge(S("consts"), CONSTS["ident"])
            pe.wait_ge(S("params_land"), 8 * 16)
            T.transpose(pb[7][:, 0:ROWS], prm[0:ROWS, :], ident[0:ROWS, 0:ROWS]).then_inc(S("prmp"), 1)
            pe.wait_ge(S("hn"), 3)
            for k in range(KT):
                if k >= 4:
                    pe.wait_ge(S("uT" if k % 2 else "uTd"), (k - 4) // 2 + 1)
                for i, (c0, rows) in enumerate(((META, P), (META + P, P), (0, META))):
                    ins = T.transpose(pb[k % 4][:, c0:c0 + rows], hn[0:rows, i, k * P:(k + 1) * P], ident[0:rows, 0:rows])
                ins.then_inc(S("turned"), 1)
            pe.wait_ge(S("uT"), KT // 2)
            pe.wait_ge(S("uTd"), KT // 2)
            pe.wait_ge(S("params_land"), 8 * 16)
            for k in range(KT):
                ins = T.matmul(pb[4][0:16, 0:L], wab[:, k, :], uT[:, k, :], start=(k == 0), stop=(k == KT - 1))
            ins.then_inc(S("ab"), 1)
            pe.wait_ge(S("abT"), 1)
            for c in range(NC_):
                ins = T.transpose(pb[5][0:CH, 16 * c:16 * c + 16], abT[:, c * CH:(c + 1) * CH], ident[0:16, 0:16])
            ins.then_inc(S("abt"), 1)
            pe.wait_ge(S("g"), 1)
            pe.wait_ge(S("consts"), CONSTS["masks"])
            pe.wait_ge(S("consts"), CONSTS["ones"])
            T.matmul(pb[6][0:CH, 0:24], uincl[:], plane(G_), start=True, stop=True)
            T.matmul(pb[6][:, 32:56], ones[0:CH, :], plane(G_), start=True, stop=True).then_inc(S("gamp"), 1)
            for h in range(HEADS):
                if h >= 4:
                    pe.wait_ge(S("gamB_free"), h - 3)
                for c in range(NC_):
                    ins = T.matmul(pb[h % 4][0:CH, c * CH:(c + 1) * CH], small[0:CH, G_, c * 8 + h:c * 8 + h + 1].to_broadcast([CH, CH]),
                                   uincl[:], start=True, stop=True)
                ins.then_inc(S("gamB"), 1)
            pe.wait_ge(S("gamB_free"), HEADS)
            pe.wait_ge(S("prmT"), 1)
            pe.wait_ge(S("eb"), 1)
            pe.wait_ge(S("kdarg"), 1)
            pe.wait_ge(S("egam"), 2)

            def cs(ap, c, n):
                return ap[:, c * n:(c + 1) * n]

            def per_chunk(key, rows, width, product):
                p = bank(pe, key)
                for c in range(NC_):
                    ins = product(p[0:rows, c * width:(c + 1) * width], c)
                fills(ins, key)

            for step in ORDER:
                kind = step[0]
                if kind == "proj":
                    n, t, j, k = step[1:]
                    if k == 0:
                        pe.wait_ge(win_land[n % WIN_SLOTS], 16 * (n // WIN_SLOTS + 1))
                        bank(pe, ("proj", n))
                    p = pb[WHERE[("proj", n)][0]]
                    lo = 0 if t in "kqvP" else META
                    ins = T.matmul(p[:, 0:L - lo], win[:, n % WIN_SLOTS, k, :], uT[:, k, lo:L], start=(k == 0), stop=(k == KT - 1))
                    if k == KT - 1:
                        fills(ins, ("proj", n))
                if kind == "norm":
                    h = step[1]
                    for i, name in enumerate(("nk", "nq")):
                        p = bank(pe, (name, h))
                        pe.wait_ge(S("sq"), 2 * h + i + 1)
                        fills(T.matmul(p[:, 0:LP], ones[:], sq[:, i, :], start=True, stop=True), (name, h))
                if kind == "gram":
                    h = step[1]

                    def part(i, c):
                        return kqv[:, h % KQV, i, c * CH:(c + 1) * CH]

                    pe.wait_ge(S("kn"), 2 * h + 1)
                    per_chunk(("G", h), CH, CH, lambda o, c: T.matmul(o, part(0, c), part(0, c), start=True, stop=True))
                    pe.wait_ge(S("kn"), 2 * h + 2)
                    per_chunk(("QK", h), CH, CH, lambda o, c: T.matmul(o, part(0, c), part(1, c), start=True, stop=True))
                    per_chunk(("KT", h), CH, P, lambda o, c: T.transpose(o, part(0, c), ident[:]))
                    pe.wait_ge(S("silu"), 3 * h + 3)
                    per_chunk(("VT", h), CH, P, lambda o, c: T.transpose(o, part(2, c), ident[:]))
                if kind == "turn":
                    h = step[1]
                    taken(pe, ("G", h))
                    per_chunk(("AT", h), CH, CH, lambda o, c: T.transpose(o, Ab[:, c, :], ident[0:CH, 0:CH]))
                if kind == "lx":
                    h, lv = step[1:]
                    pe.wait_ge(S("OT"), OT_AT[(h, lv)])
                    if lv == 0:
                        pe.wait_ge(S("base"), 2 * h + 2)
                    else:
                        taken(pe, ("Y", h, lv - 1))
                        taken(pe, ("YT", h, lv - 1))
                    per_chunk(("X", h, lv), CH, CH, lambda o, c: T.matmul(o, OTb[:, h % 2, lv % 2, c, :], Tb[:, h % 2, c, :], start=True, stop=True))
                if kind == "ly":
                    h, lv = step[1:]
                    taken(pe, ("X", h, lv))
                    if lv < NL - 1:
                        per_chunk(("Y", h, lv), CH, CH, lambda o, c: T.matmul(o, Ub[:, h % 2, c, :], Xb[:, h % 2, c, :], start=True, stop=True))
                    per_chunk(("YT", h, lv), CH, CH, lambda o, c: T.matmul(o, Xb[:, h % 2, c, :], Ub[:, h % 2, c, :], start=True, stop=True))
                if kind == "solve":
                    h = step[1]
                    taken(pe, ("YT", h, NL - 1))
                    taken(pe, ("VT", h))
                    per_chunk(("u", h), CH, P, lambda o, c: T.matmul(o, Ub[:, h % 2, c, :], Vb[:, h % 2, c, :], start=True, stop=True))
                    taken(pe, ("KT", h))
                    per_chunk(("wT", h), P, CH, lambda o, c: T.matmul(o, Kb[:, h % 2, c, :], Ub[:, h % 2, c, :], start=True, stop=True))
                if kind in ("s0", "sb"):
                    h = step[1]
                    c = 0 if kind == "s0" else step[2]
                    if c == 0:
                        taken(pe, ("u", h))
                        taken(pe, ("QK", h))
                        new = ub[:, h % 2, 0, :]
                    else:
                        taken(pe, ("ws", h, c))
                        new = vn[:, c - 1, :]
                    p = bank(pe, ("os", h, c))
                    ins = T.matmul(p[0:CH, 0:P], DT[:, h, c, :], new, start=True, stop=True)
                    if c < NC_ - 1:
                        ins = T.matmul(p[:, P:2 * P], Kd[:, h % 3, c, :], new, start=True, stop=True)
                    fills(ins, ("os", h, c))
                if kind == "sa":
                    h, c = step[1:]
                    taken(pe, ("os", h, c - 1))
                    taken(pe, ("wT", h))
                    p = bank(pe, ("ws", h, c))
                    fills(T.matmul(p[0:CH, 0:P], wT[:, h % 2, c, :], St[:, c - 1, :], start=True, stop=True), ("ws", h, c))
                    p = bank(pe, ("o1", h, c))
                    fills(T.matmul(p[0:CH, 0:P], kqv[:, h % KQV, 1, c * CH:(c + 1) * CH], St[:, c - 1, :], start=True, stop=True), ("o1", h, c))
                if kind == "out":
                    h = step[1]
                    pe.wait_ge(S("ors"), h + 1)
                    per_chunk(("oT", h), P, CH, lambda o, c: T.transpose(o, osb[:, c, :], ident[0:CH, 0:CH]))
                if kind == "mix":
                    j = step[1]
                    g = j // 2
                    pe.wait_ge(S("pooled"), j + 1)
                    pe.wait_ge(S(f"poolw_land{g % 2}"), 16 * (g // 2 + 1))
                    for d in range(2):
                        p = bank(pe, (f"m{d}", j))
                        for a in range(2):
                            ins = T.matmul(p[:, 0:SEQ], poolw[:, g % 2, a, d * P:(d + 1) * P], pooled[:, a, :], start=(a == 0), stop=(a == 1))
                        fills(ins, (f"m{d}", j))

            for b in range(8):
                if USES[b]:
                    pe.wait_ge(free[b], USES[b])
            for k in range(KT):
                n = len(TILES) + k
                pe.wait_ge(S("mixed"), k + 1)
                pe.wait_ge(win_land[n % WIN_SLOTS], 16 * (n // WIN_SLOTS + 1))
                for i in range(TT):
                    for half in range(2):
                        ins = T.matmul(pb[2 * i + half][:], merged[:, k, i * P:(i + 1) * P],
                                       wout[:, n % WIN_SLOTS, half * 512:(half + 1) * 512], start=(k == 0), stop=(k == KT - 1))
                if k < KT - WIN_SLOTS:
                    ins.then_inc(S("wout_used"), 1)
            ins.then_inc(S("outproj"), 1)
            pe.wait_ge(S("res"), 4)
            for k in range(KT):
                if k >= 4:
                    pe.wait_ge(S("uT" if k % 2 else "uTd"), KT // 2 + (k - 4) // 2 + 1)
                for i in range(TT):
                    pe.wait_ge(S("xn"), i + 1)
                    ins = T.transpose(pb[k % 4][:, i * P:(i + 1) * P], xn[:, i, k * P:(k + 1) * P], ident[:])
                ins.then_inc(S("turned"), 1)
            pe.wait_ge(S("rout_land"), 64)
            for i in range(TT):
                for k in range(KT):
                    pe.wait_ge(S("uT" if k % 2 else "uTd"), KT // 2 + k // 2 + 1)
                    ins = T.matmul(pb[4 + i][:, 0:36], x2T[:, k, i * P:(i + 1) * P], routw[:, k, :], start=(k == 0), stop=(k == KT - 1))
                ins.then_inc(S("logits"), 1)
            pe.wait_ge(S("picked"), 1)
            T.matmul(pb[6][:, 0:32], before[:], rt[:, 0, 8, :], start=True, stop=True).then_inc(S("pos"), 1)
            pe.wait_ge(S("picked"), 2)
            T.matmul(pb[6][:, 32:64], ones[:], rt[:, 0, 8, :], start=True, stop=False)
            T.matmul(pb[6][:, 32:64], before[:], rt[:, 1, 8, :], start=False, stop=True).then_inc(S("pos"), 1)
            T.matmul(pb[6][:, 64:96], ones[:], rt[:, 0, 8, :], start=True, stop=False)
            T.matmul(pb[6][:, 64:96], ones[:], rt[:, 1, 8, :], start=False, stop=True).then_inc(S("pos"), 1)

            def one_pass(ps):
                base = EXPERTS * ps
                for k in range(2):
                    for i in range(TT):
                        pe.wait_ge(S("hot"), 4 * ps + 2 * i + k + 1)
                        ins = T.matmul(pb[7][:, 32 * k:32 * k + 32], hot[:, 2 * i + k, :], rt[:, i, 6 + k, :], start=(i == 0), stop=(i == TT - 1))
                ins.then_inc(S("listp"), 1)

                def turn(n, k, landed, first):
                    pe.wait_ge(S(f"xg_land{k}"), landed)
                    if not first:
                        pe.wait_ge(S("xgT"), n)
                    for b in range(4):
                        ins = T.transpose(pb[0][:, b * P:(b + 1) * P], xg[:, k, b * P:(b + 1) * P], ident[:])
                    ins.then_inc(S("xT"), 1)

                def gate_up(n, k, landed, first):
                    pe.wait_ge(S("xgT"), n + 1)
                    for c, name in ((0, "gate"), (1, "up")):
                        pe.wait_ge(S(f"w_land{3 * k + c}"), landed)
                        if not first:
                            pe.wait_ge(S("hmid"), n)
                        w = ring[:, 3 * k + c, :].rearrange("p (k f) -> p k f", k=KT)
                        for kt in range(KT):
                            b = 2 * (kt % 4) + kt // 4
                            lhs = xgT[:, 0, b * SLOTS:(b + 1) * SLOTS]
                            for g in range(2):
                                ins = T.matmul(pb[1 + c][g * 64:g * 64 + SLOTS, 0:256], lhs, w[:, kt, g * 256:(g + 1) * 256],
                                               start=(kt == 0), stop=(kt == KT - 1), skip_group_check=True)
                        ins.then_inc(S(name), 1)

                def down(n, k, landed, first):
                    pe.wait_ge(S("hmid"), n + 1)
                    if not first:
                        pe.wait_ge(S("hT"), n)
                    for b in range(2):
                        ins = T.transpose(pb[3][:, b * P:(b + 1) * P], hmid[:, 0, b * P:(b + 1) * P], ident[:])
                    ins.then_inc(S("hTp"), 1)
                    pe.wait_ge(S("hT"), n + 1)
                    pe.wait_ge(S(f"w_land{3 * k + 2}"), landed)
                    if not first:
                        pe.wait_ge(S("yout"), n)
                    w = ring[:, 3 * k + 2, :].rearrange("p (k d) -> p k d", k=4)
                    for f in range(4):
                        g, b = f // 2, f % 2
                        for half in range(2):
                            ins = T.matmul(pb[4][half * 64:half * 64 + SLOTS, :], hT[:, 0, b, g * 64:g * 64 + SLOTS],
                                           w[:, f, half * 512:(half + 1) * 512], start=(f == 0), stop=(f == 3), skip_group_check=True)
                    ins.then_inc(S("y"), 1)

                wused = [ps * uses(EXPERTS, k, 3) for k in range(3)]
                xused = [ps * uses(EXPERTS, k, ROWS_BUF) for k in range(ROWS_BUF)]

                def step(e, i, j, first, last):
                    n = e + base
                    k = j % 3
                    landed = i * (16 * (ROWS_BUF // 3)) + 16 * (wused[k] + j // 3 + 1)
                    gate_up(n, k, landed, first)
                    if not last:
                        k2 = (j + 1) % ROWS_BUF
                        turn(e + (base + 1), k2, i * 16 + 16 * (xused[k2] + 1 + (j + 1) // ROWS_BUF), False)
                    down(n, k, landed, first)

                turn(base, 0, 16 * (xused[0] + 1), ps == 0)
                for e in range(ROWS_BUF):
                    step(e, 0, e, ps == 0 and e == 0, False)
                with pe.Fori(1, EXPERTS // ROWS_BUF) as i:
                    for j in range(ROWS_BUF):
                        step(i * ROWS_BUF + j, i, j, False, False)
                for e in range(EXPERTS // ROWS_BUF * ROWS_BUF, EXPERTS):
                    step(e, e // ROWS_BUF, e % ROWS_BUF, False, e == EXPERTS - 1)

            one_pass(0)
            overflow(pe, one_pass)
            pe.sem_inc(S("pe_done"), 1)

_INS = ["x", "meta_tokens", "norm_mix_w", "w_in", "conv_w", "pool_w", "pool_scale", "a_log", "dt_bias", "dn_norm_w",
        "w_out", "norm_ffn_w", "router_group_w", "router_group_b", "router_expert_w", "router_expert_b",
        "expert_w_gate", "expert_w_up", "expert_w_down", "norm_final_w"]
_OUTS = [((1, SEQ, D), "float32")]


def kernel(**inputs):
    import numpy as _np
    import concourse.bacc as _bacc
    from concourse import mybir as _mybir
    from concourse.bass_utils import run_bass_kernel_spmd as _run

    nc = _bacc.Bacc("TRN2", target_bir_lowering=False, num_devices=1)
    arrays, args = {}, []
    for name in _INS:
        a = _np.ascontiguousarray(inputs[name])
        arrays[f"in_{name}_dram"] = a
        args.append(nc.dram_tensor(f"in_{name}_dram", a.shape, _mybir.dt.from_np(a.dtype), kind="ExternalInput").ap())
    for i, (shape, dtype) in enumerate(_OUTS):
        dt = _mybir.dt.from_np(_np.dtype(dtype))
        args.append(nc.dram_tensor(f"out_{i}_dram", shape, dt, kind="ExternalOutput").ap())
    build_block(nc, *args)
    r = _run(nc, [arrays], core_ids=[0])
    got = tuple(r.results[0][f"out_{i}_dram"] for i in range(len(_OUTS)))
    return got[0]
```

```python
from contextlib import ExitStack

import numpy as np
import concourse.bass as bass
from concourse import mybir

F32 = mybir.dt.float32
I32 = mybir.dt.int32
U32 = mybir.dt.uint32
ALU = mybir.AluOpType
ACT = mybir.ActivationFunctionType
AX = mybir.AxisListType

P = 128
D = 1024
KT = D // P
META = 16
SEQ = 256
TT = SEQ // P
L = META + SEQ
HEADS = 8
CH = 96
PAD = 16
LP = PAD + L
NC_ = LP // CH
REAL = PAD + META
TAPS = 4
LEVELS = [2, 4, 8, 16, 32, 64]
NL = len(LEVELS)
GROUPS = 4
PER_GROUP = 8
EXPERTS = GROUPS * PER_GROUP
FF = 512
EPS = 1e-6
NEG = -1e30
COL = {"P": 0, "q": 1024, "k": 2048, "v": 3072, "z": 4096, "gA": 5136, "gB": 6160}
COL_AB = 5120
WIN_SLOTS = 6
CHUNK = 4096
SLOTS = 64
SPLIT = 3
PASSES = -(-SEQ // SLOTS)
DESK = 6192
CONSTS = {n: i + 1 for i, n in enumerate(["ident", "ones", "eps", "abz", "masks", "mups", "kqv_zero"])}
RINGS = 3
PAIRS = EXPERTS // 2
ROOMS = 3
KQV = 4
ROW_CONV, ROW_MIX, ROW_FFN, ROW_POOL, ROW_DN, ROWS = 0, 96, 104, 112, 120, 121


def plan_rounds():
    order = []
    tile = 0
    for r in range(HEADS + 3):
        kinds = [(t, r) for t in "kqv"] if r < HEADS else []
        j = r - 3
        if j >= 0:
            kinds = [("z", j), ("gB", j)] + kinds
            kinds += [("P", j), ("P", j + 1)] if j % 2 == 0 else [("gA", j - 1), ("gA", j)]
        fill = []
        for t, j2 in kinds:
            fill += [("proj", tile, t, j2, k) for k in range(KT)]
            fill += [("take", tile, t, j2)]
            if t == "v":
                fill += [("silu", x, j2) for x in "kqv"]
            tile += 1
        lists = [fill]
        if 0 <= r - 1 < HEADS:
            h = r - 1
            lists.append([("norm", h), ("gram", h), ("turn", h)] + [(s, h, lv) for lv in range(SPLIT) for s in ("lx", "ly")])
        if 0 <= r - 2 < HEADS:
            h = r - 2
            lists.append([(s, h, lv) for lv in range(SPLIT, NL) for s in ("lx", "ly")] + [("solve", h)])
        if 0 <= r - 3 < HEADS:
            h = r - 3
            lists.append([("s0", h), ("sa", h, 1), ("sb", h, 1), ("sa", h, 2), ("sb", h, 2), ("onorm", h), ("out", h)])
        at = [((i + 1) / len(lst), n, i) for n, lst in enumerate(lists) for i in range(len(lst))]
        order += [lists[n][i] for _, n, i in sorted(at)]
        if j >= 0 and j % 2 == 1:
            order += [("mix", j)]
    return order


ORDER = plan_rounds()
PSUM_OF = {
    "norm": ["nk", "nq"], "gram": ["G", "QK", "KT", "VT"], "turn": ["AT"], "lx": ["X"], "ly": ["Y", "YT"],
    "solve": ["u", "wT"], "s0": ["os"], "sa": ["ws", "o1"], "sb": ["os"], "out": ["oT"], "mix": ["m0", "m1"],
}


def plan_banks():
    where, n = {}, 0
    for step in ORDER:
        if step[0] == "take":
            where[("proj", step[1])] = (step[1] % 2, step[1] // 2)
        for name in PSUM_OF.get(step[0], []):
            if name == "Y" and step[2] == NL - 1:
                continue
            key = (name,) + tuple(step[1:]) + ((0,) if step[0] == "s0" else ())
            where[key] = (2 + n % 6, n // 6)
            n += 1
    uses = [0] * 8
    for b, u in where.values():
        uses[b] = max(uses[b], u + 1)
    return where, uses


WHERE, USES = plan_banks()
TILES = [(s[2], s[3]) for s in ORDER if s[0] == "take"]
OT_ORDER = []
for _s in ORDER:
    if _s[0] == "turn":
        OT_ORDER += [(_s[1], 0), (_s[1], 1)]
    if _s[0] == "ly" and _s[2] + 2 < NL:
        OT_ORDER.append((_s[1], _s[2] + 2))
OT_AT = {k: n + 1 for n, k in enumerate(OT_ORDER)}
TILE_OF = {t: n for n, t in enumerate(TILES)}


def uses(n, k, slots):
    return (n - k + slots - 1) // slots


def build_block(nc, x, meta_tokens, norm_mix_w, w_in, conv_w, pool_w, pool_scale, a_log, dt_bias, dn_norm_w,
                w_out, norm_ffn_w, router_group_w, router_group_b, router_expert_w, router_expert_b,
                expert_w_gate, expert_w_up, expert_w_down, norm_final_w, out):
    ctx = ExitStack()
    with ctx:
        def sb(name, shape, dt=F32):
            return ctx.enter_context(nc.sbuf_tensor(name, shape, dt))

        def sem(name):
            return ctx.enter_context(nc.semaphore(name))

        class Named:
            def __init__(self):
                self.made = {}

            def __call__(self, name):
                if name not in self.made:
                    self.made[name] = sem("s_" + name)
                return self.made[name]

        S = Named()

        ring = sb("ring", [P, 9, CHUNK])
        room = ring[:, 3:9, :].rearrange("p a b -> p (a b)")
        at = [0]

        def take(n, rows=P):
            at[0] += n
            assert at[0] <= 6 * CHUNK, at[0]
            return room[0:rows, at[0] - n:at[0]]

        win = take(WIN_SLOTS * D).rearrange("p (s k c) -> p s k c", s=WIN_SLOTS, k=KT)
        wout = win.rearrange("p s k c -> p s (k c)")
        uT = take(KT * L).rearrange("p (k t) -> p k t", k=KT)
        kqv = take(KQV * 3 * LP).rearrange("p (b i t) -> p b i t", b=KQV, i=3)
        decay_at = at[0]
        Dm = take(HEADS * LP, CH).rearrange("p (h c t) -> p h c t", h=HEADS, c=NC_)
        DT = take(HEADS * LP, CH).rearrange("p (h c t) -> p h c t", h=HEADS, c=NC_)
        hn = room[:, decay_at:decay_at + 3 * D].rearrange("p (i d) -> p i d", i=3)
        sq = take(2 * LP).rearrange("p (i t) -> p i t", i=2)
        rn = take(2 * LP).rearrange("p (i t) -> p i t", i=2)

        def chunks(n, rows=CH):
            return take(n * NC_, rows).rearrange("p (c t) -> p c t", c=NC_)

        def two_chunks():
            return take(2 * LP, CH).rearrange("p (b c t) -> p b c t", b=2, c=NC_)

        Ab = chunks(CH)
        ATb = two_chunks()
        Tb = two_chunks()
        Ub = two_chunks()
        Xb = two_chunks()

        OTb = take(4 * LP, CH).rearrange("p (b l c t) -> p b l c t", b=2, l=2, c=NC_)
        tmpT = take(2 * LP, CH).rearrange("p (b c t) -> p b c t", b=2, c=NC_)
        late = sb("late", [P, TT * D])
        xn = late[:].rearrange("p (i d) -> p i d", i=TT)
        Kb = late[0:CH, 0:2 * NC_ * P].rearrange("p (b c t) -> p b c t", b=2, c=NC_)
        Kd = late[0:CH, 2 * NC_ * P:5 * NC_ * P].rearrange("p (b c t) -> p b c t", b=3, c=NC_)
        ub = take(2 * NC_ * P, CH).rearrange("p (b c t) -> p b c t", b=2, c=NC_)
        desk = sb("desk", [P, DESK])
        desk_at = [0]

        def lay(shape, rows=P):
            n = int(np.prod(shape))
            desk_at[0] += n
            assert desk_at[0] <= DESK, desk_at[0]
            v = desk[0:rows, desk_at[0] - n:desk_at[0]]
            names = "abcd"[:len(shape)]
            return v if len(shape) == 1 else v.rearrange(f"p ({' '.join(names)}) -> p {' '.join(names)}", **dict(zip(names[1:], shape[1:])))

        Vb = lay([2, NC_, P], CH)
        wT = lay([2, NC_, CH])
        vn = lay([2, P], CH)
        St = lay([2, P])
        osb = lay([NC_, P], CH)
        o1s = lay([2, P], CH)
        acc = lay([3, L])
        zs = lay([2, SEQ])
        thB = lay([SEQ])
        thA = lay([2, SEQ])
        pt = lay([2, L])
        ps2 = lay([2, L])
        pooled = lay([2, SEQ])
        poolw = sb("poolw", [P, 2, 2, 2 * P])
        merged = sb("merged", [P, KT, SEQ])
        hres = sb("hres", [P, TT, D])
        ident = sb("ident", [P, P])
        ones = sb("ones", [P, P])
        eps = sb("eps", [P, 1])
        prm = sb("prm", [P, P])
        prmT = sb("prmT", [P, ROWS])
        halfs = sb("halfs", [P, ROWS - ROW_POOL])
        mlow = take(CH, CH)
        mup = take((1 + NL) * CH, CH).rearrange("p (l t) -> p l t", l=1 + NL)
        uincl = sb("uincl", [CH, CH])
        negs = take(2 * CH, CH).rearrange("p (l t) -> p l t", l=2)
        small = sb("small", [P, 40, 24])
        wab = sb("wab", [P, KT, 16])
        abT = sb("abT", [16, LP])
        bc8 = sb("bc8", [CH, 3, 8])

        def plane(i, rows=CH, n=24):
            return small[0:rows, i, 0:n]

        def plane3(i, rows=CH):
            return small[0:rows, i, 0:24].rearrange("p (c h) -> p c h", c=NC_)

        X_, AX_, E_, LN_, RL_, SP_, G_, EB_, BETA_, NBETA_, GAM_, EGAM_, CD_, KD_, GL_, SKB_ = range(16)
        MS_, RS_, OSS_, ORS_ = 16, 17, 18, 20

        pb = [ctx.enter_context(nc.psum_tensor(f"bank{i}", [P, 512], F32)) for i in range(8)]
        full = [sem(f"bank_full{i}") for i in range(8)]
        free = [sem(f"bank_free{i}") for i in range(8)]
        win_land = [sem(f"win_land{i}") for i in range(WIN_SLOTS)]

        desk_at[0] = 0
        xgT = lay([ROOMS, KT, 2 * SLOTS])
        sgate = lay([FF // 2])
        hmid = lay([FF // 2])
        hT = lay([2, P])
        hot = lay([TT, 2, SLOTS])
        hotw = lay([TT, 2, SLOTS])
        give = lay([TT * P])
        plan = lay([EXPERTS, 2 * TT])
        cols = lay([ROOMS, 2, 2 * TT])
        rt = lay([TT, 18, 32])
        x2T = merged
        routw = poolw[:].rearrange("p a b c -> p (a b c)")[:, 0:KT * 36].rearrange("p (k n) -> p k n", k=KT)
        rbias = sb("rbias", [P, 36])
        rs = sb("rs", [P, TT, 24])
        ru = sb("ru", [P, TT, 16], U32)
        iota_e = sb("iota_e", [P, EXPERTS])
        iota_g = sb("iota_g", [P, EXPERTS])
        iota_c = sb("iota_c", [P, SLOTS])
        before = sb("before", [P, P])
        most = sb("most", [P, 8])
        mosti = sb("mosti", [P, 1], I32)

        wfin = merged[:].rearrange("p k t -> p (k t)")[:, 0:D]

        ysb = merged[:].rearrange("p k t -> p (k t)")[:, D:2 * D].rearrange("p (g d) -> p g d", g=2)

        w_in_v = w_in[0].rearrange("(k p) n -> p k n", p=P)
        gate_v = expert_w_gate[0].rearrange("g e (k p) f -> (g e) p k f", p=P)
        up_v = expert_w_up[0].rearrange("g e (k p) f -> (g e) p k f", p=P)
        down_v = expert_w_down[0].rearrange("g e (k p) d -> (g e) p k d", p=P)

        def filled(eng, key):
            b, n = WHERE[key]
            eng.wait_ge(full[b], n + 1)
            return pb[b]

        def taken(eng, key):
            b, n = WHERE[key]
            eng.wait_ge(free[b], n + 1)

        def fills(ins, key):
            ins.then_inc(full[WHERE[key][0]], 1)

        def takes(ins, key):
            ins.then_inc(free[WHERE[key][0]], 1)

        def bank(pe, key):
            b, n = WHERE[key]
            if n >= 1:
                pe.wait_ge(free[b], n)
            return pb[b]

        LIST = {"k": 0, "q": 1, "v": 2}

        def overflow(eng, one_pass):
            eng.wait_ge(S("most"), 1)
            count = eng.value_load(mosti[0:1, 0:1], min_val=0, max_val=SEQ)
            opened = []
            for ps in range(1, PASSES):
                c = eng.If(count > ps * SLOTS)
                c.__enter__()
                opened.append(c)
                one_pass(ps)
            for c in reversed(opened):
                c.__exit__(None, None, None)

        block = ctx.enter_context(nc.Block())

        @block.sync
        def _(sp):
            sp.dma_start(prm[ROW_CONV:ROW_CONV + 96, :], conv_w[0].rearrange("j (c p) -> (j c) p", p=P)).then_inc(S("params_land"), 16)
            for row, a in ((ROW_MIX, norm_mix_w), (ROW_FFN, norm_ffn_w), (ROW_POOL, pool_scale), (ROW_DN, dn_norm_w)):
                n = a.shape[1] // P
                sp.dma_start(prm[row:row + n, :], a[0].rearrange("(c p) -> c p", p=P)).then_inc(S("params_land"), 16)
            sp.dma_start(wab[:, :, :], w_in_v[:, :, COL_AB:COL_AB + 16]).then_inc(S("params_land"), 16)
            for i, a in ((0, a_log), (1, dt_bias)):
                sp.dma_start(bc8[:, i, :], a[0:1, :].partition_broadcast(CH) if False else a[0:1, :].to_broadcast([CH, 8])).then_inc(S("params_land"), 16)

            def load_tile(n):
                t, j = TILES[n]
                if n >= WIN_SLOTS:
                    filled(sp, ("proj", n - WIN_SLOTS))
                c = COL[t] + j * P
                sp.dma_start(win[:, n % WIN_SLOTS], w_in_v[:, :, c:c + P]).then_inc(win_land[n % WIN_SLOTS], 16)
                if t == "P" and j % 2 == 0:
                    g = j // 2
                    if g >= 2:
                        filled(sp, ("m1", 2 * g - 3))
                    sp.dma_start(poolw[:, g % 2], pool_w[0, g].rearrange("(a p) c -> p a c", p=P)).then_inc(S(f"poolw_land{g % 2}"), 16)

            for n in range(WIN_SLOTS):
                load_tile(n)
            for c in range(3):
                sp.dma_start(ring[:, c, :].rearrange("p (k f) -> p k f", k=KT if c < 2 else 4),
                             (gate_v, up_v, down_v)[c][0]).then_inc(S(f"w_land{c}"), 16)
            for n in range(WIN_SLOTS, len(TILES)):
                load_tile(n)
            for k in range(KT):
                n = len(TILES) + k
                if k < WIN_SLOTS:
                    filled(sp, ("proj", n - WIN_SLOTS))
                else:
                    sp.wait_ge(S("wout_used"), k - WIN_SLOTS + 1)
                sp.dma_start(wout[:, n % WIN_SLOTS, :], w_out[0, k * P:(k + 1) * P, :]).then_inc(win_land[n % WIN_SLOTS], 16)
            filled(sp, ("m1", HEADS - 1))
            sp.dma_start(routw[:, :, 0:GROUPS], router_group_w[0].rearrange("(k p) n -> p k n", p=P)).then_inc(S("rout_land"), 16)
            sp.dma_start(routw[:, :, GROUPS:36], router_expert_w[0].rearrange("(k p) n -> p k n", p=P)).then_inc(S("rout_land"), 16)
            sp.dma_start(rbias[:, 0:GROUPS], router_group_b[0:1, :].to_broadcast([P, GROUPS])).then_inc(S("rout_land"), 16)
            sp.dma_start(rbias[:, GROUPS:36], router_expert_b[0:1, :].to_broadcast([P, EXPERTS])).then_inc(S("rout_land"), 16)
            sp.wait_ge(S("outproj"), 1)

            def load_expert(e, slot, through):
                for c, (v, used) in enumerate(((gate_v, "gate"), (up_v, "up"), (down_v, "y"))):
                    if through is not None:
                        sp.wait_ge(S(used), through)
                    src = v[e] if isinstance(e, int) else v[bass.ds(e, 1)].rearrange("a p k f -> (a p) k f")
                    sp.dma_start(ring[:, 3 * slot + c, :].rearrange("p (k f) -> p k f", k=KT if c < 2 else 4),
                                 src).then_inc(S(f"w_land{3 * slot + c}"), 16)

            def one_pass(ps):
                base = EXPERTS * ps
                for e in range(RINGS):
                    if ps or e:
                        load_expert(e, e, base if ps else None)
                with sp.Fori(1, EXPERTS // RINGS) as i:
                    for j in range(RINGS):
                        load_expert(i * RINGS + j, j, i * RINGS + (base + j - RINGS + 1))
                for e in range(EXPERTS // RINGS * RINGS, EXPERTS):
                    load_expert(e, e % RINGS, base + e - RINGS + 1)

            one_pass(0)
            sp.wait_ge(S("logits"), TT)
            sp.dma_start(wfin[:], norm_final_w[None, :].to_broadcast([P, D])).then_inc(S("wf_land"), 16)
            overflow(sp, one_pass)
            for i in range(TT):
                sp.wait_ge(S("final"), i + 1)
                sp.dma_start(out[0, i * P:(i + 1) * P, :], xn[:, i, :]).then_inc(S("stored"), 16)
            sp.wait_ge(S("stored"), TT * 16)

        @block.scalar
        def _(act):
            for i in range(TT):
                act.dma_start(hres[:, i, :], x[0, i * P:(i + 1) * P, :]).then_inc(S(f"x_land{i}"), 16)
            act.dma_start(hn[0:META, 2, :], meta_tokens).then_inc(S("meta_land"), 16)
            act.wait_ge(S("meta_land"), 16)
            junk = merged[:].rearrange("p k t -> p (k t)")[:, 0:D]
            for i in range(3):
                rows = META if i == 2 else P
                if i < 2:
                    act.wait_ge(S(f"x_land{i}"), 16)
                if i:
                    act.wait_ge(S("ms"), i)
                nc.scalar.activation(junk[0:rows], hn[0:META, 2, :] if i == 2 else hres[:, i, :], ACT.Square,
                                     scale=1.0 / 32.0, accum_out=small[0:rows, MS_, i:i + 1]).then_inc(S("ms"), 1)
            act.wait_ge(S("ms"), 3)
            act.wait_ge(S("consts"), CONSTS["eps"])
            nc.scalar.activation(small[:, MS_, 4:6], small[:, MS_, 0:2], ACT.Sqrt, bias=eps[:]).then_inc(S("rms"), 1)
            nc.scalar.activation(small[0:META, MS_, 6:7], small[0:META, MS_, 2:3], ACT.Sqrt, bias=eps[0:META]).then_inc(S("rms"), 1)
            act.wait_ge(S("prmT"), 1)
            for k in range(1, KT, 2):
                act.wait_ge(S("turned"), k + 1)
                nc.scalar.activation(uT[:, k, :], pb[k % 4][:, 0:L], ACT.Copy, scale=prmT[:, ROW_MIX + k:ROW_MIX + k + 1]).then_inc(S("uT"), 1)
            act.wait_ge(S("ab"), 1)
            act.wait_ge(S("consts"), CONSTS["abz"])
            nc.scalar.activation(abT[:, PAD:LP], pb[4][0:16, 0:L], ACT.Copy).then_inc(S("abT"), 1)
            act.wait_ge(S("xa"), 1)
            nc.scalar.activation(plane(AX_), plane(X_), ACT.Abs).then_inc(S("a_chain"), 1)
            act.wait_ge(S("a_chain"), 1)
            nc.scalar.activation(plane(E_), plane(AX_), ACT.Exp, scale=-1.0).then_inc(S("a_chain"), 1)
            act.wait_ge(S("a_chain"), 2)
            nc.scalar.activation(plane(LN_), plane(E_), ACT.Ln, bias=1.0).then_inc(S("lnp"), 1)
            nc.scalar.activation(plane3(EB_), pb[5][0:CH, 0:48].rearrange("p (c n) -> p c n", c=3)[:, :, 8:16], ACT.Exp, scale=-1.0).then_inc(S("eb"), 1)
            act.wait_ge(S("params_land"), 8 * 16)
            nc.scalar.activation(bc8[:, 2, :], bc8[:, 0, :], ACT.Exp).then_inc(S("ea"), 1)
            act.wait_ge(S("kdarg"), 1)
            nc.scalar.activation(plane(EGAM_), plane(GAM_), ACT.Exp).then_inc(S("egam"), 1)
            nc.scalar.activation(plane(CD_, P), pb[6][:, 32:56], ACT.Exp).then_inc(S("egam"), 1)
            nc.scalar.activation(plane(KD_), plane(GL_), ACT.Exp).then_inc(S("egam"), 1)
            for h in range(HEADS):
                act.wait_ge(S("darg"), 2 * h + 1)
                nc.scalar.activation(Dm[:, h], Dm[:, h], ACT.Exp).then_inc(S("Dexp"), 1)
                act.wait_ge(S("darg"), 2 * h + 2)
                nc.scalar.activation(DT[:, h], DT[:, h], ACT.Exp).then_inc(S("DTexp"), 1)

            def take_tile(n, t, j):
                p = filled(act, ("proj", n))
                if t in "kqv":
                    i = LIST[t]
                    col = {"q": 0, "k": 8, "v": 16}[t] + j
                    w3 = prmT[:, 3 * 24 + col:3 * 24 + col + 1]
                    if j >= 1:
                        act.wait_ge(S("silu"), 3 * j)
                    nc.scalar.activation(acc[:, i, :], p[:, 0:L], ACT.Copy, scale=w3).then_inc(S("tap3"), 1)
                elif t == "z":
                    if j >= 2:
                        taken(act, ("oT", j - 2))
                    takes(nc.scalar.activation(zs[:, j % 2, :], p[:, 0:SEQ], ACT.Silu), ("proj", n))
                elif t == "gB":
                    if j >= 1:
                        act.wait_ge(S("zg"), j)
                    takes(nc.scalar.activation(thB[:, :], p[:, 0:SEQ], ACT.Tanh, scale=0.5), ("proj", n))
                elif t == "gA":
                    if j >= 2:
                        act.wait_ge(S("mixed"), j // 2 * 2)
                    takes(nc.scalar.activation(thA[:, j % 2, :], p[:, 0:SEQ], ACT.Tanh, scale=0.5), ("proj", n))
                else:
                    if j >= 2:
                        act.wait_ge(S("pooled"), j // 2 * 2)
                    takes(nc.scalar.activation(pt[:, j % 2, :], p[:, 0:L], ACT.Copy), ("proj", n))

            def copy(dst, key, n, rows=CH, **kw):
                p = filled(act, key)
                takes(nc.scalar.activation(dst, p[0:rows, 0:NC_ * n].rearrange("p (c t) -> p c t", c=NC_), ACT.Copy, **kw), key)

            for step in ORDER:
                kind = step[0]
                if kind == "take":
                    take_tile(*step[1:])
                if kind == "silu":
                    t, h = step[1:]
                    i = LIST[t]
                    act.wait_ge(S("conv"), 3 * h + i + 1)
                    if h >= KQV:
                        filled(act, ("os", h - KQV, 2))
                    else:
                        act.wait_ge(S("consts"), CONSTS["kqv_zero"])
                    nc.scalar.activation(kqv[:, h % KQV, i, PAD:LP], acc[:, i, :], ACT.Silu).then_inc(S("silu"), 1)
                if kind == "norm":
                    h = step[1]
                    act.wait_ge(S("silu"), 3 * h + 2)
                    if h >= 1:
                        filled(act, ("nq", h - 1))
                    for i in range(2):
                        nc.scalar.activation(sq[:, i, :], kqv[:, h % KQV, i, :], ACT.Square).then_inc(S("sq"), 1)
                    if h >= 1:
                        act.wait_ge(S("kn"), 2 * h)
                    for i, name in enumerate(("nk", "nq")):
                        p = filled(act, (name, h))
                        takes(nc.scalar.activation(rn[:, i, :], p[:, 0:LP], ACT.Sqrt, bias=eps[:]), (name, h))
                if kind == "turn":
                    h = step[1]
                    if h >= 2:
                        act.wait_ge(S("OT"), OT_AT[(h - 2, NL - 1)])
                        act.wait_ge(S("base"), 2 * (h - 1))
                    copy(ATb[:, h % 2], ("AT", h), CH)
                if kind == "lx":
                    h, lv = step[1:]
                    if lv:
                        filled(act, ("YT", h, lv - 1))
                    elif h >= 2:
                        filled(act, ("YT", h - 2, NL - 1))
                    copy(Xb[:, h % 2], ("X", h, lv), CH)
                if kind == "solve":
                    h = step[1]
                    if h >= 2:
                        filled(act, ("os", h - 2, 2))
                        taken(act, ("ws", h - 2, 2))
                    copy(ub[:, h % 2], ("u", h), P)
                    copy(wT[:, h % 2], ("wT", h), CH, rows=P)
                if kind == "sa":
                    h, c = step[1:]
                    p = filled(act, ("o1", h, c))
                    if h >= 1:
                        taken(act, ("os", h - 1, c))
                    takes(nc.scalar.activation(o1s[:, c - 1, :], p[0:CH, 0:P], ACT.Copy,
                                               scale=small[0:CH, EGAM_, c * 8 + h:c * 8 + h + 1]), ("o1", h, c))
                if kind == "onorm":
                    h = step[1]
                    taken(act, ("os", h, 2))
                    for c in range(NC_):
                        if h or c:
                            act.wait_ge(S("oss"), 3 * h + c)
                        if h:
                            act.wait_ge(S("ors"), h)
                        nc.scalar.activation(o1s[:, 0, :], osb[:, c, :], ACT.Square, scale=float(P) ** -0.5,
                                             accum_out=small[0:CH, OSS_, c:c + 1]).then_inc(S("oss"), 1)
                    act.wait_ge(S("oss"), 3 * h + 3)
                    nc.scalar.activation(small[0:CH, ORS_, 4:7], small[0:CH, OSS_, 0:3], ACT.Sqrt, bias=eps[0:CH]).then_inc(S("orms"), 1)

            junk2 = late[:, 0:D]
            for i in range(TT):
                act.wait_ge(S("res"), 2 * (i + 1))
                if i:
                    act.wait_ge(S("ms"), 3 + i)
                nc.scalar.activation(junk2, hres[:, i, :], ACT.Square, scale=1.0 / 32.0,
                                     accum_out=rs[:, i, 0:1]).then_inc(S("ms"), 1)
            for i in range(TT):
                act.wait_ge(S("ms"), 3 + TT)
                nc.scalar.activation(rs[:, i, 22:23], rs[:, i, 0:1], ACT.Sqrt, bias=eps[:]).then_inc(S("rms"), 1)
            for k in range(1, KT, 2):
                act.wait_ge(S("turned"), KT + k + 1)
                nc.scalar.activation(x2T[:, k, :], pb[k % 4][:, 0:SEQ], ACT.Copy, scale=prmT[:, ROW_FFN + k:ROW_FFN + k + 1]).then_inc(S("uT"), 1)
            for i in range(TT):
                act.wait_ge(S("rexp_in"), i + 1)
                nc.scalar.activation(rs[:, i, 8:12], rt[:, i, 0, 0:GROUPS], ACT.Exp, bias=rs[:, i, 2:3],
                                     accum_out=rs[:, i, 3:4]).then_inc(S("rexp"), 1)
                nc.scalar.activation(rs[:, i, 4:5], rs[:, i, 5:6], ACT.Exp).then_inc(S("rexp"), 1)

            def one_pass(ps):
                base = EXPERTS * ps

                def one(e, pair, g, first):
                    n = e + base
                    act.wait_ge(S("gate"), n + 1)
                    if not first:
                        act.wait_ge(S("hmid"), n)
                    nc.scalar.activation(sgate[:], pb[1][:, 0:FF // 2], ACT.Silu).then_inc(S("sgate"), 1)
                    act.wait_ge(S("hTp"), n + 1)
                    if not first:
                        act.wait_ge(S("y"), n)
                    nc.scalar.activation(hT[:].rearrange("p a b -> p (a b)"), pb[1][:, FF // 2:FF], ACT.Copy).then_inc(S("hT"), 1)
                    act.wait_ge(S("y"), n + 1)
                    if g == 0 and not first:
                        act.wait_ge(S("given"), pair + PAIRS * ps)
                    for half in range(2):
                        nc.scalar.activation(ysb[g * SLOTS:(g + 1) * SLOTS, half, :], pb[3][half * 64:half * 64 + SLOTS, :], ACT.Copy).then_inc(S("ysb"), 1)

                for g in range(2):
                    one(g, 0, g, ps == 0 and g == 0)
                with act.Fori(1, PAIRS) as i:
                    for g in range(2):
                        one(i * 2 + g, i, g, False)

            one_pass(0)
            overflow(act, one_pass)
            for i in range(TT):
                act.wait_ge(S("fin_h"), i + 1)
                if i:
                    act.wait_ge(S("ms"), 3 + TT + i)
                nc.scalar.activation(ring[:, 6, 0:D], hres[:, i, :], ACT.Square, scale=1.0 / 32.0,
                                     accum_out=rs[:, i, 12:13]).then_inc(S("ms"), 1)
            for i in range(TT):
                act.wait_ge(S("ms"), 3 + TT + i + 1)
                nc.scalar.activation(rs[:, i, 23:24], rs[:, i, 12:13], ACT.Sqrt, bias=eps[:]).then_inc(S("rms"), 1)

        @block.gpsimd
        def _(pool):
            done = [0]

            def chain(ins):
                done[0] += 1
                ins.then_inc(S("pool_chain"), 1)
                pool.wait_ge(S("pool_chain"), done[0])

            chain(nc.gpsimd.memset(ident[:], 0.0))
            chain(nc.gpsimd.affine_select(out=ident[:], in_=ident[:], compare_op=ALU.not_equal, fill=1.0, base=0,
                                          pattern=[[-1, P]], channel_multiplier=1))
            pool.sem_inc(S("consts"), 1)
            nc.gpsimd.memset(ones[:], 1.0).then_inc(S("consts"), 1)
            nc.gpsimd.memset(eps[:], EPS).then_inc(S("consts"), 1)
            nc.gpsimd.memset(abT[:, 0:PAD], 0.0).then_inc(S("consts"), 1)
            chain(nc.gpsimd.memset(uincl[:], 1.0))
            chain(nc.gpsimd.affine_select(out=uincl[:], in_=uincl[:], compare_op=ALU.is_ge, fill=0.0, base=0,
                                          pattern=[[1, CH]], channel_multiplier=-1))
            chain(nc.gpsimd.memset(negs[:], 0.0))
            chain(nc.gpsimd.affine_select(out=negs[:, 0, :], in_=negs[:, 0, :], compare_op=ALU.is_gt, fill=NEG, base=0,
                                          pattern=[[-1, CH]], channel_multiplier=1))
            chain(nc.gpsimd.affine_select(out=negs[:, 1, :], in_=negs[:, 1, :], compare_op=ALU.is_ge, fill=NEG, base=0,
                                          pattern=[[1, CH]], channel_multiplier=-1))
            pool.sem_inc(S("consts"), 1)
            chain(nc.gpsimd.memset(mlow[:], 0.0))
            v = mlow[:].rearrange("p (a r) -> p a r", r=2)[:, :, 0]
            chain(nc.gpsimd.affine_select(out=v, in_=v, compare_op=ALU.not_equal, fill=1.0, base=-1,
                                          pattern=[[-2, CH // 2]], channel_multiplier=1))
            chain(nc.gpsimd.memset(mup[:], 0.0))
            for lv, b in enumerate([1] + LEVELS):
                if 2 * b <= CH and CH % (2 * b) == 0:
                    v = mup[:, lv, :].rearrange("p (a r) -> p a r", r=2 * b)[:, :, b:2 * b]
                    na, nb = CH // (2 * b), b
                elif b == 32:
                    v, na, nb = mup[:, lv, 32:64].rearrange("p (a r) -> p a r", a=1), 1, 32
                else:
                    v, na, nb = mup[:, lv, b:CH].rearrange("p (a r) -> p a r", a=1), 1, CH - b
                chain(nc.gpsimd.memset(v, 1.0))
                chain(nc.gpsimd.affine_select(out=v, in_=v, compare_op=ALU.is_ge, fill=0.0, base=0,
                                              pattern=[[-2 * b, na], [0, nb]], channel_multiplier=1))
                chain(nc.gpsimd.affine_select(out=v, in_=v, compare_op=ALU.is_ge, fill=0.0, base=b - 1,
                                              pattern=[[2 * b, na], [0, nb]], channel_multiplier=-1))
            pool.sem_inc(S("consts"), 1)
            for b in range(KQV):
                nc.gpsimd.memset(kqv[:, b, :, 0:PAD], 0.0).then_inc(S("pool_chain"), 1)
                done[0] += 1
            pool.wait_ge(S("pool_chain"), done[0])
            pool.sem_inc(S("consts"), 1)
            for h in range(HEADS):
                pool.wait_ge(S("Dexp"), h + 1)
                pool.wait_ge(S("beta"), 1)
                nc.gpsimd.tensor_tensor(Dm[:, h], Dm[:, h],
                                        plane3(NBETA_)[:, :, h:h + 1].to_broadcast([CH, NC_, CH]), ALU.mult).then_inc(S("Dm"), 1)

            def mask_blocks(h, lv):
                nc.gpsimd.tensor_tensor(OTb[:, h % 2, lv % 2], ATb[:, h % 2], mup[:, 1 + lv:2 + lv, :].to_broadcast([CH, NC_, CH]), ALU.mult).then_inc(S("OT"), 1)

            pools = [0]

            def window(j):
                g = j // 2
                b = j % 2
                src = pt[:, b, :]
                taken(pool, ("proj", TILE_OF[("P", j)]))
                lo = 0
                a, n = src, 0
                for s in range(g + 1):
                    w = 1 << s
                    dst = ps2[:, s % 2, :]
                    lo += w
                    pools[0] += 1
                    nc.gpsimd.tensor_tensor(dst[:, lo:L], a[:, lo:L], a[:, lo - w:L - w], ALU.add).then_inc(S("win_chain"), 1)
                    pool.wait_ge(S("win_chain"), pools[0])
                    a = dst
                pools[0] += 1
                nc.gpsimd.tensor_scalar(ps2[:, (g + 1) % 2, META:L], a[:, META:L], 1.0 / (2 << g), None, ALU.mult).then_inc(S("win_chain"), 1)
                pool.wait_ge(S("win_chain"), pools[0])
                if j >= 2:
                    filled(pool, ("m1", j // 2 * 2 - 1))
                nc.gpsimd.tensor_tensor(pooled[:, b, :], ps2[:, (g + 1) % 2, META:L], src[:, META:L], ALU.subtract).then_inc(S("pooled"), 1)
                pool.wait_ge(S("pooled"), j + 1)

            for step in ORDER:
                if step[0] == "take" and step[2] == "P":
                    window(step[3])
                if step[0] == "turn":
                    h = step[1]
                    taken(pool, ("AT", h))
                    for lv in range(2):
                        if h >= 2:
                            filled(pool, ("X", h - 2, NL - 2 + lv))
                        mask_blocks(h, lv)
                if step[0] == "ly" and step[2] + 2 < NL:
                    h, lv = step[1:]
                    filled(pool, ("X", h, lv))
                    mask_blocks(h, lv + 2)

            chain(nc.gpsimd.iota(iota_e[:], pattern=[[1, EXPERTS]], base=0, channel_multiplier=0, allow_small_or_imprecise_dtypes=True))
            chain(nc.gpsimd.iota(iota_g[:], pattern=[[1, GROUPS], [0, PER_GROUP]], base=0, channel_multiplier=0, allow_small_or_imprecise_dtypes=True))
            chain(nc.gpsimd.iota(iota_c[:], pattern=[[1, SLOTS]], base=0, channel_multiplier=0, allow_small_or_imprecise_dtypes=True))
            chain(nc.gpsimd.memset(before[:], 1.0))
            chain(nc.gpsimd.affine_select(out=before[:], in_=before[:], compare_op=ALU.is_gt, fill=0.0, base=0,
                                          pattern=[[1, P]], channel_multiplier=-1))
            pool.sem_inc(S("rconst"), 1)
            pairs = plan[:].rearrange("p (i g) n -> p i (g n)", g=2)

            def one_pass(ps):
                pool.wait_ge(S("plan"), ps + 1)

                def column(i, k, first):
                    if not first:
                        pool.wait_ge(S("hotw"), i + (PAIRS * ps - ROOMS + 1))
                    nc.gpsimd.tensor_copy(cols[:, k].rearrange("p a b -> p (a b)"), pairs[:, bass.ds(i, 1), :].rearrange("p a b -> p (a b)")).then_inc(S("col"), 1)

                for i in range(ROOMS):
                    column(i, i, ps == 0)
                with pool.Fori(1, PAIRS // ROOMS) as i:
                    for j in range(ROOMS):
                        column(i * ROOMS + j, j, False)
                for i in range(PAIRS // ROOMS * ROOMS, PAIRS):
                    column(i, i % ROOMS, False)

            one_pass(0)
            overflow(pool, one_pass)

        @block.vector
        def _(dve):
            V = nc.vector
            counts = {"dve_chain": 0, "dve_chain_over": 0, "dve_chain_last": 0}
            which = ["dve_chain"]

            def chain(ins):
                counts[which[0]] += 1
                ins.then_inc(S(which[0]), 1)
                dve.wait_ge(S(which[0]), counts[which[0]])

            dve.wait_ge(S("rms"), 2)
            chain(V.reciprocal(small[:, RS_, 0:2], small[:, MS_, 4:6]))
            chain(V.reciprocal(small[0:META, RS_, 2:3], small[0:META, MS_, 6:7]))
            for i in range(3):
                rows = META if i == 2 else P
                src = hn[0:META, 2, :] if i == 2 else hres[:, i, :]
                V.tensor_scalar(hn[0:rows, i, :], src, small[0:rows, RS_, i:i + 1], None, ALU.mult).then_inc(S("hn"), 1)
            dve.wait_ge(S("prmp"), 1)
            V.tensor_copy(prmT[:], pb[7][:, 0:ROWS]).then_inc(S("prmT"), 1)
            dve.wait_ge(S("prmT"), 1)
            chain(V.tensor_scalar(halfs[:], prmT[:, ROW_POOL:ROWS], 0.5, None, ALU.mult))
            for k in range(0, KT, 2):
                dve.wait_ge(S("turned"), k + 1)
                V.tensor_scalar(uT[:, k, :], pb[k % 4][:, 0:L], prmT[:, ROW_MIX + k:ROW_MIX + k + 1], None, ALU.mult).then_inc(S("uTd"), 1)
            dve.wait_ge(S("abt"), 1)
            dve.wait_ge(S("params_land"), 8 * 16)
            abp = pb[5][0:CH, 0:48].rearrange("p (c n) -> p c n", c=3)
            V.tensor_tensor(plane3(X_), abp[:, :, 0:8], bc8[:, 1:2, :].to_broadcast([CH, 3, 8]), ALU.add).then_inc(S("xa"), 1)
            dve.wait_ge(S("xa"), 1)
            chain(V.tensor_scalar(plane(RL_), plane(X_), 0.0, None, ALU.max))
            dve.wait_ge(S("lnp"), 1)
            chain(V.tensor_tensor(plane(SP_), plane(RL_), plane(LN_), ALU.add))
            dve.wait_ge(S("ea"), 1)
            V.scalar_tensor_tensor(plane3(G_), plane3(SP_), -1.0, bc8[:, 2:3, :].to_broadcast([CH, 3, 8]), ALU.mult, ALU.mult).then_inc(S("g"), 1)
            dve.wait_ge(S("eb"), 1)
            chain(V.tensor_scalar(plane(BETA_), plane(EB_), 1.0, None, ALU.add))
            chain(V.reciprocal(plane(BETA_), plane(BETA_)))
            V.tensor_scalar(plane(NBETA_), plane(BETA_), -1.0, None, ALU.mult).then_inc(S("beta"), 1)
            dve.wait_ge(S("gamp"), 1)
            chain(V.tensor_copy(plane(GAM_), pb[6][0:CH, 0:24]))
            V.tensor_tensor(plane(GL_), pb[6][0:CH, 32:56], plane(GAM_), ALU.subtract).then_inc(S("kdarg"), 1)
            dve.wait_ge(S("egam"), 1)
            chain(V.tensor_tensor(plane(SKB_), plane(BETA_), plane(EGAM_), ALU.mult))
            dve.wait_ge(S("consts"), CONSTS["masks"])
            dve.wait_ge(S("turned"), KT)
            for h in range(HEADS):
                dve.wait_ge(S("gamB"), h + 1)
                chain(V.tensor_tensor(tmpT[:, h % 2], pb[h % 4][0:CH, 0:LP].rearrange("p (c t) -> p c t", c=3),
                                      plane3(GAM_)[:, :, h:h + 1].to_broadcast([CH, 3, CH]), ALU.subtract))
                V.tensor_tensor(Dm[:, h], negs[:, 0:1, :].to_broadcast([CH, 3, CH]), tmpT[:, h % 2], ALU.subtract).then_inc(S("darg"), 1)
                V.tensor_tensor(DT[:, h], negs[:, 1:2, :].to_broadcast([CH, 3, CH]), tmpT[:, h % 2], ALU.add).then_inc(S("darg"), 1)
                dve.wait_ge(S("darg"), 2 * h + 2)
                dve.sem_inc(S("gamB_free"), 1)

            def c3(ap, n=CH):
                return ap.rearrange("p (c t) -> p c t", c=NC_)

            def per_token(i, h, n):
                return plane3(i)[:, :, h:h + 1].to_broadcast([CH, NC_, n])

            def spread(mask, n=CH):
                return mask.rearrange("p (o t) -> p o t", o=1).to_broadcast([CH, NC_, n])

            for step in ORDER:
                kind = step[0]
                if kind == "take":
                    n, t, j = step[1:]
                    if t in "kqv":
                        i = LIST[t]
                        p = pb[WHERE[("proj", n)][0]]
                        dve.wait_ge(S("tap3"), 3 * j + i + 1)
                        filled(dve, ("proj", n))
                        col = {"q": 0, "k": 8, "v": 16}[t] + j
                        for tap in (2, 1, 0):
                            sh = 3 - tap
                            ins = V.scalar_tensor_tensor(acc[:, i, sh:L], p[:, 0:L - sh], prmT[:, tap * 24 + col:tap * 24 + col + 1],
                                                         acc[:, i, sh:L], ALU.mult, ALU.add)
                            if tap:
                                chain(ins)
                            else:
                                ins.then_inc(S("conv"), 1)
                                dve.wait_ge(S("conv"), 3 * j + i + 1)
                                dve.sem_inc(free[WHERE[("proj", n)][0]], 1)
                    if t == "gB":
                        taken(dve, ("proj", n))
                        taken(dve, ("proj", TILE_OF[("z", j)]))
                        V.scalar_tensor_tensor(zs[:, j % 2, :], thB[:, :], 1.0, zs[:, j % 2, :], ALU.add, ALU.mult).then_inc(S("zg"), 1)
                if kind == "norm":
                    h = step[1]
                    for i, name in enumerate(("nk", "nq")):
                        taken(dve, (name, h))
                        chain(V.reciprocal(rn[:, i, :], rn[:, i, :]))
                        src = kqv[:, h % KQV, i, :]
                        V.scalar_tensor_tensor(src, src, 1.0 if i == 0 else float(P) ** -0.5, rn[:, i, :], ALU.mult, ALU.mult).then_inc(S("kn"), 1)
                if kind == "gram":
                    h = step[1]
                    dve.wait_ge(S("Dm"), h + 1)
                    p = filled(dve, ("G", h))
                    if h:
                        filled(dve, ("AT", h - 1))
                    takes(V.tensor_tensor(Ab[:], c3(p[0:CH, 0:LP]), Dm[:, h], ALU.mult), ("G", h))
                    taken(dve, ("G", h))
                    if h == 0:
                        dve.wait_ge(S("consts"), CONSTS["mups"])
                    chain(V.tensor_tensor(tmpT[:, 0], Ab[:], spread(mlow), ALU.mult))
                    if h >= 2:
                        filled(dve, ("X", h - 2, NL - 1))
                    V.tensor_tensor(Tb[:, h % 2], tmpT[:, 0], spread(ident[0:CH, 0:CH]), ALU.add).then_inc(S("base"), 1)
                    dve.wait_ge(S("DTexp"), h + 1)
                    p = filled(dve, ("QK", h))
                    takes(V.tensor_tensor(DT[:, h], c3(p[0:CH, 0:LP]), DT[:, h], ALU.mult), ("QK", h))
                    if h >= 2:
                        filled(dve, ("wT", h - 2))
                    p = filled(dve, ("KT", h))
                    chain(V.tensor_tensor(Kb[:, h % 2], c3(p[0:CH, 0:NC_ * P]), per_token(SKB_, h, P), ALU.mult))
                    if h == 0:
                        dve.wait_ge(S("egam"), 3)
                    if h >= 3:
                        filled(dve, ("os", h - 3, 1))
                    takes(V.tensor_tensor(Kd[:, h % 3], c3(p[0:CH, 0:NC_ * P]), per_token(KD_, h, P), ALU.mult), ("KT", h))
                    p = filled(dve, ("VT", h))
                    takes(V.tensor_tensor(Vb[:, h % 2], c3(p[0:CH, 0:NC_ * P]), per_token(BETA_, h, P), ALU.mult), ("VT", h))
                if kind == "turn":
                    h = step[1]
                    taken(dve, ("AT", h))
                    chain(V.tensor_tensor(tmpT[:, 1], ATb[:, h % 2], spread(mup[:, 0, :]), ALU.mult))
                    if h >= 2:
                        filled(dve, ("wT", h - 2))
                    V.tensor_tensor(Ub[:, h % 2], tmpT[:, 1], spread(ident[0:CH, 0:CH]), ALU.add).then_inc(S("base"), 1)
                if kind == "ly":
                    h, lv = step[1:]
                    q = filled(dve, ("YT", h, lv))
                    if lv < NL - 1:
                        p = pb[WHERE[("Y", h, lv)][0]]
                        takes(V.tensor_tensor(Tb[:, h % 2], c3(p[0:CH, 0:LP]), Tb[:, h % 2], ALU.add), ("Y", h, lv))
                    takes(V.tensor_tensor(Ub[:, h % 2], c3(q[0:CH, 0:LP]), Ub[:, h % 2], ALU.add), ("YT", h, lv))
                if kind in ("s0", "sb"):
                    h = step[1]
                    c = 0 if kind == "s0" else step[2]
                    key = ("os",) + ((h, 0) if kind == "s0" else (h, c))
                    p = filled(dve, key)
                    if h:
                        filled(dve, ("oT", h - 1))
                    if c == 0:
                        V.tensor_copy(osb[:, 0, :], p[0:CH, 0:P]).then_inc(S("o"), 1)
                        if h:
                            filled(dve, ("o1", h - 1, 2))
                        takes(V.tensor_copy(St[:, 0, :], p[:, P:2 * P]), key)
                    else:
                        taken(dve, ("o1", h, c))
                        ins = V.tensor_tensor(osb[:, c, :], p[0:CH, 0:P], o1s[:, c - 1, :], ALU.add)
                        if c == 1:
                            ins.then_inc(S("o"), 1)
                            if h:
                                filled(dve, ("o1", h - 1, 2))
                            takes(V.scalar_tensor_tensor(St[:, 1, :], St[:, 0, :], small[:, CD_, c * 8 + h:c * 8 + h + 1],
                                                         p[:, P:2 * P], ALU.mult, ALU.add), key)
                        else:
                            takes(ins, key)
                if kind == "sa":
                    h, c = step[1:]
                    p = filled(dve, ("ws", h, c))
                    if h:
                        filled(dve, ("os", h - 1, c))
                    takes(V.scalar_tensor_tensor(vn[:, c - 1, :], p[0:CH, 0:P], -1.0, ub[:, h % 2, c, :], ALU.mult, ALU.add), ("ws", h, c))
                if kind == "onorm":
                    h = step[1]
                    dve.wait_ge(S("orms"), h + 1)
                    chain(V.reciprocal(small[0:CH, ORS_, 0:3], small[0:CH, ORS_, 4:7]))
                    V.tensor_tensor(osb[:], osb[:], small[0:CH, ORS_, 0:3].rearrange("p (c o) -> p c o", o=1).to_broadcast([CH, 3, P]), ALU.mult).then_inc(S("ors"), 1)
                if kind == "out":
                    h = step[1]
                    p = filled(dve, ("oT", h))
                    dve.wait_ge(S("zg"), h + 1)
                    takes(V.scalar_tensor_tensor(merged[:, h, :], p[:, REAL:LP], halfs[:, 8:9], zs[:, h % 2, :], ALU.mult, ALU.mult), ("oT", h))
                if kind == "mix":
                    j = step[1]
                    for d in range(2):
                        ch = j - 1 + d
                        p = filled(dve, (f"m{d}", j))
                        taken(dve, ("proj", TILE_OF[("gA", ch)]))
                        takes(V.scalar_tensor_tensor(thA[:, d, :], thA[:, d, :], 1.0, p[:, 0:SEQ], ALU.add, ALU.mult), (f"m{d}", j))
                        taken(dve, (f"m{d}", j))
                        taken(dve, ("oT", ch))
                        V.scalar_tensor_tensor(merged[:, ch, :], thA[:, d, :], halfs[:, ch:ch + 1], merged[:, ch, :], ALU.mult, ALU.add).then_inc(S("mixed"), 1)

            for i in range(TT):
                for half in range(2):
                    dve.wait_ge(S("outproj"), 1)
                    o = hres[:, i, half * 512:(half + 1) * 512]
                    V.tensor_tensor(o, pb[2 * i + half][:], o, ALU.add).then_inc(S("res"), 1)
            for i in range(TT):
                dve.wait_ge(S("rms"), 2 + TT)
                chain(V.reciprocal(rs[:, i, 1:2], rs[:, i, 22:23]))
                V.tensor_scalar(xn[:, i, :], hres[:, i, :], rs[:, i, 1:2], None, ALU.mult).then_inc(S("xn"), 1)
            for k in range(0, KT, 2):
                dve.wait_ge(S("turned"), KT + k + 1)
                V.tensor_scalar(x2T[:, k, :], pb[k % 4][:, 0:SEQ], prmT[:, ROW_FFN + k:ROW_FFN + k + 1], None, ALU.mult).then_inc(S("uTd"), 1)
            dve.wait_ge(S("rconst"), 1)
            dve.wait_ge(S("rout_land"), 64)
            for i in range(TT):
                dve.wait_ge(S("logits"), i + 1)
                lg, le = rt[:, i, 0, 0:8], rt[:, i, 1, :]
                chain(V.memset(rt[:, i, 0, 0:8], NEG))
                chain(V.tensor_tensor(rt[:, i, 0, 0:GROUPS], pb[4 + i][:, 0:GROUPS], rbias[:, 0:GROUPS], ALU.add))
                chain(V.tensor_tensor(le, pb[4 + i][:, GROUPS:36], rbias[:, GROUPS:36], ALU.add))
                chain(V.max(rt[:, i, 2, 0:8], lg))
                chain(V.max_index(ru[:, i, 0:8], rt[:, i, 2, 0:8], lg))
                chain(V.tensor_copy(rs[:, i, 13:14], ru[:, i, 0:1]))
                chain(V.tensor_scalar(rt[:, i, 3, :], iota_g[:], rs[:, i, 13:14], 1.0, ALU.is_equal, ALU.subtract))
                chain(V.scalar_tensor_tensor(rt[:, i, 4, :], rt[:, i, 3, :], -NEG, le, ALU.mult, ALU.add))
                chain(V.max(rt[:, i, 5, 0:8], rt[:, i, 4, :]))
                chain(V.max_index(ru[:, i, 8:16], rt[:, i, 5, 0:8], rt[:, i, 4, :]))
                chain(V.tensor_copy(rs[:, i, 14:16], ru[:, i, 8:10]))
                for k in range(2):
                    chain(V.tensor_scalar(rt[:, i, 6 + k, :], iota_e[:], rs[:, i, 14 + k:15 + k], None, ALU.is_equal))
                V.tensor_tensor(rt[:, i, 8, :], rt[:, i, 6, :], rt[:, i, 7, :], ALU.add).then_inc(S("picked"), 1)
                chain(V.tensor_scalar(rs[:, i, 2:3], rt[:, i, 2, 0:1], -1.0, None, ALU.mult))
                V.tensor_tensor(rs[:, i, 5:6], rt[:, i, 5, 1:2], rt[:, i, 5, 0:1], ALU.subtract).then_inc(S("rexp_in"), 1)
            for i in range(TT):
                dve.wait_ge(S("rexp"), 2 * i + 2)
                chain(V.reciprocal(rs[:, i, 6:7], rs[:, i, 3:4]))
                chain(V.tensor_scalar(rs[:, i, 7:8], rs[:, i, 4:5], 1.0, None, ALU.add))
                chain(V.reciprocal(rs[:, i, 18:19], rs[:, i, 7:8]))
                chain(V.tensor_tensor(rs[:, i, 19:20], rs[:, i, 18:19], rs[:, i, 6:7], ALU.mult))
                chain(V.tensor_tensor(rs[:, i, 20:21], rs[:, i, 19:20], rs[:, i, 4:5], ALU.mult))
                chain(V.tensor_scalar(rt[:, i, 10, :], rt[:, i, 6, :], rs[:, i, 19:20], None, ALU.mult))
                chain(V.scalar_tensor_tensor(plan[:, :, TT + i], rt[:, i, 7, :], rs[:, i, 20:21], rt[:, i, 10, :], ALU.mult, ALU.add))
            dve.wait_ge(S("pos"), 3)
            for i in range(TT):
                chain(V.scalar_tensor_tensor(rt[:, i, 9, :], pb[6][:, 32 * i:32 * i + 32], 1.0, rt[:, i, 8, :], ALU.add, ALU.mult))
                chain(V.tensor_scalar(plan[:, :, i], rt[:, i, 9, :], -1.0, None, ALU.add))
            dve.sem_inc(S("plan"), 1)
            chain(V.max(most[:], pb[6][:, 64:96]))
            V.tensor_copy(mosti[:], most[:, 0:1]).then_inc(S("most"), 1)

            def one_pass(ps):
                base = PAIRS * ps
                if ps:
                    dve.wait_ge(S("col"), base)
                    for i in range(TT):
                        chain(V.tensor_scalar(plan[:, :, i], plan[:, :, i], -float(SLOTS), None, ALU.add))
                    dve.sem_inc(S("plan"), 1)

                def where(i, k, first):
                    n = i + base
                    dve.wait_ge(S("col"), n + 1)
                    if not first:
                        dve.wait_ge(S("gathered"), n * 2)
                    for t in range(TT):
                        for g in range(2):
                            ins = V.tensor_scalar(hot[:, t, g, :], iota_c[:], cols[:, k, g, t:t + 1], None, ALU.is_equal)
                    ins.then_inc(S("hot"), 1)

                def bring(i, k, part, first):
                    n = i + base
                    dve.wait_ge(S("gathered"), n * 2 + part + 1)
                    if not first:
                        dve.wait_ge(S("up"), n * 2 - 2 * (ROOMS - 1))
                    half = KT // 2
                    gains = prmT[:, ROW_FFN + half * part:ROW_FFN + half * (part + 1)].rearrange("p (k o) -> p k o", o=1)
                    V.tensor_tensor(xgT[:, k, half * part:half * (part + 1), :], pb[0][:].rearrange("p (k s) -> p k s", k=half),
                                    gains.to_broadcast([P, half, 2 * SLOTS]), ALU.mult).then_inc(S("xgT"), 1)

                def hidden(e, first):
                    dve.wait_ge(S("sgate"), e + 1)
                    dve.wait_ge(S("up"), e + 1)
                    if not first:
                        dve.wait_ge(S("hTp"), e)
                    V.tensor_tensor(hmid[:], pb[2][:, 0:FF // 2], sgate[:], ALU.mult).then_inc(S("hmid"), 1)

                def pair(i, k, first, last, fresh):
                    n = i + base
                    if not last:
                        where(i + 1, (k + 1) % ROOMS, False)
                    hidden(n * 2, first)
                    if not last:
                        bring(i + 1, (k + 1) % ROOMS, 0, fresh)
                    if not first:
                        dve.wait_ge(S("givep"), n)
                    for t in range(TT):
                        for g in range(2):
                            ins = V.tensor_scalar(hotw[:, t, g, :], iota_c[:], cols[:, k, g, t:t + 1], cols[:, k, g, TT + t:TT + t + 1], ALU.is_equal, ALU.mult)
                    ins.then_inc(S("hotw"), 1)
                    hidden(n * 2 + 1, False)
                    if not last:
                        bring(i + 1, (k + 1) % ROOMS, 1, fresh)
                    dve.wait_ge(S("givep"), n + 1)
                    if not first:
                        dve.wait_ge(S("given"), n)
                    V.tensor_copy(give[:], pb[2][:, FF // 2:FF // 2 + TT * P]).then_inc(S("give"), 1)

                where(0, 0, ps == 0)
                for part in range(2):
                    bring(0, 0, part, ps == 0)
                for i in range(ROOMS):
                    pair(i, i, ps == 0 and i == 0, False, ps == 0 and i + 1 < ROOMS)
                with dve.Fori(1, PAIRS // ROOMS) as i:
                    for j in range(ROOMS):
                        pair(i * ROOMS + j, j, False, False, False)
                for i in range(PAIRS // ROOMS * ROOMS, PAIRS):
                    pair(i, i % ROOMS, False, i == PAIRS - 1, False)

            one_pass(0)
            which[0] = "dve_chain_over"
            overflow(dve, one_pass)
            which[0] = "dve_chain_last"
            dve.wait_ge(S("experts_done"), 1)
            for i in range(TT):
                for half in range(2):
                    o = hres[:, i, half * 512:(half + 1) * 512]
                    ins = V.tensor_tensor(o, pb[4 + 2 * i + half][:], o, ALU.add)
                ins.then_inc(S("fin_h"), 1)
            for i in range(TT):
                dve.wait_ge(S("rms"), 2 + TT + i + 1)
                chain(V.reciprocal(rs[:, i, 21:22], rs[:, i, 23:24]))
                dve.wait_ge(S("wf_land"), 16)
                V.scalar_tensor_tensor(xn[:, i, :], hres[:, i, :], rs[:, i, 21:22], wfin[:], ALU.mult, ALU.mult).then_inc(S("final"), 1)

        @block.tensor
        def _(pe):
            T = nc.tensor
            pe.wait_ge(S("consts"), CONSTS["ident"])
            pe.wait_ge(S("params_land"), 8 * 16)
            T.transpose(pb[7][:, 0:ROWS], prm[0:ROWS, :], ident[0:ROWS, 0:ROWS]).then_inc(S("prmp"), 1)
            pe.wait_ge(S("hn"), 3)
            for k in range(KT):
                if k >= 4:
                    pe.wait_ge(S("uT" if k % 2 else "uTd"), (k - 4) // 2 + 1)
                for i, (c0, rows) in enumerate(((META, P), (META + P, P), (0, META))):
                    ins = T.transpose(pb[k % 4][:, c0:c0 + rows], hn[0:rows, i, k * P:(k + 1) * P], ident[0:rows, 0:rows])
                ins.then_inc(S("turned"), 1)
            pe.wait_ge(S("uT"), KT // 2)
            pe.wait_ge(S("uTd"), KT // 2)
            pe.wait_ge(S("params_land"), 8 * 16)
            for k in range(KT):
                ins = T.matmul(pb[4][0:16, 0:L], wab[:, k, :], uT[:, k, :], start=(k == 0), stop=(k == KT - 1))
            ins.then_inc(S("ab"), 1)
            pe.wait_ge(S("abT"), 1)
            for c in range(NC_):
                ins = T.transpose(pb[5][0:CH, 16 * c:16 * c + 16], abT[:, c * CH:(c + 1) * CH], ident[0:16, 0:16])
            ins.then_inc(S("abt"), 1)
            pe.wait_ge(S("g"), 1)
            pe.wait_ge(S("consts"), CONSTS["masks"])
            pe.wait_ge(S("consts"), CONSTS["ones"])
            T.matmul(pb[6][0:CH, 0:24], uincl[:], plane(G_), start=True, stop=True)
            T.matmul(pb[6][:, 32:56], ones[0:CH, :], plane(G_), start=True, stop=True).then_inc(S("gamp"), 1)
            for h in range(HEADS):
                if h >= 4:
                    pe.wait_ge(S("gamB_free"), h - 3)
                for c in range(NC_):
                    ins = T.matmul(pb[h % 4][0:CH, c * CH:(c + 1) * CH], small[0:CH, G_, c * 8 + h:c * 8 + h + 1].to_broadcast([CH, CH]),
                                   uincl[:], start=True, stop=True)
                ins.then_inc(S("gamB"), 1)
            pe.wait_ge(S("gamB_free"), HEADS)
            pe.wait_ge(S("prmT"), 1)
            pe.wait_ge(S("eb"), 1)
            pe.wait_ge(S("kdarg"), 1)
            pe.wait_ge(S("egam"), 2)

            def cs(ap, c, n):
                return ap[:, c * n:(c + 1) * n]

            def per_chunk(key, rows, width, product):
                p = bank(pe, key)
                for c in range(NC_):
                    ins = product(p[0:rows, c * width:(c + 1) * width], c)
                fills(ins, key)

            for step in ORDER:
                kind = step[0]
                if kind == "proj":
                    n, t, j, k = step[1:]
                    if k == 0:
                        pe.wait_ge(win_land[n % WIN_SLOTS], 16 * (n // WIN_SLOTS + 1))
                        bank(pe, ("proj", n))
                    p = pb[WHERE[("proj", n)][0]]
                    lo = 0 if t in "kqvP" else META
                    ins = T.matmul(p[:, 0:L - lo], win[:, n % WIN_SLOTS, k, :], uT[:, k, lo:L], start=(k == 0), stop=(k == KT - 1))
                    if k == KT - 1:
                        fills(ins, ("proj", n))
                if kind == "norm":
                    h = step[1]
                    for i, name in enumerate(("nk", "nq")):
                        p = bank(pe, (name, h))
                        pe.wait_ge(S("sq"), 2 * h + i + 1)
                        fills(T.matmul(p[:, 0:LP], ones[:], sq[:, i, :], start=True, stop=True), (name, h))
                if kind == "gram":
                    h = step[1]

                    def part(i, c):
                        return kqv[:, h % KQV, i, c * CH:(c + 1) * CH]

                    pe.wait_ge(S("kn"), 2 * h + 1)
                    per_chunk(("G", h), CH, CH, lambda o, c: T.matmul(o, part(0, c), part(0, c), start=True, stop=True))
                    pe.wait_ge(S("kn"), 2 * h + 2)
                    per_chunk(("QK", h), CH, CH, lambda o, c: T.matmul(o, part(0, c), part(1, c), start=True, stop=True))
                    per_chunk(("KT", h), CH, P, lambda o, c: T.transpose(o, part(0, c), ident[:]))
                    pe.wait_ge(S("silu"), 3 * h + 3)
                    per_chunk(("VT", h), CH, P, lambda o, c: T.transpose(o, part(2, c), ident[:]))
                if kind == "turn":
                    h = step[1]
                    taken(pe, ("G", h))
                    per_chunk(("AT", h), CH, CH, lambda o, c: T.transpose(o, Ab[:, c, :], ident[0:CH, 0:CH]))
                if kind == "lx":
                    h, lv = step[1:]
                    pe.wait_ge(S("OT"), OT_AT[(h, lv)])
                    if lv == 0:
                        pe.wait_ge(S("base"), 2 * h + 2)
                    else:
                        taken(pe, ("Y", h, lv - 1))
                        taken(pe, ("YT", h, lv - 1))
                    per_chunk(("X", h, lv), CH, CH, lambda o, c: T.matmul(o, OTb[:, h % 2, lv % 2, c, :], Tb[:, h % 2, c, :], start=True, stop=True))
                if kind == "ly":
                    h, lv = step[1:]
                    taken(pe, ("X", h, lv))
                    if lv < NL - 1:
                        per_chunk(("Y", h, lv), CH, CH, lambda o, c: T.matmul(o, Ub[:, h % 2, c, :], Xb[:, h % 2, c, :], start=True, stop=True))
                    per_chunk(("YT", h, lv), CH, CH, lambda o, c: T.matmul(o, Xb[:, h % 2, c, :], Ub[:, h % 2, c, :], start=True, stop=True))
                if kind == "solve":
                    h = step[1]
                    taken(pe, ("YT", h, NL - 1))
                    taken(pe, ("VT", h))
                    per_chunk(("u", h), CH, P, lambda o, c: T.matmul(o, Ub[:, h % 2, c, :], Vb[:, h % 2, c, :], start=True, stop=True))
                    taken(pe, ("KT", h))
                    per_chunk(("wT", h), P, CH, lambda o, c: T.matmul(o, Kb[:, h % 2, c, :], Ub[:, h % 2, c, :], start=True, stop=True))
                if kind in ("s0", "sb"):
                    h = step[1]
                    c = 0 if kind == "s0" else step[2]
                    if c == 0:
                        taken(pe, ("u", h))
                        taken(pe, ("QK", h))
                        new = ub[:, h % 2, 0, :]
                    else:
                        taken(pe, ("ws", h, c))
                        new = vn[:, c - 1, :]
                    p = bank(pe, ("os", h, c))
                    ins = T.matmul(p[0:CH, 0:P], DT[:, h, c, :], new, start=True, stop=True)
                    if c < NC_ - 1:
                        ins = T.matmul(p[:, P:2 * P], Kd[:, h % 3, c, :], new, start=True, stop=True)
                    fills(ins, ("os", h, c))
                if kind == "sa":
                    h, c = step[1:]
                    taken(pe, ("os", h, c - 1))
                    taken(pe, ("wT", h))
                    p = bank(pe, ("ws", h, c))
                    fills(T.matmul(p[0:CH, 0:P], wT[:, h % 2, c, :], St[:, c - 1, :], start=True, stop=True), ("ws", h, c))
                    p = bank(pe, ("o1", h, c))
                    fills(T.matmul(p[0:CH, 0:P], kqv[:, h % KQV, 1, c * CH:(c + 1) * CH], St[:, c - 1, :], start=True, stop=True), ("o1", h, c))
                if kind == "out":
                    h = step[1]
                    pe.wait_ge(S("ors"), h + 1)
                    per_chunk(("oT", h), P, CH, lambda o, c: T.transpose(o, osb[:, c, :], ident[0:CH, 0:CH]))
                if kind == "mix":
                    j = step[1]
                    g = j // 2
                    pe.wait_ge(S("pooled"), j + 1)
                    pe.wait_ge(S(f"poolw_land{g % 2}"), 16 * (g // 2 + 1))
                    for d in range(2):
                        p = bank(pe, (f"m{d}", j))
                        for a in range(2):
                            ins = T.matmul(p[:, 0:SEQ], poolw[:, g % 2, a, d * P:(d + 1) * P], pooled[:, a, :], start=(a == 0), stop=(a == 1))
                        fills(ins, (f"m{d}", j))

            for b in range(8):
                if USES[b]:
                    pe.wait_ge(free[b], USES[b])
            for k in range(KT):
                n = len(TILES) + k
                pe.wait_ge(S("mixed"), k + 1)
                pe.wait_ge(win_land[n % WIN_SLOTS], 16 * (n // WIN_SLOTS + 1))
                for i in range(TT):
                    for half in range(2):
                        ins = T.matmul(pb[2 * i + half][:], merged[:, k, i * P:(i + 1) * P],
                                       wout[:, n % WIN_SLOTS, half * 512:(half + 1) * 512], start=(k == 0), stop=(k == KT - 1))
                if k < KT - WIN_SLOTS:
                    ins.then_inc(S("wout_used"), 1)
            ins.then_inc(S("outproj"), 1)
            pe.wait_ge(S("res"), 4)
            for k in range(KT):
                if k >= 4:
                    pe.wait_ge(S("uT" if k % 2 else "uTd"), KT // 2 + (k - 4) // 2 + 1)
                for i in range(TT):
                    pe.wait_ge(S("xn"), i + 1)
                    ins = T.transpose(pb[k % 4][:, i * P:(i + 1) * P], xn[:, i, k * P:(k + 1) * P], ident[:])
                ins.then_inc(S("turned"), 1)
            pe.wait_ge(S("rout_land"), 64)
            for i in range(TT):
                for k in range(KT):
                    pe.wait_ge(S("uT" if k % 2 else "uTd"), KT // 2 + k // 2 + 1)
                    ins = T.matmul(pb[4 + i][:, 0:36], x2T[:, k, i * P:(i + 1) * P], routw[:, k, :], start=(k == 0), stop=(k == KT - 1))
                ins.then_inc(S("logits"), 1)
            pe.wait_ge(S("picked"), 1)
            T.matmul(pb[6][:, 0:32], before[:], rt[:, 0, 8, :], start=True, stop=True).then_inc(S("pos"), 1)
            pe.wait_ge(S("picked"), 2)
            T.matmul(pb[6][:, 32:64], ones[:], rt[:, 0, 8, :], start=True, stop=False)
            T.matmul(pb[6][:, 32:64], before[:], rt[:, 1, 8, :], start=False, stop=True).then_inc(S("pos"), 1)
            T.matmul(pb[6][:, 64:96], ones[:], rt[:, 0, 8, :], start=True, stop=False)
            T.matmul(pb[6][:, 64:96], ones[:], rt[:, 1, 8, :], start=False, stop=True).then_inc(S("pos"), 1)

            def one_pass(ps):
                base = EXPERTS * ps

                def gather(i, part, first):
                    n = i + PAIRS * ps
                    pe.wait_ge(S("hot"), n + 1)
                    if not first:
                        pe.wait_ge(S("xgT"), n * 2 + part)
                    for k in range(KT // 2):
                        ch = (part * KT // 2 + k) * P
                        for t in range(TT):
                            ins = T.matmul(pb[0][:, k * 2 * SLOTS:(k + 1) * 2 * SLOTS], xn[:, t, ch:ch + P], hot[:, t].rearrange("p g s -> p (g s)"),
                                           start=(t == 0), stop=(t == TT - 1))
                    ins.then_inc(S("gathered"), 1)

                def gate_up(i, room, g, k, landed, first):
                    n = i * 2 + (g + base)
                    pe.wait_ge(S("xgT"), (i + PAIRS * ps) * 2 + 2)
                    for c, name in ((0, "gate"), (1, "up")):
                        pe.wait_ge(S(f"w_land{3 * k + c}"), landed)
                        if not first:
                            pe.wait_ge(S("hmid"), n)
                            if c == 0:
                                pe.wait_ge(S("hT"), n)
                            elif g == 0:
                                pe.wait_ge(S("give"), i + PAIRS * ps)
                        w = ring[:, 3 * k + c, :].rearrange("p (k f) -> p k f", k=KT)
                        for kt in range(KT):
                            for half in range(2):
                                ins = T.matmul(pb[1 + c][half * 64:half * 64 + SLOTS, 0:256], xgT[:, room, kt, g * SLOTS:(g + 1) * SLOTS],
                                               w[:, kt, half * 256:(half + 1) * 256], start=(kt == 0), stop=(kt == KT - 1), skip_group_check=True)
                        ins.then_inc(S(name), 1)

                def spread(i, first):
                    n = i + PAIRS * ps
                    pe.wait_ge(S("ysb"), n * 4 + 4)
                    pe.wait_ge(S("give"), n + 1)
                    if first:
                        pe.wait_ge(S("most"), 1)
                    for t in range(TT):
                        for half in range(2):
                            ins = T.matmul(pb[4 + 2 * t + half][:], give[:, t * P:(t + 1) * P], ysb[:, half, :],
                                           start=first, stop=True, skip_group_check=True)
                    ins.then_inc(S("given"), 1)

                def down(i, g, k, landed, first):
                    n = i * 2 + (g + base)
                    pe.wait_ge(S("hmid"), n + 1)
                    for b in range(2):
                        ins = T.transpose(pb[1][:, FF // 2 + b * P:FF // 2 + (b + 1) * P], hmid[:, b * P:(b + 1) * P], ident[:])
                    ins.then_inc(S("hTp"), 1)
                    if g == 1:
                        pe.wait_ge(S("hotw"), i + (PAIRS * ps + 1))
                        for t in range(TT):
                            ins = T.transpose(pb[2][:, FF // 2 + t * P:FF // 2 + (t + 1) * P], hotw[:, t].rearrange("p g s -> p (g s)"), ident[:])
                        ins.then_inc(S("givep"), 1)
                    pe.wait_ge(S("hT"), n + 1)
                    pe.wait_ge(S(f"w_land{3 * k + 2}"), landed)
                    if not first:
                        pe.wait_ge(S("ysb"), n * 2)
                    w = ring[:, 3 * k + 2, :].rearrange("p (k d) -> p k d", k=4)
                    for f in range(4):
                        side, b = f // 2, f % 2
                        for half in range(2):
                            ins = T.matmul(pb[3][half * 64:half * 64 + SLOTS, :], hT[:, b, side * 64:side * 64 + SLOTS],
                                           w[:, f, half * 512:(half + 1) * 512], start=(f == 0), stop=(f == 3), skip_group_check=True)
                    ins.then_inc(S("y"), 1)

                used = [ps * uses(EXPERTS, k, RINGS) for k in range(RINGS)]

                def pair(i, turn, j, first, last):
                    for g in range(2):
                        k = (2 * j + g) % RINGS
                        landed = turn * (16 * 2 * ROOMS // RINGS) + 16 * (used[k] + (2 * j + g) // RINGS + 1)
                        gate_up(i, j, g, k, landed, first and g == 0 and ps == 0)
                        if g == 0 and not first:
                            spread(i - 1, isinstance(i, int) and i == 1 and ps == 0)
                        if not last:
                            gather(i + 1, g, False)
                        down(i, g, k, landed, first and g == 0 and ps == 0)

                for part in range(2):
                    gather(0, part, ps == 0 and part == 0)
                for i in range(ROOMS):
                    pair(i, 0, i, i == 0, False)
                with pe.Fori(1, PAIRS // ROOMS) as i:
                    for j in range(ROOMS):
                        pair(i * ROOMS + j, i, j, False, False)
                for i in range(PAIRS // ROOMS * ROOMS, PAIRS):
                    pair(i, i // ROOMS, i % ROOMS, False, i == PAIRS - 1)
                spread(PAIRS - 1, False)
                pe.wait_ge(S("given"), PAIRS * (ps + 1))

            one_pass(0)
            overflow(pe, one_pass)
            pe.sem_inc(S("experts_done"), 1)


_INS = ["x", "meta_tokens", "norm_mix_w", "w_in", "conv_w", "pool_w", "pool_scale", "a_log", "dt_bias", "dn_norm_w",
        "w_out", "norm_ffn_w", "router_group_w", "router_group_b", "router_expert_w", "router_expert_b",
        "expert_w_gate", "expert_w_up", "expert_w_down", "norm_final_w"]
_OUTS = [((1, SEQ, D), "float32")]


def kernel(**inputs):
    import numpy as _np
    import concourse.bacc as _bacc
    from concourse import mybir as _mybir
    from concourse.bass_utils import run_bass_kernel_spmd as _run

    nc = _bacc.Bacc("TRN2", target_bir_lowering=False, num_devices=1)
    arrays, args = {}, []
    for name in _INS:
        a = _np.ascontiguousarray(inputs[name])
        arrays[f"in_{name}_dram"] = a
        args.append(nc.dram_tensor(f"in_{name}_dram", a.shape, _mybir.dt.from_np(a.dtype), kind="ExternalInput").ap())
    for i, (shape, dtype) in enumerate(_OUTS):
        dt = _mybir.dt.from_np(_np.dtype(dtype))
        args.append(nc.dram_tensor(f"out_{i}_dram", shape, dt, kind="ExternalOutput").ap())
    build_block(nc, *args)
    r = _run(nc, [arrays], core_ids=[0])
    got = tuple(r.results[0][f"out_{i}_dram"] for i in range(len(_OUTS)))
    return got[0]
```
